# Optimizing a Trainium2 kernel written in Bass

```python
import jax, jax.numpy as jnp
from jax import lax
import numpy as np

D_MODEL = 1024
BATCH = 1
SEQ = 1024
DEPTH = 1
DEC_BATCH = 8
DEC_SEQ = 1
PAST_LEN = 4096
PAGE_SIZE = 128

N_HEADS = 8
HEAD_DIM = 64
ATT_DIM = N_HEADS * HEAD_DIM
CONV_DIM = D_MODEL - ATT_DIM
CONV_GROUPS = 8
CONV_WIDTH = 3
Q_BLOCK = 128
EPS = 1e-6
SB_BIAS_INIT = -8.0
PROJ_WIDTHS = (CONV_DIM, CONV_DIM, CONV_DIM, CONV_DIM, ATT_DIM, ATT_DIM, ATT_DIM, ATT_DIM)
PROJ_DIM = 4 * CONV_DIM + 4 * ATT_DIM

kernel_name = "hymba_shortconv_stickbreaking_decode_step"

def _rmsnorm(x, g):
    xf = x.astype(jnp.float32)
    y = xf * lax.rsqrt(jnp.mean(xf * xf, axis=-1, keepdims=True) + EPS)
    return (y * g.astype(jnp.float32)).astype(x.dtype)

def _split_points():
    pts, acc = [], 0
    for w in PROJ_WIDTHS[:-1]:
        acc += w
        pts.append(acc)
    return pts

def _stick_breaking(q, k, v, b_sb, q_pos, k_pos):
    z = jnp.einsum('bqhd,bkhd->bhqk', q, k).astype(jnp.float32) * (HEAD_DIM ** -0.5)
    z = z + b_sb.astype(jnp.float32)[None, :, None, None]
    mask = k_pos[None, :] < q_pos[:, None]
    log_keep = jnp.where(mask, jax.nn.log_sigmoid(-z), 0.0)
    after = lax.cumsum(log_keep, axis=3, reverse=True) - log_keep
    a = jnp.where(mask, jnp.exp(jax.nn.log_sigmoid(z) + after), 0.0)
    return jnp.einsum('bhqk,bkhd->bqhd', a.astype(v.dtype), v)

def _prompt_attend(q, k, v, b_sb):
    B, S, H, Dh = q.shape
    nb = S // Q_BLOCK
    qb = q.reshape(B, nb, Q_BLOCK, H, Dh).transpose(1, 0, 2, 3, 4)
    k_pos = jnp.arange(S, dtype=jnp.int32)

    def block(args):
        q_blk, i = args
        q_pos = i * Q_BLOCK + jnp.arange(Q_BLOCK, dtype=jnp.int32)
        return _stick_breaking(q_blk, k, v, b_sb, q_pos, k_pos)

    o = lax.map(block, (qb, jnp.arange(nb, dtype=jnp.int32)))
    return o.transpose(1, 0, 2, 3, 4).reshape(B, S, H, Dh)

def _sample_attend(q, k, v, b_sb, pool_k, pool_v, page_table):
    Bd, L, H, Dh = q.shape
    past = page_table.shape[1] * pool_k.shape[1]
    past_k = pool_k[page_table].reshape(Bd, past, H, Dh)
    past_v = pool_v[page_table].reshape(Bd, past, H, Dh)
    kk = jnp.concatenate([past_k, k], axis=1)
    vv = jnp.concatenate([past_v, v], axis=1)
    q_pos = past + jnp.arange(L, dtype=jnp.int32)
    k_pos = jnp.arange(past + L, dtype=jnp.int32)
    return _stick_breaking(q, kk, vv, b_sb, q_pos, k_pos)

def _mixer_layer(x, c, conv_prev, attend, w_ada, b_ada, g_pre, w_in, conv_w,
                 g_conv, b_sb, g_attn, w_out, g_post):
    Bsz, L, _ = x.shape
    shift, scale, gate = jnp.split(jax.nn.silu(c) @ w_ada + b_ada, 3, axis=-1)
    h = _rmsnorm(x, g_pre) * (1 + scale[:, None]) + shift[:, None]
    p = h @ w_in
    hc, bc, cc, gc, q, k, v, ga = jnp.split(p, _split_points(), axis=-1)
    u = cc * hc
    u_pad = jnp.concatenate([conv_prev.astype(u.dtype), u], axis=1)
    conv_y = sum(conv_w[i] * u_pad[:, i:i + L] for i in range(CONV_WIDTH))
    new_conv = u_pad[:, L:]
    ya = _rmsnorm(bc * conv_y, g_conv) * jax.nn.silu(gc)
    q = q.reshape(Bsz, L, N_HEADS, HEAD_DIM)
    k = k.reshape(Bsz, L, N_HEADS, HEAD_DIM)
    v = v.reshape(Bsz, L, N_HEADS, HEAD_DIM)
    o = attend(q, k, v, b_sb).reshape(Bsz, L, ATT_DIM)
    yb = _rmsnorm(o, g_attn) * jax.nn.silu(ga)
    m = jnp.concatenate([ya, yb], axis=-1) @ w_out
    y = x + gate[:, None] * _rmsnorm(m, g_post)
    return y, k, v, new_conv

def setup_inputs(seed: int = 0) -> dict:
    key = jax.random.key(seed)
    ks = jax.random.split(key, 20)
    n_pages = PAST_LEN // PAGE_SIZE
    n_used = DEC_BATCH * n_pages
    n_pool = n_used + max(1, n_used // 4)
    f32 = jnp.float32
    D = D_MODEL
    page_table = jax.random.permutation(ks[0], n_pool)[:n_used].reshape(DEC_BATCH, n_pages).astype(jnp.int32)
    return {
        "x_prompt": jax.random.normal(ks[1], (BATCH, SEQ, D), f32),
        "x_sample": jax.random.normal(ks[2], (DEC_BATCH, DEC_SEQ, D), f32),
        "c_prompt": jax.random.normal(ks[3], (BATCH, D), f32),
        "c_sample": jax.random.normal(ks[4], (DEC_BATCH, D), f32),
        "cache_k": jax.random.normal(ks[5], (DEPTH, n_pool, PAGE_SIZE, N_HEADS, HEAD_DIM), f32),
        "cache_v": jax.random.normal(ks[6], (DEPTH, n_pool, PAGE_SIZE, N_HEADS, HEAD_DIM), f32),
        "state_conv": jax.random.normal(ks[7], (DEPTH, DEC_BATCH, CONV_WIDTH - 1, CONV_DIM), f32),
        "page_table": page_table,
        "w_ada": jax.random.normal(ks[8], (DEPTH, D, 3 * D), f32) * (0.5 * D ** -0.5),
        "b_ada": jax.random.normal(ks[9], (DEPTH, 3 * D), f32) * 0.02,
        "g_pre": 1.0 + 0.01 * jax.random.normal(ks[10], (DEPTH, D), f32),
        "w_in": jax.random.normal(ks[11], (DEPTH, D, PROJ_DIM), f32) * D ** -0.5,
        "conv_w": jax.random.normal(ks[12], (DEPTH, CONV_WIDTH, CONV_DIM), f32) * CONV_WIDTH ** -0.5,
        "g_conv": 1.0 + 0.01 * jax.random.normal(ks[13], (DEPTH, CONV_DIM), f32),
        "b_sb": SB_BIAS_INIT + 0.1 * jax.random.normal(ks[17], (DEPTH, N_HEADS), f32),
        "g_attn": 1.0 + 0.01 * jax.random.normal(ks[14], (DEPTH, ATT_DIM), f32),
        "w_out": jax.random.normal(ks[15], (DEPTH, CONV_DIM + ATT_DIM, D), f32) * (CONV_DIM + ATT_DIM) ** -0.5,
        "g_post": 1.0 + 0.01 * jax.random.normal(ks[16], (DEPTH, D), f32),
    }

def reference(x_prompt, x_sample, c_prompt, c_sample, cache_k, cache_v, state_conv,
              page_table, w_ada, b_ada, g_pre, w_in, conv_w, g_conv, b_sb, g_attn, w_out, g_post):
    xp, xs = x_prompt, x_sample
    kp_l, vp_l, cp_l, ks_l, vs_l, cs_l = [], [], [], [], [], []
    for l in range(DEPTH):
        weights = (w_ada[l], b_ada[l], g_pre[l], w_in[l], conv_w[l], g_conv[l],
                   b_sb[l], g_attn[l], w_out[l], g_post[l])
        conv0 = jnp.zeros((xp.shape[0], CONV_WIDTH - 1, CONV_DIM), xp.dtype)
        xp, kp, vp, cp = _mixer_layer(xp, c_prompt, conv0, _prompt_attend, *weights)
        pool_k, pool_v = cache_k[l], cache_v[l]
        attend_s = lambda q, k, v, b, pk=pool_k, pv=pool_v: _sample_attend(q, k, v, b, pk, pv, page_table)
        xs, ksn, vsn, csn = _mixer_layer(xs, c_sample, state_conv[l], attend_s, *weights)
        kp_l.append(kp); vp_l.append(vp); cp_l.append(cp)
        ks_l.append(ksn); vs_l.append(vsn); cs_l.append(csn)
    return (xp, xs, jnp.stack(kp_l), jnp.stack(vp_l), jnp.stack(cp_l),
            jnp.stack(ks_l), jnp.stack(vs_l), jnp.stack(cs_l))


_drawn_inputs = setup_inputs


def setup_inputs(seed=0):
    import zlib

    import numpy as np

    out = dict(_drawn_inputs(seed))
    spreads = {}
    factors = {'g_pre': 4.568, 'g_conv': 8.0, 'b_sb': 7.991, 'g_attn': 8.0, 'g_post': 8.0}
    for name, (base, spread) in spreads.items():
        noise = np.random.default_rng([zlib.crc32(name.encode()), seed]).standard_normal(out[name].shape)
        drawn = base * np.exp(spread * noise) if base else spread * noise
        out[name] = __import__('jax').numpy.asarray(drawn.astype(out[name].dtype))
    for name, factor in factors.items():
        out[name] = (out[name] * factor).astype(out[name].dtype)
    return out
```

```python
from contextlib import ExitStack

import concourse.bass as bass
from concourse import mybir

F32 = mybir.dt.float32
BF16 = mybir.dt.bfloat16
I32 = mybir.dt.int32
ALU = mybir.AluOpType
ACT = mybir.ActivationFunctionType
AX_X = mybir.AxisListType.X

P = 128
D = 1024
KT = D // P
SEQ = 1024
TT = SEQ // P
NB = 8
NT = SEQ + NB
NTP = SEQ + 32
CH = NT // 3
HALF = 512
GROUPS = HALF // P
HD = 64
NH = 8
QC = 512
PAGES = 32
NPAIR = PAGES // 2
EPS = 1e-6
CLAMP = 40.0
HIDE = -2.0 ** 100
POOL_CONSTS = 9
SLOTS = 32

Q_, K_, V_, GC_, GA_, HC_, CC_, BC_ = range(8)
PART = [4, 5, 6, 3, 7, 0, 2, 1]
PJ = 24
MS = 7
M_QB0, M_KN0, M_KN1, M_KNS, M_QB1, M_CUM0, M_CUM1 = range(MS)
UNITS = [(c, i, h) for c in range(2) for i in range(4 * c + 3, -1, -1) for h in range(2)]
NU = len(UNITS)
RUPD = [u for u, (c, i, h) in enumerate(UNITS) if i > 0]

R_BA, R_GP, R_CW, R_GC, R_GA, NPAR = 0, 16, 24, 36, 40, 44

LINKS = 10


def first_col(u):
    c, i, h = UNITS[u]
    return max(0, P * (i - 4 * c))


def pairs_of(slot):
    if 1 <= slot <= 15:
        a = slot - 1
        return 1, [a] if slot < 15 else [14, 15]
    if 18 <= slot < SLOTS:
        a = slot - 18
        return 0, [a] if slot < 30 else [12 + 2 * (slot - 30), 13 + 2 * (slot - 30)]
    return 0, []


def stick_breaking_mixer(nc, x_prompt, x_sample, c_prompt, c_sample, cache_k, cache_v, state_conv,
                         page_table, w_ada, b_ada, g_pre, w_in, conv_w, g_conv, b_sb, g_attn, w_out,
                         g_post, y_prompt, y_sample, k_prompt, v_prompt, conv_prompt, k_sample,
                         v_sample, conv_sample):
    ctx = ExitStack()
    with ctx:
        ctx.enter_context(nc.allow_non_contiguous_dma(reason="per-channel rows of 512 bytes"))

        def sb(name, shape, dt=F32):
            return ctx.enter_context(nc.sbuf_tensor(name, shape, dt))

        def sem(name):
            return ctx.enter_context(nc.semaphore(name))

        hT = sb("hT", [P, KT, NTP])
        xy = sb("xy", [P, TT, D])
        ring = sb("ring", [P, 8192])
        wsl = sb("wsl", [P, 4, KT, P])
        qz = sb("qz", [P, 2, SEQ])
        kT = sb("kT", [P, NT])
        vN = sb("vN", [P, TT, P])
        gcb = sb("gcb", [P, NT])
        gab = sb("gab", [P, NT])
        hcb = sb("hcb", [P, NT])
        ub = sb("ub", [P, 2 + NT])
        bcb = sb("bcb", [P, NT])
        tmp = sb("tmp", [P, NT])
        oT = sb("oT", [P, SEQ])
        ssa = sb("ssa", [P, SEQ])
        ssb = sb("ssb", [P, SEQ])
        zc = sb("zc", [P, 2, QC])
        sp = sb("sp", [P, 2, QC])
        av = sb("av", [P, 2, QC])
        later = sb("later", [P, 2, QC])
        qsP = sb("qsP", [P, HALF])
        qb = sb("qb", [P, 2, HALF])
        prod = sb("prod", [P, 2, 2 * HALF])
        zd = sb("zd", [P, 2, NH, PAGES])
        zb = sb("zb", [P, NH * PAGES])
        zx = sb("zx", [P, NH * PAGES])
        tsc = zx
        spd = sb("spd", [P, NH * PAGES])
        tsh = sb("tsh", [P, NH, PAGES])
        keep = sb("keep", [P, NH, PAGES])
        apad = sb("apad", [P, 32, PAGES])
        om = sb("om", [P, HALF])
        osT = sb("osT", [P, GROUPS, NB])
        samp = sb("samp", [P, 4, GROUPS, NB])
        tail = sb("tail", [P, GROUPS, 2])
        ident = sb("ident", [P, P])
        e32 = sb("e32", [P, 32])
        ntri = sb("ntri", [P, P])
        nones = sb("nones", [P, P])
        unseen = sb("unseen", [P, P], BF16)
        ident_b = sb("ident_b", [P, P], BF16)
        ones = sb("ones", [P, P])
        par = sb("par", [P, NPAR])
        bsb = sb("bsb", [P, NH])
        gp = sb("gp", [P, D])
        rows = sb("rows", [64, D])
        pages = sb("pages", [1, NB * PAGES], I32)
        stT = sb("stT", [P, GROUPS, NB, 2])
        mods = sb("mods", [P, 2 * KT, 9])
        ss = sb("ss", [P, 32])
        rs = sb("rs", [P, 32])
        half = sb("half", [P, 16])

        kring = ring[:, 0:4096].rearrange("p (s j c) -> p s j c", s=4, j=2)
        vring = ring[:, 4096:8192].rearrange("p (s j c) -> p s j c", s=4, j=2)
        ada_slot = [ring[:, 4096 * i:4096 * (i + 1)].rearrange("p (k c) -> p k c", k=KT) for i in range(2)]
        yT = xy
        kN = oT[:, :].rearrange("p (t c) -> p t c", t=TT)
        qsel = om
        gps = rows[0:NB, :]
        kS, vS = rows[32:32 + NB, 0:HALF], rows[32:32 + NB, HALF:D]

        ps = ctx.enter_context(nc.psum_tensor("ps", [P, 8, HALF], F32))
        Z, OB, PJB, DB, MB = 0, 3, 4, 6, 7

        small_in = sem("small_in"); x_in = [sem(f"x_in{i}") for i in range(2)]
        ada_full = [sem(f"ada_full{i}") for i in range(2)]; 
        w_full = [sem(f"w_full{i}") for i in range(4)]
        k_full = [sem(f"k_full{i}") for i in range(4)]
        v_full = [sem(f"v_full{i}") for i in range(4)]; v_used = sem("v_used")
        pool_const = sem("pool_const"); dve_const = sem("dve_const")
        c_w = sem("c_w"); c_act = sem("c_act"); c_silu = sem("c_silu")
        cT_full = sem("cT_full"); cT_copied = sem("cT_copied")
        par_full = sem("par_full"); par_copied = sem("par_copied")
        ssq = sem("ssq"); var_ready = sem("var_ready"); rstd_ready = sem("rstd_ready")
        x_scaled = sem("x_scaled"); xT_full = sem("xT_full")
        xT_act = sem("xT_act"); xT_dve = sem("xT_dve"); xT_sdve = sem("xT_sdve")
        ada_ps = sem("ada_ps"); ada_copied = sem("ada_copied")
        mod_ps = sem("mod_ps"); h_ready = sem("h_ready")
        qs_ps = sem("qs_ps"); qs_copied = sem("qs_copied")
        gate_ps = sem("gate_ps"); gate_copied = sem("gate_copied")
        step_dve = sem("step_dve")
        pj_full = sem("pj_full"); pj_free = sem("pj_free")
        ms_full = sem("ms_full"); ms_free = sem("ms_free")
        qsel_ready = sem("qsel_ready")
        z_full = sem("z_full"); zc_ready = sem("zc_ready"); exp_done = sem("exp_done")
        ln_done = sem("ln_done"); sp_ready = sem("sp_ready")
        c_full = sem("c_full"); later_ready = sem("later_ready")
        a_ready = sem("a_ready"); pv_done = sem("pv_done")
        o_free = sem("o_free")
        prod_ready = sem("prod_ready"); red_done = sem("red_done")
        d_zx = sem("d_zx"); d_exp = sem("d_exp"); d_ln = sem("d_ln"); d_sp = sem("d_sp")
        d_t = sem("d_t"); d_a = sem("d_a")
        d_om = sem("d_om"); d_oT = sem("d_oT"); d_free = sem("d_free")
        sw_ready = sem("sw_ready"); s_exp = sem("s_exp"); s_ln = sem("s_ln"); s_max = sem("s_max")
        s_sig = sem("s_sig")
        ob_ready = sem("ob_ready"); bconv_ready = sem("bconv_ready"); sq_done = sem("sq_done")
        group_done = sem("group_done")
        kout = sem("kout"); vout = sem("vout"); out_done = sem("out_done")
        wo_full = sem("wo_full"); xr_full = [sem(f"xr_full{i}") for i in range(4)]
        e_w = sem("e_w"); e_exp = sem("e_exp"); e_dve = sem("e_dve"); e_ysT = sem("e_ysT")
        ss_ps = sem("ss_ps"); ss_var = sem("ss_var"); ss_rstd = sem("ss_rstd")
        conv_ps = sem("conv_ps"); conv_sb = sem("conv_sb")
        m_ps = sem("m_ps"); ma_ready = sem("ma_ready"); m_ready = sem("m_ready")
        msq = sem("msq"); m_var = sem("m_var"); m_rstd = sem("m_rstd"); y_ready = sem("y_ready")
        y_out = [sem(f"y_out{i}") for i in range(2)]

        xs = bcb[0:NB, 0:D]
        cnat = gcb[0:9, 0:D]
        cwk = gab[0:9, 0:D]
        parN = qb[0:NPAR, 0, 0:P]
        stN = qb[0:2 * NB, 1, :].rearrange("p (r c) -> p r c", c=P)
        cT = vN[:, 0:2, :].rearrange("p a (k c) -> p (a k) c", k=4)
        bb = oT[:, :]
        adaA = prod[:, :, :].rearrange("p a b -> p (a b)")
        adaB = ssa[:, :]

        def ma(t):
            return (gcb if t % 2 else gab)[:, 0:D]

        def mm_(t):
            return (hcb if t % 2 else bcb)[:, 0:D]

        def yo(t):
            return (ub if t % 2 else oT)[:, 0:D]

        def tmp_s(b, k):
            return tmp[:, 192 + 32 * b + 8 * k:200 + 32 * b + 8 * k]

        def ada_cols(lo, n):
            return adaA[:, lo:lo + n] if lo < 2048 else adaB[:, lo - 2048:lo - 2048 + n]

        N_SMALL = 13
        def run_groups(eng, body, last_differs=False):
            body(0, True, False)
            if last_differs:
                with eng.Fori(1, GROUPS - 1) as g:
                    body(g, False, False)
                body(GROUPS - 1, False, True)
            else:
                with eng.Fori(1, GROUPS) as g:
                    body(g, False, False)

        block = ctx.enter_context(nc.Block())

        @block.sync
        def _(sp_e):
            def bcast(ap, n):
                return ap.to_broadcast([P, n])

            sp_e.dma_start(cnat[0:1, :], c_prompt).then_inc(small_in, 16)
            sp_e.dma_start(cnat[1:9, :], c_sample).then_inc(small_in, 16)
            sp_e.dma_start(xs, x_sample.rearrange("b l d -> (b l) d")).then_inc(small_in, 16)
            sp_e.dma_start(parN[R_BA:R_BA + 16, :],
                           b_ada[:, 0:2048].rearrange("a (r c) -> (a r) c", c=P)).then_inc(small_in, 16)
            sp_e.dma_start(parN[R_GP:R_GP + 8, :],
                           g_pre.rearrange("a (r c) -> (a r) c", c=P)).then_inc(small_in, 16)
            sp_e.dma_start(parN[R_CW:R_CW + 12, :],
                           conv_w.rearrange("a w (r c) -> (a w r) c", c=P)).then_inc(small_in, 16)
            sp_e.dma_start(parN[R_GC:R_GC + 4, :],
                           g_conv.rearrange("a (r c) -> (a r) c", c=P)).then_inc(small_in, 16)
            sp_e.dma_start(parN[R_GA:R_GA + 4, :],
                           g_attn.rearrange("a (r c) -> (a r) c", c=P)).then_inc(small_in, 16)
            sp_e.dma_start(stN, state_conv.rearrange("a b w (r c) -> (a b w) r c", c=P)).then_inc(small_in, 16)
            sp_e.dma_start(bsb[:, :], bcast(b_sb, NH)).then_inc(small_in, 16)
            sp_e.dma_start(gp[:, :], bcast(g_post, D)).then_inc(small_in, 16)
            sp_e.dma_start(bb, bcast(b_ada[:, 2048:3072], D)).then_inc(small_in, 16)
            sp_e.dma_start(pages[:, :], page_table.rearrange("(a b) n -> a (b n)", a=1)).then_inc(small_in, 16)
            sp_e.dma_start(conv_sample[0, :, 0, :], state_conv[0, :, 1, :]).then_inc(out_done, 16)

            ada_v = w_ada.rearrange("a (k p) (n c) -> n p (a k) c", p=P, c=HALF)
            w_v = w_in.rearrange("a (k p) (s g c) -> s g p (a k) c", p=P, s=8, g=GROUPS)
            x_v = x_prompt.rearrange("b (h t p) d -> h p (b t) d", p=P, h=2)

            def load_w(g, s):
                src = w_v[PART[s]][bass.ds(g, 1)].rearrange("a p k c -> (a p) k c")
                sp_e.dma_start(wsl[:, s % 4, :, :], src).then_inc(w_full[s % 4], 16)

            def load_ada(n, src):
                if 2 <= n < 6:
                    sp_e.wait_ge(ada_ps, n - 1)
                elif n == 6:
                    sp_e.wait_ge(qs_ps, 1)
                sp_e.dma_start(ada_slot[n % 2], src).then_inc(ada_full[n % 2], 16)

            sp_e.dma_start(xy[:, 0:4, :], x_v[0]).then_inc(x_in[0], 16)
            load_ada(0, ada_v[0])
            sp_e.dma_start(xy[:, 4:8, :], x_v[1]).then_inc(x_in[1], 16)
            load_ada(1, ada_v[1])
            load_w(0, 0)
            load_w(0, 1)
            load_ada(2, ada_v[2])
            load_ada(3, ada_v[3])
            load_w(0, 2)
            load_w(0, 3)
            load_ada(4, w_in[0, :, 2048:2560].rearrange("(k p) c -> p k c", p=P))
            load_ada(5, ada_v[4])
            load_ada(6, ada_v[5])
            sp_e.wait_ge(small_in, 16 * N_SMALL)
            sp_e.wait_ge(ada_ps, 6)

            def load_pair(dst, cache, seq, r, full):
                for j in range(2):
                    page = sp_e.value_load(pages[0:1, bass.ds(seq * PAGES + (PAGES - 1 - r - j), 1)],
                                           min_val=0, max_val=cache_k.shape[1] - 1)
                    src = cache[0][bass.ds(page, 1)].rearrange("a p h d -> (a p) (h d)")
                    sp_e.dma_start(dst[:, j, :], src).then_inc(full, 16)

            def load_v(seq, first_q, rr):
                load_pair(vring[:, rr % 4], cache_v, seq, 2 * rr, v_full[rr % 4])

            def body(g, first, last):
                for t in range(SLOTS):
                    if not (first and t < 4):
                        sp_e.wait_ge(prod_ready, 32 * g + t - 3)
                    load_pair(kring[:, t % 4], cache_k, 2 * g + t // 16, 2 * (t % 16), k_full[t % 4])
                    parity, prs = pairs_of(t)
                    if not (first and parity == 1):
                        for rr in prs:
                            seq = 2 * g - parity
                            q = 32 * g - 16 * parity + rr
                            if not (first and rr < 4):
                                sp_e.wait_ge(v_used, q - 3)
                            load_v(seq, q, rr)
                    for slot, gg, s in ((3, 0, V_), (4, 0, GC_), (6, 0, GA_), (9, 0, HC_), (11, 0, CC_),
                                        (17, 0, BC_), (23, 1, Q_), (29, 1, K_)):
                        if slot == t and not (first and slot < 6) and not (last and gg):
                            sp_e.wait_ge(pj_full, PJ * (g + gg) + 3 * (s - 3))
                            load_w(g + gg, s)
                    if t == 12:
                        sp_e.wait_ge(pj_free, PJ * g + 8)
                        sp_e.dma_start(v_prompt.rearrange("a b (t p) (g h) d -> g (a b) p t (h d)", p=P, g=GROUPS)[
                            bass.ds(g, 1)].rearrange("a b p t c -> (a b p) t c"), vN[:, :, :]).then_inc(vout, 16)
                    if t == 13:
                        sp_e.wait_ge(ms_free, MS * g + M_KN1 + 1)
                        sp_e.dma_start(k_prompt.rearrange("a b (t p) (g h) d -> g (a b) p t (h d)", p=P, g=GROUPS)[
                            bass.ds(g, 1)].rearrange("a b p t c -> (a b p) t c"), kN[:, :, :]).then_inc(kout, 16)

            run_groups(sp_e, body, last_differs=True)

            for rr in range(NPAIR):
                sp_e.wait_ge(v_used, 32 * GROUPS - 16 + rr - 3)
                load_v(NB - 1, 32 * GROUPS - 16 + rr, rr)
            sp_e.wait_ge(pj_full, PJ * GROUPS)
            sp_e.dma_start(hT[:, :, 0:D], w_out.rearrange("a (k p) n -> p (a k) n", p=P)).then_inc(wo_full, 16)
            sp_e.wait_ge(prod_ready, 32 * GROUPS)
            xr_v = x_prompt.rearrange("b (t p) d -> t (b p) d", p=P)

            def load_residual(t):
                dst = kring[:, t % 4].rearrange("p j c -> p (j c)")
                if t < TT:
                    sp_e.dma_start(dst, xr_v[t]).then_inc(xr_full[t % 4], 16)
                else:
                    sp_e.dma_start(dst[0:NB, :], x_sample.rearrange("b l d -> (b l) d")).then_inc(xr_full[t % 4], 16)

            for t in range(4):
                load_residual(t)
            sp_e.wait_ge(ms_free, MS * GROUPS)
            sp_e.wait_ge(pj_free, PJ * GROUPS)
            sp_e.dma_start(k_sample.rearrange("a b l h d -> (a b l) (h d)"), kS[:, :]).then_inc(out_done, 16)
            sp_e.dma_start(v_sample.rearrange("a b l h d -> (a b l) (h d)"), vS[:, :]).then_inc(out_done, 16)
            sp_e.wait_ge(conv_sb, 1)
            sp_e.dma_start(conv_sample[0, :, 1, :], om[0:NB, :]).then_inc(out_done, 16)
            sp_e.dma_start(conv_prompt[0, 0], qb[0:2, 0, :]).then_inc(out_done, 16)
            for t in range(TT + 1):
                sp_e.wait_ge(y_ready, t + 1)
                if t < TT:
                    sp_e.dma_start(y_prompt.rearrange("b (t p) d -> t (b p) d", p=P)[t], yo(t)).then_inc(y_out[t % 2], 16)
                else:
                    sp_e.dma_start(y_sample.rearrange("b l d -> (b l) d"), yo(t)[0:NB, :]).then_inc(y_out[t % 2], 16)
                if t + 4 <= TT:
                    load_residual(t + 4)
            sp_e.wait_ge(out_done, 16 * 5)
            sp_e.wait_ge(kout, 16 * GROUPS)
            sp_e.wait_ge(vout, 16 * GROUPS)
            sp_e.wait_ge(y_out[0], 16 * 5)
            sp_e.wait_ge(y_out[1], 16 * 4)

        @block.gpsimd
        def _(pool):
            pool.memset(ident[:, :], 0.0).then_inc(pool_const, 1)
            pool.memset(ntri[:, :], -1.0).then_inc(pool_const, 1)
            pool.memset(half[:, :], -0.5).then_inc(pool_const, 1)
            pool.memset(unseen[:, :], HIDE).then_inc(pool_const, 1)
            pool.memset(ident_b[:, :], 0.0).then_inc(pool_const, 1)
            pool.wait_ge(pool_const, 5)
            pool.affine_select(out=ident[:, :], in_=ident[:, :], compare_op=ALU.not_equal, fill=1.0, base=0,
                               pattern=[[-1, P]], channel_multiplier=1).then_inc(pool_const, 1)
            pool.affine_select(out=ntri[:, :], in_=ntri[:, :], compare_op=ALU.is_ge, fill=0.0, base=0,
                               pattern=[[-1, P]], channel_multiplier=1).then_inc(pool_const, 1)
            pool.affine_select(out=unseen[:, :], in_=unseen[:, :], compare_op=ALU.is_ge, fill=0.0, base=0,
                               pattern=[[-1, P]], channel_multiplier=1).then_inc(pool_const, 1)
            pool.affine_select(out=ident_b[:, :], in_=ident_b[:, :], compare_op=ALU.not_equal, fill=1.0, base=0,
                               pattern=[[-1, P]], channel_multiplier=1).then_inc(pool_const, 1)
            pool.wait_ge(var_ready, 2)
            pool.tensor_tensor(rs[:, 0:TT], ss[:, 0:TT], half[:, 0:TT], ALU.pow).then_inc(rstd_ready, 1)
            pool.tensor_tensor(rs[0:NB, TT:TT + 1], ss[0:NB, TT:TT + 1], half[0:NB, 0:1], ALU.pow).then_inc(rstd_ready, 1)

            def body(g, first, last):
                for t in range(SLOTS):
                    if t % 16 == 0:
                        pool.wait_ge(ms_free, MS * g + (M_QB1 if t else M_QB0) + 1)
                    pool.wait_ge(k_full[t % 4], 32 * (8 * g + t // 4 + 1))
                    if not (first and t < 2):
                        pool.wait_ge(red_done, 32 * g + t - 1)
                    pool.tensor_tensor(
                        prod[:, t % 2].rearrange("p (j c) -> p j c", j=2), kring[:, t % 4],
                        qb[:, t // 16].unsqueeze(1).to_broadcast([P, 2, HALF]), ALU.mult).then_inc(prod_ready, 1)

            run_groups(pool, body)
            pool.wait_ge(ss_var, 1)
            pool.tensor_tensor(rs[:, 0:16], ss[:, 0:16], half[:, 0:16], ALU.pow).then_inc(ss_rstd, 1)
            pool.tensor_tensor(rs[0:NB, 16:18], ss[0:NB, 16:18], half[0:NB, 0:2], ALU.pow).then_inc(ss_rstd, 1)
            for t in range(TT + 1):
                n = P if t < TT else NB
                pool.wait_ge(m_var, t + 1)
                pool.tensor_tensor(rs[0:n, 20 + t % 2:21 + t % 2], ss[0:n, 20 + t % 2:21 + t % 2],
                                   half[0:n, 0:1], ALU.pow).then_inc(m_rstd, 1)

        @block.scalar
        def _(act):
            def run(out, in_, func, done, **kw):
                nc.scalar.activation(out, in_, func, **kw).then_inc(done, 1)

            act.wait_ge(small_in, 16 * N_SMALL)
            act.wait_ge(c_w, 1)
            run(cwk, cwk, ACT.Exp, c_act)
            act.wait_ge(c_act, 1)
            run(cwk, cwk, ACT.Ln, c_act, bias=1.0)
            act.wait_ge(c_w, 2)
            run(cwk, cwk, ACT.Exp, c_act, scale=-1.0)
            for t in range(TT):
                if t % 4 == 0:
                    act.wait_ge(x_in[t // 4], 16)
                if t >= 2:
                    act.wait_ge(ssq, t - 1)
                run((tmp if t % 2 else hcb)[:, 0:D], xy[:, t, :], ACT.Square, ssq, accum_out=ss[:, t:t + 1])
            act.wait_ge(ssq, TT)
            run(tmp[0:NB, 0:D], xs, ACT.Square, ssq, accum_out=ss[0:NB, TT:TT + 1])
            for n in range(0, 2 * KT, 2):
                act.wait_ge(xT_full, n + 1)
                run(hT[:, n // 2, 0:HALF], ps[:, n % 4, :], ACT.Copy, xT_act)
            for n in range(4):
                act.wait_ge(ada_ps, n + 1)
                run(ada_cols(HALF * n, HALF), ps[:, PJB + n % 2, :], ACT.Copy, ada_copied)
            act.wait_ge(qs_ps, 1)
            run(qsP[:, :], ps[:, DB, :], ACT.Copy, qs_copied, scale=HD ** -0.5)
            for n in range(4, 6):
                act.wait_ge(ada_ps, n + 1)
                run(ada_cols(HALF * n, HALF), ps[:, PJB + n % 2, :], ACT.Copy, ada_copied)

            def evac(g, first, m):
                act.wait_ge(pj_full, PJ * g + m + 1)
                src = ps[:, PJB + m % 2, :]
                if m < 3:
                    n = CH if m < 2 else SEQ - 2 * CH
                    cols = slice(CH * m, CH * m + n)
                    nc.scalar.activation(qz[0:HD, 0, cols], src[0:HD, 0:n], ACT.Copy, scale=HD ** -0.5)
                    run(qz[HD:P, 1, cols], src[HD:P, 0:n], ACT.Copy, pj_free, scale=HD ** -0.5)
                elif m < 6:
                    run(kT[:, CH * (m - 3):CH * (m - 2)], src[:, 0:CH], ACT.Copy, pj_free)
                elif m < 8:
                    if m == 6 and not first:
                        act.wait_ge(vout, 16 * g)
                    run(vN[:, 4 * (m - 6):4 * (m - 5), :], src.rearrange("p (t c) -> p t c", t=4), ACT.Copy, pj_free)
                elif m == 8:
                    run(vS[:, bass.ds(g * P, P)], src[0:NB, 0:P], ACT.Copy, pj_free)
                else:
                    s, c = (m - 9) // 3, (m - 9) % 3
                    buf, off = ((gcb, 0), (gab, 0), (hcb, 0), (ub, 2), (bcb, 0))[s]
                    if m == 9 and not first:
                        act.wait_ge(group_done, g)
                    run(buf[:, off + CH * c:off + CH * (c + 1)], src[:, 0:CH], ACT.Copy, pj_free)

            def silu_mid(g, k):
                act.wait_ge(sw_ready, 2 * g + k + 1)
                run(tmp[:, :], tmp[:, :], ACT.Exp, s_exp)
                act.wait_ge(s_exp, 2 * g + k + 1)
                run(tmp[:, :], tmp[:, :], ACT.Ln, s_ln, bias=1.0)

            def silu_end(g, k):
                act.wait_ge(s_max, 2 * g + k + 1)
                run(tmp[:, :], tmp[:, :], ACT.Exp, s_sig, scale=-1.0)

            def decode_ln(g, k):
                act.wait_ge(d_zx, 2 * g + k + 1)
                run(zx[:, :], zx[:, :], ACT.Exp, d_exp)
                act.wait_ge(d_exp, 2 * g + k + 1)
                run(zx[:, :], zx[:, :], ACT.Ln, d_ln, bias=1.0)

            def decode_a(g, k, first):
                act.wait_ge(d_t, 2 * g + k + 1)
                if not (first and k == 0):
                    act.wait_ge(v_used, 32 * g - 16 + 16 * k + 16)
                run(apad[:, 0:NH, :], zb[:, :].rearrange("p (h r) -> p h r", h=NH), ACT.Exp, d_a)

            def body(g, first, last):
                for t in range(SLOTS + 1):
                    u = t - 8
                    if 0 <= u < NU:
                        lo, z = first_col(u), zc[:, u % 2, first_col(u):QC]
                        act.wait_ge(zc_ready, NU * g + u + 1)
                        run(z, z, ACT.Exp, exp_done)
                        act.wait_ge(exp_done, NU * g + u + 1)
                        run(z, z, ACT.Ln, ln_done, bias=1.0)
                    if 1 <= u <= NU:
                        v, lo = u - 1, first_col(u - 1)
                        head = UNITS[v][2]
                        act.wait_ge(c_full, NU * g + v + 1)
                        if not (first and v < 2):
                            act.wait_ge(pv_done, NU * g + v - 1)
                        run(av[:, v % 2, lo:QC], ps[:, Z + v % 3, lo:QC], ACT.Exp, a_ready,
                            bias=bsb[:, bass.ds(2 * g + head, 1)])
                    if t < 8:
                        evac(g, first, t)
                        if t == 7:
                            evac(g, first, 8)
                    elif t < SLOTS and u % 2 == 1:
                        evac(g, first, 9 + u // 2)
                    if t == 15:
                        silu_mid(g, 0)
                    if t == 16:
                        decode_ln(g, 0)
                        silu_end(g, 0)
                    if t == 17:
                        decode_a(g, 0, first)
                    if t == 21:
                        silu_mid(g, 1)
                    if t == 22:
                        silu_end(g, 1)
                decode_ln(g, 1)
                evac(g, first, 21)
                evac(g, first, 22)
                evac(g, first, 23)
                decode_a(g, 1, first)
                act.wait_ge(ob_ready, g + 1)
                run(tmp[:, 0:SEQ], oT[:, :], ACT.Square, sq_done)
                act.wait_ge(bconv_ready, g + 1)
                run(gab[:, 0:SEQ], hcb[:, 0:SEQ], ACT.Square, sq_done)

            run_groups(act, body)

            act.wait_ge(e_w, 1)
            run(tmp[:, 0:64], tmp[:, 64:128], ACT.Square, e_exp)
            for t in range(TT + 1):
                n = P if t < TT else NB
                col = t if t < TT else 16
                if t == 0:
                    act.wait_ge(ss_rstd, 2)
                act.wait_ge(m_ps, t + 1)
                if t >= 2:
                    act.wait_ge(m_ready, t - 1)
                run(ma(t)[0:n].rearrange("p (j c) -> p j c", j=2), ps[0:n, 4 * (t % 2):4 * (t % 2) + 2, :],
                    ACT.Copy, ma_ready, scale=rs[0:n, col:col + 1])
                act.wait_ge(m_ready, t + 1)
                if t >= 2:
                    act.wait_ge(m_var, t - 1)
                run(ma(t)[0:n], mm_(t)[0:n], ACT.Square, msq, accum_out=ss[0:n, 24 + t % 2:25 + t % 2])

        @block.vector
        def _(v):
            links = [0]

            def link(ins, base=None):
                links[0] += 1
                ins.then_inc(step_dve, 1)
                v.wait_ge(step_dve, links[0] if base is None else base + links[0])

            v.memset(ones[:, :], 1.0).then_inc(dve_const, 1)
            v.memset(nones[:, :], -1.0).then_inc(dve_const, 1)
            v.memset(qz[:, :, :], 0.0).then_inc(dve_const, 1)
            v.memset(cT, 0.0).then_inc(dve_const, 1)
            v.memset(hT[:, :, SEQ:NTP], 0.0).then_inc(dve_const, 1)
            v.memset(ub[:, 0:2], 0.0).then_inc(dve_const, 1)
            v.memset(apad[:, :, :], 0.0).then_inc(dve_const, 1)
            v.memset(ssb[:, :], 0.0).then_inc(dve_const, 1)
            v.memset(keep[:, :, :], 1.0).then_inc(dve_const, 1)
            v.memset(tsh[:, :, :], 0.0).then_inc(dve_const, 1)
            v.wait_ge(dve_const, 10)
            v.memset(keep[:, :, 0:1], 0.0).then_inc(dve_const, 1)
            v.wait_ge(pool_const, POOL_CONSTS)
            v.tensor_reduce(e32[:, :], ident[:, :].rearrange("p (a i) -> p i a", a=4), AX_X, ALU.add)\
                .then_inc(dve_const, 1)
            v.wait_ge(dve_const, 12)

            v.wait_ge(small_in, 16 * N_SMALL)
            v.tensor_scalar(cwk, cnat, -1.0, CLAMP, ALU.mult, ALU.min).then_inc(c_w, 1)
            v.wait_ge(c_act, 2)
            v.scalar_tensor_tensor(cwk, cnat, -1.0, cwk, ALU.mult, ALU.max).then_inc(c_w, 1)
            v.wait_ge(c_act, 3)
            v.tensor_tensor(cwk, cnat, cwk, ALU.mult).then_inc(c_silu, 1)
            v.wait_ge(cT_full, 1)
            v.tensor_copy(cT[:, :, 0:9], ps[:, MB, 0:9 * KT].rearrange("p (k c) -> p k c", k=KT)).then_inc(cT_copied, 1)
            v.wait_ge(par_full, 1)
            v.tensor_copy(par[:, :], ps[:, DB, 0:NPAR]).then_inc(par_copied, 1)
            v.tensor_copy(stT[:, :, :, :], ps[:, DB, 64:64 + 64].rearrange("p (g b w) -> p g b w", g=GROUPS, b=NB))\
                .then_inc(par_copied, 1)

            v.wait_ge(ssq, TT + 1)
            v.tensor_scalar(ss[:, 0:TT], ss[:, 0:TT], 1.0 / D, EPS, ALU.mult, ALU.add).then_inc(var_ready, 1)
            v.tensor_scalar(ss[0:NB, TT:TT + 1], ss[0:NB, TT:TT + 1], 1.0 / D, EPS, ALU.mult, ALU.add)\
                .then_inc(var_ready, 1)
            v.wait_ge(rstd_ready, 2)
            for t in range(TT):
                v.tensor_scalar(xy[:, t, :], xy[:, t, :], rs[:, t:t + 1], None, ALU.mult).then_inc(x_scaled, 1)
            v.tensor_scalar(xs, xs, rs[0:NB, TT:TT + 1], None, ALU.mult).then_inc(x_scaled, 1)
            for n in range(1, 2 * KT, 2):
                v.wait_ge(xT_full, n + 1)
                v.tensor_copy(hT[:, n // 2, HALF:SEQ], ps[:, n % 4, :]).then_inc(xT_dve, 1)
            v.wait_ge(xT_full, 2 * KT + 1)
            v.tensor_copy(hT[:, :, SEQ:NT], ps[:, MB, 128:128 + NB * KT].rearrange("p (k b) -> p k b", k=KT))\
                .then_inc(xT_sdve, 1)

            v.wait_ge(mod_ps, 1)
            mps = ps[:, MB, 256:256 + 9 * 2 * KT].rearrange("p (k c) -> p k c", c=9)
            link(v.tensor_tensor(mods[:, :, :], mps, par[:, R_BA:R_BA + 16].unsqueeze(2).to_broadcast([P, 16, 9]), ALU.add))
            link(v.tensor_scalar(mods[:, KT:, :], mods[:, KT:, :], 1.0, None, ALU.add))
            link(v.tensor_tensor(mods[:, KT:, :], mods[:, KT:, :],
                                 par[:, R_GP:R_GP + 8].unsqueeze(2).to_broadcast([P, KT, 9]), ALU.mult))
            v.wait_ge(xT_act, KT)
            v.wait_ge(xT_sdve, 1)
            link(v.tensor_tensor(hT[:, :, SEQ:NT], hT[:, :, SEQ:NT], mods[:, KT:, 1:9], ALU.mult))
            v.tensor_tensor(hT[:, :, SEQ:NT], hT[:, :, SEQ:NT], mods[:, 0:KT, 1:9], ALU.add).then_inc(h_ready, 1)
            for k in range(KT):
                v.tensor_scalar(hT[:, k, 0:SEQ], hT[:, k, 0:SEQ], mods[:, KT + k, 0:1], mods[:, k, 0:1],
                                ALU.mult, ALU.add).then_inc(h_ready, 1)
            for n in range(2):
                cols = slice(HALF * n, HALF * (n + 1))
                v.wait_ge(gate_ps, n + 1)
                link(v.tensor_tensor(gps[:, cols], ps[0:NB, MB, :], bb[0:NB, cols], ALU.add))
                link(v.tensor_tensor(gps[:, cols], gps[:, cols], gp[0:NB, cols], ALU.mult))
                link(v.tensor_tensor(bb[:, cols], ps[:, Z, :], bb[:, cols], ALU.add))
                v.tensor_tensor(gp[:, cols], gp[:, cols], bb[:, cols], ALU.mult).then_inc(gate_copied, 1)
            v.wait_ge(gate_copied, 2)
            link(v.memset(ssa[:, :], 0.0))
            PRO = links[0]

            def seq_q(g, k):
                if k == 0 and isinstance(g, int):
                    v.wait_ge(qs_copied, 1)
                v.tensor_scalar(qsel[:, :], qsP[:, :], e32[:, bass.ds(2 * g + k, 1)], None, ALU.mult)\
                    .then_inc(qsel_ready, 1)

            def seq_q_copy(g, k):
                v.wait_ge(ms_full, MS * g + (M_QB1 if k else M_QB0) + 1)
                v.tensor_copy(qb[:, k, :], ps[:, MB, :]).then_inc(ms_free, 1)

            def body(g, first, last):
                links[0] = 0
                base = PRO + g * LINKS

                def lk(ins):
                    link(ins, base)

                def decode_scores(k):
                    lk(v.tensor_tensor(zb[:, :].rearrange("p (h r) -> p h r", h=NH), zd[:, k],
                                       bsb[:, :].unsqueeze(2).to_broadcast([P, NH, PAGES]), ALU.add))
                    v.tensor_scalar(zx[:, :], zb[:, :], CLAMP, None, ALU.min).then_inc(d_zx, 1)

                def decode_softplus(k):
                    v.wait_ge(d_ln, 2 * g + k + 1)
                    v.tensor_tensor(spd[:, :], zb[:, :], zx[:, :], ALU.max).then_inc(d_sp, 1)

                def decode_log_weights(k):
                    v.wait_ge(ms_full, MS * g + (M_CUM1 if k else M_CUM0) + 1)
                    tot = ps[:, MB, 256:512].rearrange("p (h r) -> p h r", h=NH)
                    lk(v.tensor_copy(tsh[:, :, 1:PAGES], tot[:, :, 0:PAGES - 1]))
                    lk(v.tensor_tensor_scan(tsc[:, :], keep[:, :, :].rearrange("p h r -> p (h r)"),
                                            tsh[:, :, :].rearrange("p h r -> p (h r)"), 0.0, ALU.mult, ALU.add))
                    ins = v.tensor_tensor(zb[:, :], ps[:, MB, 0:256], zb[:, :], ALU.add)
                    ins.then_inc(ms_free, 1)
                    v.wait_ge(ms_free, MS * g + (M_CUM1 if k else M_CUM0) + 1)
                    v.tensor_tensor(zb[:, :], zb[:, :], tsc[:, :], ALU.add).then_inc(d_t, 1)

                def own_heads(parity):
                    seq = 2 * g - parity
                    v.wait_ge(v_used, NPAIR * (seq + 1))
                    v.tensor_tensor(om[:, :].rearrange("p (h d) -> p h d", h=NH),
                                    ps[:, DB, :].rearrange("p (h d) -> p h d", h=NH),
                                    e32[:, 0:NH].unsqueeze(2).to_broadcast([P, NH, HD]), ALU.mult).then_inc(d_om, 1)

                def own_heads_copy(parity):
                    seq = 2 * g - parity
                    v.wait_ge(d_oT, seq + 1)
                    v.tensor_copy(osT[:, :, bass.ds(seq, 1)], ps[:, DB, 0:GROUPS].unsqueeze(2)).then_inc(d_free, 1)

                seq_q(g, 0)
                seq_q_copy(g, 0)
                for t in range(SLOTS):
                    u = t - 8
                    if t == 16:
                        v.wait_ge(red_done, 32 * g + 16)
                        decode_scores(0)
                    if u >= 0:
                        c, i, h = UNITS[u]
                        lo = first_col(u)
                        v.wait_ge(z_full, NU * g + u + 1)
                        v.tensor_scalar(zc[:, u % 2, lo:QC], ps[:, Z + u % 3, lo:QC], bsb[:, bass.ds(2 * g + h, 1)],
                                        CLAMP, ALU.add, ALU.min).then_inc(zc_ready, 1)
                    v.wait_ge(prod_ready, 32 * g + t + 1)
                    r = 2 * (t % 16)
                    v.tensor_reduce(zd[:, t // 16, :, r:r + 2],
                                    prod[:, t % 2].rearrange("p (j h d) -> p h j d", j=2, h=NH), AX_X, ALU.add)\
                        .then_inc(red_done, 1)
                    if u >= 0:
                        v.wait_ge(ln_done, NU * g + u + 1)
                        v.scalar_tensor_tensor(sp[:, u % 2, lo:QC], ps[:, Z + u % 3, lo:QC],
                                               bsb[:, bass.ds(2 * g + h, 1)], zc[:, u % 2, lo:QC],
                                               ALU.add, ALU.max).then_inc(sp_ready, 1)
                    if u >= 1:
                        add_later(g, u - 1)
                    if t in (8, 9):
                        v.wait_ge(ms_full, MS * g + M_KN0 + t - 8 + 1)
                        v.tensor_copy(kN[:, 4 * (t - 8):4 * (t - 7), :],
                                      ps[:, MB, :].rearrange("p (t c) -> p t c", t=4)).then_inc(ms_free, 1)
                    if t == 10:
                        v.wait_ge(ms_full, MS * g + M_KNS + 1)
                        v.tensor_copy(kS[:, bass.ds(g * P, P)], ps[0:NB, MB, 0:P]).then_inc(ms_free, 1)
                    if t == 11:
                        seq_q(g, 1)
                    if t == 13:
                        seq_q_copy(g, 1)
                    if t in (14, 20):
                        silu_start(g, gcb if t == 14 else gab, 11 if t == 14 else 14)
                    if t in (15, 21):
                        silu_max(g, gcb if t == 15 else gab, t == 21)
                    if t in (16, 22):
                        silu_mul(g, gcb if t == 16 else gab, t == 22)
                    if t == 16:
                        decode_softplus(0)
                        if not first:
                            own_heads(1)
                    if t == 17:
                        if not first:
                            own_heads_copy(1)
                        decode_log_weights(0)
                    if t == 18:
                        out_copy(g, 0)
                v.wait_ge(red_done, 32 * g + 32)
                decode_scores(1)
                own_heads(0)
                add_later(g, NU - 1)
                v.wait_ge(pj_free, PJ * g + 21)
                lk(v.tensor_tensor(ub[:, 2:2 + NT], ub[:, 2:2 + NT], hcb[:, :], ALU.mult))
                decode_softplus(1)
                tap = lambda w: par[:, bass.ds(R_CW + 4 * w + g, 1)]
                lk(v.tensor_scalar(hcb[:, 0:SEQ], ub[:, 2:2 + SEQ], tap(2), None, ALU.mult))
                lk(v.scalar_tensor_tensor(hcb[:, 0:SEQ], ub[:, 1:1 + SEQ], tap(1), hcb[:, 0:SEQ], ALU.mult, ALU.add))
                lk(v.scalar_tensor_tensor(hcb[:, 0:SEQ], ub[:, 0:SEQ], tap(0), hcb[:, 0:SEQ], ALU.mult, ALU.add))
                out_copy(g, 1)
                own_heads_copy(0)
                decode_log_weights(1)
                v.scalar_tensor_tensor(yT[:, bass.ds(GROUPS + g, 1), :].rearrange("p a s -> p (a s)"), oT[:, :],
                                       par[:, bass.ds(R_GA + g, 1)], gab[:, 0:SEQ], ALU.mult, ALU.mult)
                v.tensor_copy(tail[:, bass.ds(g, 1), :].rearrange("p a s -> p (a s)"), ub[:, SEQ:SEQ + 2])
                v.tensor_copy(samp[:, 0, bass.ds(g, 1), :].rearrange("p a s -> p (a s)"), ub[:, 2 + SEQ:2 + NT])
                v.tensor_copy(samp[:, 2, bass.ds(g, 1), :].rearrange("p a s -> p (a s)"), gcb[:, SEQ:NT])
                v.tensor_copy(samp[:, 3, bass.ds(g, 1), :].rearrange("p a s -> p (a s)"), gab[:, SEQ:NT])
                v.wait_ge(pj_free, PJ * g + 24)
                v.tensor_copy(samp[:, 1, bass.ds(g, 1), :].rearrange("p a s -> p (a s)"), bcb[:, SEQ:NT])
                v.tensor_tensor(hcb[:, 0:SEQ], hcb[:, 0:SEQ], bcb[:, 0:SEQ], ALU.mult).then_inc(bconv_ready, 1)
                v.wait_ge(bconv_ready, g + 1)
                v.scalar_tensor_tensor(yT[:, bass.ds(g, 1), :].rearrange("p a s -> p (a s)"), hcb[:, 0:SEQ],
                                       par[:, bass.ds(R_GC + g, 1)], gcb[:, 0:SEQ], ALU.mult, ALU.mult)
                v.wait_ge(sq_done, 2 * g + 1)
                v.tensor_tensor(ssb[:, :], ssb[:, :], tmp[:, 0:SEQ], ALU.add)
                v.wait_ge(sq_done, 2 * g + 2)
                v.tensor_tensor(ssa[:, :], ssa[:, :], gab[:, 0:SEQ], ALU.add).then_inc(group_done, 1)
                v.wait_ge(group_done, g + 1)
                assert links[0] == LINKS, links

            def add_later(g, u):
                c, i, h = UNITS[u]
                lo, di = first_col(u), i - 4 * c
                v.wait_ge(c_full, NU * g + u + 1)
                if i == 0:
                    return
                fresh = P if di >= 0 else 0
                if fresh:
                    ins = v.tensor_copy(later[:, h, lo:lo + P], sp[:, u % 2, lo:lo + P])
                if lo + fresh < QC:
                    ins = v.tensor_tensor(later[:, h, lo + fresh:QC], later[:, h, lo + fresh:QC],
                                          sp[:, u % 2, lo + fresh:QC], ALU.add)
                ins.then_inc(later_ready, 1)

            def silu_start(g, x, use):
                v.wait_ge(pj_free, PJ * g + use + 1)
                v.tensor_scalar(tmp[:, :], x[:, :], -1.0, CLAMP, ALU.mult, ALU.min).then_inc(sw_ready, 1)

            def silu_max(g, x, k):
                v.wait_ge(s_ln, 2 * g + int(k) + 1)
                v.scalar_tensor_tensor(tmp[:, :], x[:, :], -1.0, tmp[:, :], ALU.mult, ALU.max).then_inc(s_max, 1)

            def silu_mul(g, x, k):
                v.wait_ge(s_sig, 2 * g + int(k) + 1)
                v.tensor_tensor(x[:, :], x[:, :], tmp[:, :], ALU.mult)

            def out_copy(g, c):
                v.wait_ge(pv_done, NU * g + (8 if c == 0 else NU))
                if c == 0:
                    v.wait_ge(kout, 16 * (g + 1))
                v.tensor_copy(oT[:, QC * c:QC * (c + 1)], ps[:, OB, :]).then_inc(o_free if c == 0 else ob_ready, 1)
                if c == 1:
                    v.wait_ge(ob_ready, g + 1)

            run_groups(v, body)

            v.wait_ge(v_used, NPAIR * NB)
            v.tensor_tensor(om[:, :].rearrange("p (h d) -> p h d", h=NH), ps[:, DB, :].rearrange("p (h d) -> p h d", h=NH),
                            e32[:, 0:NH].unsqueeze(2).to_broadcast([P, NH, HD]), ALU.mult).then_inc(d_om, 1)
            v.wait_ge(d_oT, NB)
            links[0] = 0
            base = PRO + GROUPS * LINKS

            def lk(ins):
                link(ins, base)

            v.tensor_copy(osT[:, :, NB - 1:NB], ps[:, DB, 0:GROUPS].unsqueeze(2)).then_inc(d_free, 1)
            v.wait_ge(d_free, NB)
            blk = lambda k: tmp[:, 32 * k:32 * k + 32].rearrange("p (g b) -> p g b", g=GROUPS)
            chan = lambda row: par[:, row:row + GROUPS].unsqueeze(2).to_broadcast([P, GROUPS, NB])
            lk(v.tensor_tensor(blk(2), stT[:, :, :, 0], chan(R_CW), ALU.mult))
            lk(v.tensor_tensor(blk(4), stT[:, :, :, 1], chan(R_CW + 4), ALU.mult))
            lk(v.tensor_tensor(blk(2), blk(2), blk(4), ALU.add))
            lk(v.tensor_tensor(blk(4), samp[:, 0], chan(R_CW + 8), ALU.mult))
            lk(v.tensor_tensor(blk(2), blk(2), blk(4), ALU.add))
            lk(v.tensor_tensor(blk(2), blk(2), samp[:, 1], ALU.mult))
            v.tensor_copy(blk(3), osT[:, :, :]).then_inc(e_w, 1)
            v.wait_ge(e_w, 1)
            lk(v.tensor_tensor(blk(4), blk(2), chan(R_GC), ALU.mult))
            lk(v.tensor_tensor(blk(5), blk(3), chan(R_GA), ALU.mult))
            v.tensor_tensor(blk(6), blk(4), samp[:, 2], ALU.mult).then_inc(e_ysT, 1)
            v.tensor_tensor(blk(7), blk(5), samp[:, 3], ALU.mult).then_inc(e_ysT, 1)
            v.wait_ge(conv_ps, 1)
            lk(v.tensor_copy(om[0:NB, :], ps[0:NB, MB, :]))
            v.tensor_copy(qb[0:2, 0, :], ps[0:2, DB, :]).then_inc(conv_sb, 1)
            v.wait_ge(ss_ps, 1)
            lk(v.tensor_scalar(ss[:, 0:16], ps[:, OB, 0:16], 1.0 / HALF, EPS, ALU.mult, ALU.add))
            v.tensor_scalar(ss[0:NB, 16:18], ps[0:NB, OB, 16:18], 1.0 / HALF, EPS, ALU.mult, ALU.add).then_inc(ss_var, 1)
            v.wait_ge(ss_rstd, 2)
            for t in range(TT + 1):
                n = P if t < TT else NB
                col = 8 + t if t < TT else 17
                v.wait_ge(ma_ready, t + 1)
                if t >= 2:
                    v.wait_ge(msq, t - 1)
                v.scalar_tensor_tensor(mm_(t)[0:n].rearrange("p (j c) -> p j c", j=2),
                                       ps[0:n, 4 * (t % 2) + 2:4 * (t % 2) + 4, :], rs[0:n, col:col + 1],
                                       ma(t)[0:n].rearrange("p (j c) -> p j c", j=2), ALU.mult, ALU.add)\
                    .then_inc(m_ready, 1)
                v.wait_ge(msq, t + 1)
                v.tensor_scalar(ss[0:n, 20 + t % 2:21 + t % 2], ss[0:n, 24 + t % 2:25 + t % 2], 1.0 / D, EPS,
                                ALU.mult, ALU.add).then_inc(m_var, 1)
                v.wait_ge(m_rstd, t + 1)
                if t >= 2:
                    v.wait_ge(y_out[t % 2], 16 * (t // 2))
                gate = gp if t < TT else gps
                lk(v.scalar_tensor_tensor(yo(t)[0:n], mm_(t)[0:n], rs[0:n, 20 + t % 2:21 + t % 2], gate[0:n, :],
                                          ALU.mult, ALU.mult))
                v.wait_ge(xr_full[t % 4], 16 * (t // 4 + 1))
                ins = v.tensor_tensor(yo(t)[0:n], yo(t)[0:n], kring[0:n, t % 4].rearrange("p j c -> p (j c)"), ALU.add)
                ins.then_inc(y_ready, 1)

        @block.tensor
        def _(pe):
            def mm(out, l, r, start, stop):
                return nc.tensor.matmul(out, l, r, start=start, stop=stop, skip_group_check=True)

            pe.wait_ge(pool_const, POOL_CONSTS)
            pe.wait_ge(c_silu, 1)
            for k in range(KT):
                last = nc.tensor.transpose(ps[:, MB, 9 * k:9 * k + 9], cwk[:, P * k:P * (k + 1)], ident[0:9, 0:9])
            last.then_inc(cT_full, 1)
            pe.wait_ge(small_in, 16 * N_SMALL)
            nc.tensor.transpose(ps[:, DB, 0:NPAR], parN, ident[0:NPAR, 0:NPAR])
            for g in range(GROUPS):
                last = nc.tensor.transpose(ps[:, DB, 64 + 16 * g:80 + 16 * g], stN[:, g, :], ident[0:16, 0:16])
            last.then_inc(par_full, 1)

            pe.wait_ge(dve_const, 12)
            pe.wait_ge(cT_copied, 1)

            def strips(bank, lhs, slot, n):
                pe.wait_ge(ada_full[n % 2], 16 * (n // 2 + 1))
                for k in range(KT):
                    j = k % 4
                    last = mm(ps[32 * j:32 * j + 32, bank, :], lhs(k), ada_slot[n % 2][:, k, :], k < 4, k >= 4)
                return last

            def ada(n, chunk):
                if n >= 2:
                    pe.wait_ge(ada_copied, n - 1)
                strips(PJB + n % 2, lambda k: cT[:, k, :], n % 2, chunk).then_inc(ada_ps, 1)

            ada(0, 0)
            ada(1, 1)
            pe.wait_ge(x_scaled, TT + 1)
            for n in range(2 * KT):
                if n >= 4:
                    pe.wait_ge(xT_dve if n % 2 else xT_act, (n - 4) // 2 + 1)
                for j in range(4):
                    last = nc.tensor.transpose(ps[:, n % 4, P * j:P * (j + 1)],
                                               xy[:, 4 * (n % 2) + j, P * (n // 2):P * (n // 2 + 1)], ident[:, :])
                last.then_inc(xT_full, 1)
            for k in range(KT):
                last = nc.tensor.transpose(ps[:, MB, P + NB * k:P + NB * (k + 1)], xs[:, P * k:P * (k + 1)],
                                           ident[0:NB, 0:NB])
            last.then_inc(xT_full, 1)
            ada(2, 2)
            ada(3, 3)
            pe.wait_ge(ada_copied, 4)
            pe.wait_ge(xT_sdve, 1)
            for k in range(2 * KT):
                last = mm(ps[:, MB, 256 + 9 * k:265 + 9 * k], ada_cols(P * k, P), e32[:, 0:9], True, True)
            last.then_inc(mod_ps, 1)
            pe.wait_ge(h_ready, 1)
            pe.wait_ge(par_copied, 2)
            strips(DB, lambda k: hT[:, k, SEQ:NTP], 0, 4).then_inc(qs_ps, 1)
            for n, chunk in ((4, 5), (5, 6)):
                ada(n, chunk)
            for n in range(2):
                pe.wait_ge(ada_copied, 5 + n)
                pe.wait_ge(xT_act, KT)
                if n:
                    pe.wait_ge(gate_copied, n)
                mm(ps[0:NB, MB, :], e32[:, 1:9], ada_cols(2048 + HALF * n, HALF), True, True)
                mm(ps[:, Z, :], e32[:, 0:1].to_broadcast([P, P]), ada_cols(2048 + HALF * n, HALF), True, True)\
                    .then_inc(gate_ps, 1)
            pe.wait_ge(gate_copied, 2)
            pe.wait_ge(h_ready, KT + 1)
            pe.wait_ge(ada_copied, 6)
            pe.wait_ge(qs_copied, 1)

            def body(g, first, last_):
                def project(m, part, chunk, ks=range(KT)):
                    if ks[0] == 0:
                        if chunk == 0:
                            pe.wait_ge(w_full[part % 4], 16 * (2 * g + part // 4 + 1))
                        if not (first and m < 2):
                            pe.wait_ge(pj_free, PJ * g + m - 1)
                    for k in ks:
                        last = mm(ps[:, PJB + m % 2, 0:CH], wsl[:, part % 4, k, :], hT[:, k, CH * chunk:CH * (chunk + 1)],
                                  k == 0, k == KT - 1)
                    if ks[-1] == KT - 1:
                        last.then_inc(pj_full, 1)

                def values(m):
                    pe.wait_ge(pj_free, PJ * g + m - 1)
                    if m == 6:
                        pe.wait_ge(w_full[V_], 16 * (2 * g + 1))
                    if m < 8:
                        for j in range(4):
                            for k in range(KT):
                                t = 4 * (m - 6) + j
                                last = mm(ps[:, PJB + m % 2, P * j:P * (j + 1)], hT[:, k, P * t:P * (t + 1)],
                                          wsl[:, V_, k, :], k == 0, k == KT - 1)
                    else:
                        for k in range(KT):
                            last = mm(ps[0:NB, PJB + m % 2, 0:P], hT[:, k, SEQ:NT], wsl[:, V_, k, :], k == 0, k == KT - 1)
                    last.then_inc(pj_full, 1)

                def misc_ready(n):
                    if not (first and n == 0):
                        pe.wait_ge(ms_free, MS * g + n)

                def spread_q(k):
                    misc_ready(M_QB1 if k else M_QB0)
                    pe.wait_ge(qsel_ready, 2 * g + k + 1)
                    mm(ps[:, MB, :], ones[:, :], qsel[:, :], True, True).then_inc(ms_full, 1)

                def cumulate(k):
                    misc_ready(M_CUM1 if k else M_CUM0)
                    pe.wait_ge(d_sp, 2 * g + k + 1)
                    mm(ps[:, MB, 0:256], ntri[:, :], spd[:, :], True, True)
                    mm(ps[:, MB, 256:512], nones[:, :], spd[:, :], True, True).then_inc(ms_full, 1)

                def page_values(t):
                    parity, prs = pairs_of(t)
                    if first and parity == 1:
                        return
                    for rr in prs:
                        value_pair(2 * g - parity, 32 * g - 16 * parity + rr, rr, 2 * g - parity)

                def own_heads_T(parity):
                    pe.wait_ge(d_om, 2 * g - parity + 1)
                    heads_T(2 * g - parity)

                def scores(u):
                    c, i, h = UNITS[u]
                    lo = first_col(u)
                    if u == 0:
                        pe.wait_ge(pj_free, PJ * g + 6)
                    if not (first and u < 3):
                        pe.wait_ge(a_ready, NU * g + u - 2)
                    last = mm(ps[:, Z + u % 3, lo:QC], kT[:, P * i:P * (i + 1)], qz[:, h, QC * c + lo:QC * (c + 1)],
                              True, False)
                    if i >= 4 * c:
                        last = mm(ps[:, Z + u % 3, lo:lo + P], ident_b[:, :], unseen[:, :], False, False)
                    last.then_inc(z_full, 1)

                def suffix(u):
                    c, i, h = UNITS[u]
                    lo, di = first_col(u), i - 4 * c
                    pe.wait_ge(sp_ready, NU * g + u + 1)
                    seen = min(QC, lo + (P if di >= 0 else 0))
                    if seen < QC:
                        pe.wait_ge(later_ready, len(RUPD) * g + RUPD.index(u - 2) + 1)
                        mm(ps[:, Z + u % 3, seen:QC], nones[:, :], later[:, h, seen:QC], False, False)
                    mm(ps[:, Z + u % 3, lo:QC], ntri[:, :], sp[:, u % 2, lo:QC], False, True).then_inc(c_full, 1)

                def outputs(u):
                    c, i, h = UNITS[u]
                    lo = first_col(u)
                    pe.wait_ge(a_ready, NU * g + u + 1)
                    if u == 0:
                        pe.wait_ge(pj_free, PJ * g + 8)
                        if not first:
                            pe.wait_ge(ob_ready, g)
                    if u == 8:
                        pe.wait_ge(o_free, g + 1)
                    mm(ps[HD * h:HD * (h + 1), OB, lo:QC], vN[:, i, HD * h:HD * (h + 1)], av[:, u % 2, lo:QC],
                       i == 4 * c + 3, i == 0).then_inc(pv_done, 1)

                def key_rows(n):
                    misc_ready(M_KN0 + n)
                    if n < 2:
                        for j in range(4):
                            last = nc.tensor.transpose(ps[:, MB, P * j:P * (j + 1)],
                                                       kT[:, P * (4 * n + j):P * (4 * n + j + 1)], ident[:, :])
                    else:
                        last = nc.tensor.transpose(ps[0:NB, MB, 0:P], kT[:, SEQ:NT], ident[:, :])
                    last.then_inc(ms_full, 1)

                for t in range(8):
                    if t < 3:
                        project(t, Q_, t)
                    elif t < 6:
                        project(t, K_, t - 3)
                    else:
                        values(t)
                    if t == 2:
                        spread_q(0)
                    page_values(t)
                values(8)
                for t in range(8, SLOTS + 2):
                    u = t - 8
                    if u < NU:
                        scores(u)
                        m = 9 + u // 2
                        ks = range(0, 4) if u % 2 == 0 else range(4, 8)
                        part, chunk = GC_ + (m - 9) // 3, (m - 9) % 3
                        project(m, part, chunk, ks[0:2])
                        if t == 17:
                            cumulate(0)
                    else:
                        project(21 + u - NU, BC_, u - NU)
                    if 1 <= u <= NU:
                        suffix(u - 1)
                    if u < NU:
                        project(m, part, chunk, ks[2:4])
                    if u >= 2:
                        outputs(u - 2)
                    if t in (8, 9, 10):
                        key_rows(t - 8)
                    if t == 12:
                        spread_q(1)
                    if t == 16 and not first:
                        own_heads_T(1)
                    page_values(t)
                project(23, BC_, 2)
                own_heads_T(0)
                cumulate(1)

            def value_pair(seq, q, rr, done_before):
                if rr == 0:
                    pe.wait_ge(d_a, seq + 1)
                    if not (isinstance(seq, int) and seq == 0):
                        pe.wait_ge(d_free, done_before)
                pe.wait_ge(v_full[rr % 4], v_fill(seq, rr))
                for j in range(2):
                    r = 2 * rr + j
                    strip = 32 * (r % 4)
                    last = mm(ps[strip:strip + 32, DB, :], apad[:, :, r], vring[:, rr % 4, j, :], r < 4, r >= PAGES - 4)
                last.then_inc(v_used, 1)

            def v_fill(seq, rr):
                return 32 * (4 * seq + rr // 4 + 1)

            def heads_T(seq):
                for c in range(GROUPS):
                    last = mm(ps[:, DB, c:c + 1], om[:, P * c:P * (c + 1)], ones[:, 0:1], True, True)
                last.then_inc(d_oT, 1)

            run_groups(pe, body)

            for rr in range(NPAIR):
                value_pair(NB - 1, 16 * (NB - 1) + rr, rr, NB - 1)
            pe.wait_ge(d_om, NB)
            heads_T(NB - 1)
            pe.wait_ge(group_done, GROUPS)
            pe.wait_ge(ms_free, MS * GROUPS)
            for c in range(GROUPS):
                nc.tensor.transpose(ps[0:NB, MB, P * c:P * (c + 1)], samp[:, 0, c, :], ident[:, :])
            pe.wait_ge(d_free, NB)
            for c in range(GROUPS):
                last = nc.tensor.transpose(ps[0:2, DB, P * c:P * (c + 1)], tail[:, c, :], ident[:, :])
            last.then_inc(conv_ps, 1)
            pe.wait_ge(ob_ready, GROUPS)
            for b, src in enumerate((ssa, ssb)):
                for t in range(TT):
                    mm(ps[:, OB, 8 * b + t:8 * b + t + 1], src[:, P * t:P * (t + 1)], ones[:, 0:1], True, True)
            pe.wait_ge(e_exp, 1)
            for b in range(2):
                for c in range(GROUPS):
                    last = mm(ps[0:NB, OB, 16 + b:17 + b], tmp[:, 32 * b + 8 * c:32 * b + 8 * c + 8], ones[:, 0:1],
                              c == 0, c == GROUPS - 1)
            last.then_inc(ss_ps, 1)
            pe.wait_ge(wo_full, 16)
            pe.wait_ge(ss_var, 1)
            pe.wait_ge(conv_sb, 1)
            pe.wait_ge(e_ysT, 2)
            for t in range(TT + 1):
                if t >= 2:
                    pe.wait_ge(m_ready, t - 1)
                n = P if t < TT else NB
                for b in range(2):
                    for j in range(2):
                        for k in range(GROUPS):
                            if t < TT:
                                lhs = yT[:, GROUPS * b + k, P * t:P * (t + 1)]
                            else:
                                lhs = tmp_s(b, k)
                            last = mm(ps[0:n, 4 * (t % 2) + 2 * b + j, :], lhs,
                                      hT[:, GROUPS * b + k, HALF * j:HALF * (j + 1)], k == 0, k == GROUPS - 1)
                last.then_inc(m_ps, 1)


_INS = ["x_prompt", "x_sample", "c_prompt", "c_sample", "cache_k", "cache_v", "state_conv", "page_table",
        "w_ada", "b_ada", "g_pre", "w_in", "conv_w", "g_conv", "b_sb", "g_attn", "w_out", "g_post"]
_OUTS = [(1, SEQ, D), (NB, 1, D), (1, 1, SEQ, NH, HD), (1, 1, SEQ, NH, HD), (1, 1, 2, HALF),
         (1, NB, 1, NH, HD), (1, NB, 1, NH, HD), (1, NB, 2, HALF)]


def kernel(**inputs):
    import numpy as _np
    import concourse.bacc as _bacc
    from concourse import mybir as _mybir
    from concourse.bass_utils import run_bass_kernel_spmd as _run

    nc = _bacc.Bacc("TRN2", target_bir_lowering=False, num_devices=1, dynamic_dma_scratch_size=1024)
    nc.disable_value_cache = True
    arrays, args = {}, []
    for name in _INS:
        a = _np.ascontiguousarray(inputs[name])
        arrays[f"in_{name}_dram"] = a
        args.append(nc.dram_tensor(f"in_{name}_dram", a.shape, _mybir.dt.from_np(a.dtype), kind="ExternalInput").ap())
    for i, shape in enumerate(_OUTS):
        args.append(nc.dram_tensor(f"out_{i}_dram", shape, _mybir.dt.float32, kind="ExternalOutput").ap())
    stick_breaking_mixer(nc, *args)
    r = _run(nc, [arrays], core_ids=[0])
    return tuple(r.results[0][f"out_{i}_dram"] for i in range(len(_OUTS)))
```

```python
from contextlib import ExitStack

import concourse.bass as bass
from concourse import mybir

F32 = mybir.dt.float32
BF16 = mybir.dt.bfloat16
I32 = mybir.dt.int32
ALU = mybir.AluOpType
ACT = mybir.ActivationFunctionType
AX_X = mybir.AxisListType.X

P = 128
D = 1024
KT = D // P
SEQ = 1024
TT = SEQ // P
NB = 8
NT = SEQ + NB
NTP = SEQ + 32
CH = NT // 3
HALF = 512
GROUPS = HALF // P
HD = 64
NH = 8
QC = 512
PAGES = 32
NPAIR = PAGES // 2
EPS = 1e-6
CLAMP = 40.0
HIDE = -2.0 ** 100
ADA3_AT = 8
OUT_UNITS = 2 * (TT + 1)
LAST_PV = NPAIR - 4
POOL_CONSTS = 9
SLOTS = 32
ACT_SET = "natural_log_exp_and_others"

Q_, K_, V_, GC_, GA_, HC_, CC_, BC_ = range(8)
PART = [4, 5, 6, 3, 7, 0, 2, 1]
PJ = 24
MS = 7
M_QB0, M_KN0, M_KN1, M_KNS, M_QB1, M_CUM0, M_CUM1 = range(MS)
UNITS = [(c, i, h) for c in range(2) for i in range(4 * c + 3, -1, -1) for h in range(2)]
NU = len(UNITS)
RUPD = [u for u, (c, i, h) in enumerate(UNITS) if i > 0]

R_BA, R_GP, R_CW, R_GC, R_GA, NPAR = 0, 16, 24, 36, 40, 44

LINKS = 10


def first_col(u):
    c, i, h = UNITS[u]
    return max(0, P * (i - 4 * c))


def pairs_of(slot):
    if 1 <= slot <= 15:
        a = slot - 1
        return 1, [a] if slot < 15 else [14, 15]
    if 18 <= slot < SLOTS:
        a = slot - 18
        return 0, [a] if slot < 30 else [12 + 2 * (slot - 30), 13 + 2 * (slot - 30)]
    return 0, []


def stick_breaking_mixer(nc, x_prompt, x_sample, c_prompt, c_sample, cache_k, cache_v, state_conv,
                         page_table, w_ada, b_ada, g_pre, w_in, conv_w, g_conv, b_sb, g_attn, w_out,
                         g_post, y_prompt, y_sample, k_prompt, v_prompt, conv_prompt, k_sample,
                         v_sample, conv_sample):
    ctx = ExitStack()
    with ctx:
        ctx.enter_context(nc.allow_non_contiguous_dma(reason="per-channel rows of 512 bytes"))

        def sb(name, shape, dt=F32):
            return ctx.enter_context(nc.sbuf_tensor(name, shape, dt))

        def sem(name):
            return ctx.enter_context(nc.semaphore(name))

        hT = sb("hT", [P, KT, NTP])
        xy = sb("xy", [P, TT, D])
        ring = sb("ring", [P, 8192])
        wsl = sb("wsl", [P, 4, KT, P])
        qz = sb("qz", [P, 2, SEQ])
        kT = sb("kT", [P, NT])
        vN = sb("vN", [P, TT, P])
        gcb = sb("gcb", [P, NT])
        gab = sb("gab", [P, NT])
        hcb = sb("hcb", [P, NT])
        ub = sb("ub", [P, 2 + NT])
        bcb = sb("bcb", [P, NT])
        tmp = sb("tmp", [P, NT])
        oT = sb("oT", [P, SEQ])
        ssa = sb("ssa", [P, SEQ])
        ssb = sb("ssb", [P, SEQ])
        zc = sb("zc", [P, 2, QC])
        sp = sb("sp", [P, 2, QC])
        av = sb("av", [P, 2, QC])
        later = sb("later", [P, 2, QC])
        qsP = sb("qsP", [P, HALF])
        qb = sb("qb", [P, 2, HALF])
        prod = sb("prod", [P, 2, 2 * HALF])
        zd = sb("zd", [P, 2, NH, PAGES])
        zb = sb("zb", [P, NH * PAGES])
        zx = sb("zx", [P, NH * PAGES])
        tsc = zx
        spd = sb("spd", [P, NH * PAGES])
        tsh = sb("tsh", [P, NH, PAGES])
        keep = sb("keep", [P, NH, PAGES])
        apad = sb("apad", [P, 32, PAGES])
        om = sb("om", [P, HALF])
        osT = sb("osT", [P, GROUPS, NB])
        samp = sb("samp", [P, 4, GROUPS, NB])
        tail = sb("tail", [P, GROUPS, 2])
        ident = sb("ident", [P, P])
        e32 = sb("e32", [P, 32])
        ntri = sb("ntri", [P, P])
        nones = sb("nones", [P, P])
        unseen = sb("unseen", [P, P], BF16)
        ident_b = sb("ident_b", [P, P], BF16)
        ones = sb("ones", [P, P])
        par = sb("par", [P, NPAR])
        bsb = sb("bsb", [P, NH])
        gp = sb("gp", [P, D])
        rows = sb("rows", [64, D])
        pages = sb("pages", [1, NB * PAGES], I32)
        stT = sb("stT", [P, GROUPS, NB, 2])
        mods = sb("mods", [P, 2 * KT, 9])
        ss = sb("ss", [P, 32])
        rs = sb("rs", [P, 32])
        half = sb("half", [P, 16])

        kring = ring[:, 0:4096].rearrange("p (s j c) -> p s j c", s=4, j=2)
        vring = ring[:, 4096:8192].rearrange("p (s j c) -> p s j c", s=4, j=2)
        ada_slot = [ring[:, 4096 * i:4096 * (i + 1)].rearrange("p (k c) -> p k c", k=KT) for i in range(2)]
        yT = xy
        kN = oT[:, :].rearrange("p (t c) -> p t c", t=TT)
        qsel = om
        gps = rows[0:NB, :]
        kS, vS = rows[32:32 + NB, 0:HALF], rows[32:32 + NB, HALF:D]

        ps = ctx.enter_context(nc.psum_tensor("ps", [P, 8, HALF], F32))
        Z, OB, PJB, DB, MB = 0, 3, 4, 6, 7

        small_in = sem("small_in"); c_in = sem("c_in"); gate_in = sem("gate_in"); gate_step = sem("gate_step"); silu_done = sem("silu_done"); ssa_zero = sem("ssa_zero"); x_in = [sem(f"x_in{i}") for i in range(2)]
        ada_full = [sem(f"ada_full{i}") for i in range(2)]; 
        w_full = [sem(f"w_full{i}") for i in range(4)]
        k_full = [sem(f"k_full{i}") for i in range(4)]
        v_full = [sem(f"v_full{i}") for i in range(4)]; v_used = sem("v_used")
        pool_const = sem("pool_const"); dve_const = sem("dve_const")
        c_w = sem("c_w"); c_act = sem("c_act"); c_silu = sem("c_silu")
        cT_full = sem("cT_full"); cT_copied = sem("cT_copied")
        par_full = sem("par_full"); par_copied = sem("par_copied")
        ssq = sem("ssq"); var_ready = sem("var_ready"); rstd_ready = sem("rstd_ready")
        x_scaled = sem("x_scaled"); xT_full = sem("xT_full")
        xT_act = sem("xT_act"); xT_dve = sem("xT_dve"); xT_sdve = sem("xT_sdve")
        ada_ps = sem("ada_ps"); ada_copied = sem("ada_copied")
        mod_ps = sem("mod_ps"); h_ready = sem("h_ready")
        qs_ps = sem("qs_ps"); qs_copied = sem("qs_copied")
        gate_ps = sem("gate_ps"); gate_copied = sem("gate_copied")
        step_dve = sem("step_dve")
        pj_full = sem("pj_full"); pj_free = sem("pj_free")
        ms_full = sem("ms_full"); ms_free = sem("ms_free")
        qsel_ready = sem("qsel_ready")
        z_full = sem("z_full"); zc_ready = sem("zc_ready"); exp_done = sem("exp_done")
        ln_done = sem("ln_done"); sp_ready = sem("sp_ready")
        c_full = sem("c_full"); later_ready = sem("later_ready")
        a_ready = sem("a_ready"); pv_done = sem("pv_done")
        o_free = sem("o_free")
        prod_ready = sem("prod_ready"); red_done = sem("red_done")
        d_zx = sem("d_zx"); d_exp = sem("d_exp"); d_ln = sem("d_ln"); d_sp = sem("d_sp")
        d_t = sem("d_t"); d_a = sem("d_a")
        d_om = sem("d_om"); d_oT = sem("d_oT"); d_free = sem("d_free")
        s_abs = sem("s_abs"); s_exp = sem("s_exp"); s_ln = sem("s_ln"); s_min = sem("s_min")
        s_sig = sem("s_sig")
        ob_ready = sem("ob_ready"); bconv_ready = sem("bconv_ready"); sq_done = sem("sq_done")
        group_done = sem("group_done")
        kout = sem("kout"); vout = sem("vout"); out_done = sem("out_done")
        wo_full = [sem(f"wo_full{k}") for k in range(KT)]; xr_full = [sem(f"xr_full{i}") for i in range(4)]
        e_w = sem("e_w"); e_exp = sem("e_exp"); e_dve = sem("e_dve"); e_ysT = sem("e_ysT")
        ss_ps = sem("ss_ps"); ss_var = sem("ss_var"); ss_rstd = sem("ss_rstd")
        conv_ps = sem("conv_ps"); conv_sb = sem("conv_sb")
        m_ps = sem("m_ps"); ma_ready = sem("ma_ready"); m_ready = sem("m_ready")
        msq = sem("msq"); m_var = sem("m_var"); m_rstd = sem("m_rstd"); y_ready = sem("y_ready")
        y_out = [sem(f"y_out{i}") for i in range(2)]

        xs = bcb[0:NB, 0:D]
        cnat = gcb[0:9, 0:D]
        cwk = gab[0:9, 0:D]
        parN = qb[0:NPAR, 0, 0:P]
        stN = qb[0:2 * NB, 1, :].rearrange("p (r c) -> p r c", c=P)
        cT = zb[:, :].rearrange("p (k c) -> p k c", k=KT)
        bb = ub[:, 2:2 + D]
        adaA = prod[:, :, :].rearrange("p a b -> p (a b)")
        adaB = ssa[:, :]

        def wo(k):
            return wsl[:, k, :, :].rearrange("p k c -> p (k c)") if k < 3 else hT[:, k, 0:D]

        def ma(t):
            return (gcb if t % 2 else gab)[:, 0:D]

        def mm_(t):
            return (hcb if t % 2 else bcb)[:, 0:D]

        def yo(t):
            return (ub if t % 2 else oT)[:, 0:D]

        def tmp_s(b, k):
            return tmp[:, 192 + 32 * b + 8 * k:200 + 32 * b + 8 * k]

        def ada_cols(lo, n):
            return adaA[:, lo:lo + n] if lo < 2048 else adaB[:, lo - 2048:lo - 2048 + n]

        N_SMALL = 9

        def run_groups(eng, body, last_differs=False):
            body(0, True, False)
            if last_differs:
                with eng.Fori(1, GROUPS - 1) as g:
                    body(g, False, False)
                body(GROUPS - 1, False, True)
            else:
                with eng.Fori(1, GROUPS) as g:
                    body(g, False, False)

        block = ctx.enter_context(nc.Block())

        @block.sync
        def _(sp_e):
            def bcast(ap, n):
                return ap.to_broadcast([P, n])

            ada_v = w_ada.rearrange("a (k p) (n c) -> n p (a k) c", p=P, c=HALF)
            w_v = w_in.rearrange("a (k p) (s g c) -> s g p (a k) c", p=P, s=8, g=GROUPS)
            x_v = x_prompt.rearrange("b (h t p) d -> h p (b t) d", p=P, h=2)

            def load_w(g, s):
                src = w_v[PART[s]][bass.ds(g, 1)].rearrange("a p k c -> (a p) k c")
                sp_e.dma_start(wsl[:, s % 4, :, :], src).then_inc(w_full[s % 4], 16)

            ADA_FREE = {2: 1, 3: 2, 4: 3, 5: 4, 7: 5}

            def load_ada(n, src):
                if n >= 2:
                    sp_e.wait_ge(ada_ps, ADA_FREE[n])
                sp_e.dma_start(ada_slot[n % 2], src).then_inc(ada_full[n % 2], 16)

            sp_e.dma_start(cnat[0:1, :], c_prompt).then_inc(c_in, 16)
            sp_e.dma_start(cnat[1:9, :], c_sample).then_inc(c_in, 16)
            sp_e.dma_start(xy[:, 0:4, :], x_v[0]).then_inc(x_in[0], 16)
            load_ada(0, ada_v[0])
            sp_e.dma_start(xs, x_sample.rearrange("b l d -> (b l) d")).then_inc(small_in, 16)
            sp_e.dma_start(parN[R_BA:R_BA + 16, :],
                           b_ada[:, 0:2048].rearrange("a (r c) -> (a r) c", c=P)).then_inc(small_in, 16)
            sp_e.dma_start(parN[R_GP:R_GP + 8, :],
                           g_pre.rearrange("a (r c) -> (a r) c", c=P)).then_inc(small_in, 16)
            sp_e.dma_start(parN[R_CW:R_CW + 12, :],
                           conv_w.rearrange("a w (r c) -> (a w r) c", c=P)).then_inc(small_in, 16)
            sp_e.dma_start(parN[R_GC:R_GC + 4, :],
                           g_conv.rearrange("a (r c) -> (a r) c", c=P)).then_inc(small_in, 16)
            sp_e.dma_start(parN[R_GA:R_GA + 4, :],
                           g_attn.rearrange("a (r c) -> (a r) c", c=P)).then_inc(small_in, 16)
            sp_e.dma_start(stN, state_conv.rearrange("a b w (r c) -> (a b w) r c", c=P)).then_inc(small_in, 16)
            sp_e.dma_start(bsb[:, :], bcast(b_sb, NH)).then_inc(small_in, 16)
            sp_e.dma_start(pages[:, :], page_table.rearrange("(a b) n -> a (b n)", a=1)).then_inc(small_in, 16)
            sp_e.dma_start(conv_sample[0, :, 0, :], state_conv[0, :, 1, :]).then_inc(out_done, 16)

            sp_e.dma_start(xy[:, 4:8, :], x_v[1]).then_inc(x_in[1], 16)
            load_ada(1, ada_v[1])
            load_ada(2, ada_v[2])
            load_ada(3, ada_v[3])
            load_ada(4, w_in[0, :, 2048:2560].rearrange("(k p) c -> p k c", p=P))
            load_w(0, 0)
            load_w(0, 1)
            sp_e.dma_start(gp[:, :], bcast(g_post, D)).then_inc(gate_in, 16)
            sp_e.dma_start(bb, bcast(b_ada[:, 2048:3072], D)).then_inc(gate_in, 16)
            load_w(0, 2)
            load_w(0, 3)
            load_ada(5, ada_v[4])
            sp_e.wait_ge(small_in, 16 * N_SMALL)
            sp_e.wait_ge(qs_ps, 1)

            def load_pair(dst, cache, seq, r, full):
                for j in range(2):
                    page = sp_e.value_load(pages[0:1, bass.ds(seq * PAGES + (PAGES - 1 - r - j), 1)],
                                           min_val=0, max_val=cache_k.shape[1] - 1)
                    src = cache[0][bass.ds(page, 1)].rearrange("a p h d -> (a p) (h d)")
                    sp_e.dma_start(dst[:, j, :], src).then_inc(full, 16)

            wo_v = w_out.rearrange("a (k p) n -> k p (a n)", p=P)

            def load_wo(k):
                if k < 3:
                    sp_e.wait_ge(pj_full, PJ * (GROUPS - 1) + 3 * (k + 5))
                sp_e.dma_start(wo(k), wo_v[k]).then_inc(wo_full[k], 16)

            def load_v(seq, first_q, rr):
                load_pair(vring[:, rr % 4], cache_v, seq, 2 * rr, v_full[rr % 4])

            def body(g, first, last):
                for t in range(SLOTS):
                    if not (first and t < 4):
                        sp_e.wait_ge(prod_ready, 32 * g + t - 3)
                    load_pair(kring[:, t % 4], cache_k, 2 * g + t // 16, 2 * (t % 16), k_full[t % 4])
                    if first and t == 5:
                        load_ada(7, ada_v[5])
                    parity, prs = pairs_of(t)
                    if first and t == 18:
                        sp_e.wait_ge(ada_ps, 6)
                    if not (first and parity == 1):
                        for rr in prs:
                            seq = 2 * g - parity
                            q = 32 * g - 16 * parity + rr
                            if not (first and rr < 4):
                                sp_e.wait_ge(v_used, q - 3)
                            load_v(seq, q, rr)
                    for slot, gg, s in ((3, 0, V_), (4, 0, GC_), (6, 0, GA_), (9, 0, HC_), (11, 0, CC_),
                                        (17, 0, BC_), (23, 1, Q_), (29, 1, K_)):
                        if slot == t and not (first and slot < 6) and not (last and gg):
                            sp_e.wait_ge(pj_full, PJ * (g + gg) + 3 * (s - 3))
                            load_w(g + gg, s)
                    if last and t in (22, 28):
                        load_wo(0 if t == 22 else 1)
                    if t == 12:
                        sp_e.wait_ge(pj_free, PJ * g + 8)
                        sp_e.dma_start(v_prompt.rearrange("a b (t p) (g h) d -> g (a b) p t (h d)", p=P, g=GROUPS)[
                            bass.ds(g, 1)].rearrange("a b p t c -> (a b p) t c"), vN[:, :, :]).then_inc(vout, 16)
                    if t == 13:
                        sp_e.wait_ge(ms_free, MS * g + M_KN1 + 1)
                        sp_e.dma_start(k_prompt.rearrange("a b (t p) (g h) d -> g (a b) p t (h d)", p=P, g=GROUPS)[
                            bass.ds(g, 1)].rearrange("a b p t c -> (a b p) t c"), kN[:, :, :]).then_inc(kout, 16)

            run_groups(sp_e, body, last_differs=True)

            def last_values(rrs):
                for rr in rrs:
                    sp_e.wait_ge(v_used, 32 * GROUPS - 16 + rr - 3)
                    load_v(NB - 1, 32 * GROUPS - 16 + rr, rr)

            last_values(range(4))
            load_wo(2)
            sp_e.wait_ge(pj_full, PJ * GROUPS)
            for k in range(3, KT):
                load_wo(k)
            sp_e.wait_ge(prod_ready, 32 * GROUPS)
            xr_v = x_prompt.rearrange("b (t p) d -> t (b p) d", p=P)

            def load_residual(t):
                dst = kring[:, t % 4].rearrange("p j c -> p (j c)")
                if t < TT:
                    sp_e.dma_start(dst, xr_v[t]).then_inc(xr_full[t % 4], 16)
                else:
                    sp_e.dma_start(dst[0:NB, :], x_sample.rearrange("b l d -> (b l) d")).then_inc(xr_full[t % 4], 16)

            for t in range(4):
                load_residual(t)
                last_values(range(4 + 3 * t, 7 + 3 * t))
            sp_e.wait_ge(ms_free, MS * GROUPS)
            sp_e.wait_ge(pj_free, PJ * GROUPS)
            sp_e.dma_start(k_sample.rearrange("a b l h d -> (a b l) (h d)"), kS[:, :]).then_inc(out_done, 16)
            sp_e.dma_start(v_sample.rearrange("a b l h d -> (a b l) (h d)"), vS[:, :]).then_inc(out_done, 16)
            for t in range(TT + 1):
                sp_e.wait_ge(y_ready, t + 1)
                if t < TT:
                    sp_e.dma_start(y_prompt.rearrange("b (t p) d -> t (b p) d", p=P)[t], yo(t)).then_inc(y_out[t % 2], 16)
                else:
                    sp_e.dma_start(y_sample.rearrange("b l d -> (b l) d"), yo(t)[0:NB, :]).then_inc(y_out[t % 2], 16)
                if t + 4 <= TT:
                    load_residual(t + 4)
                if t == TT - 2:
                    sp_e.wait_ge(conv_sb, 1)
                    sp_e.dma_start(conv_sample[0, :, 1, :], om[0:NB, :]).then_inc(out_done, 16)
                    sp_e.dma_start(conv_prompt[0, 0], qb[0:2, 0, :]).then_inc(out_done, 16)
            sp_e.wait_ge(out_done, 16 * 5)
            sp_e.wait_ge(kout, 16 * GROUPS)
            sp_e.wait_ge(vout, 16 * GROUPS)
            sp_e.wait_ge(y_out[0], 16 * 5)
            sp_e.wait_ge(y_out[1], 16 * 4)

        @block.gpsimd
        def _(pool):
            pool.memset(ident[:, :], 0.0).then_inc(pool_const, 1)
            pool.memset(ntri[:, :], -1.0).then_inc(pool_const, 1)
            pool.memset(half[:, :], -0.5).then_inc(pool_const, 1)
            pool.memset(unseen[:, :], HIDE).then_inc(pool_const, 1)
            pool.memset(ident_b[:, :], 0.0).then_inc(pool_const, 1)
            pool.wait_ge(pool_const, 5)
            pool.affine_select(out=ident[:, :], in_=ident[:, :], compare_op=ALU.not_equal, fill=1.0, base=0,
                               pattern=[[-1, P]], channel_multiplier=1).then_inc(pool_const, 1)
            pool.affine_select(out=ntri[:, :], in_=ntri[:, :], compare_op=ALU.is_ge, fill=0.0, base=0,
                               pattern=[[-1, P]], channel_multiplier=1).then_inc(pool_const, 1)
            pool.affine_select(out=unseen[:, :], in_=unseen[:, :], compare_op=ALU.is_ge, fill=0.0, base=0,
                               pattern=[[-1, P]], channel_multiplier=1).then_inc(pool_const, 1)
            pool.affine_select(out=ident_b[:, :], in_=ident_b[:, :], compare_op=ALU.not_equal, fill=1.0, base=0,
                               pattern=[[-1, P]], channel_multiplier=1).then_inc(pool_const, 1)
            pool.wait_ge(var_ready, 2)
            pool.tensor_tensor(rs[:, 0:TT], ss[:, 0:TT], half[:, 0:TT], ALU.pow).then_inc(rstd_ready, 1)
            pool.tensor_tensor(rs[0:NB, TT:TT + 1], ss[0:NB, TT:TT + 1], half[0:NB, 0:1], ALU.pow).then_inc(rstd_ready, 1)

            def body(g, first, last):
                for t in range(SLOTS):
                    if t % 16 == 0:
                        pool.wait_ge(ms_free, MS * g + (M_QB1 if t else M_QB0) + 1)
                    pool.wait_ge(k_full[t % 4], 32 * (8 * g + t // 4 + 1))
                    if not (first and t < 2):
                        pool.wait_ge(red_done, 32 * g + t - 1)
                    pool.tensor_tensor(
                        prod[:, t % 2].rearrange("p (j c) -> p j c", j=2), kring[:, t % 4],
                        qb[:, t // 16].unsqueeze(1).to_broadcast([P, 2, HALF]), ALU.mult).then_inc(prod_ready, 1)

            run_groups(pool, body)
            pool.wait_ge(ss_var, 1)
            pool.tensor_tensor(rs[:, 0:16], ss[:, 0:16], half[:, 0:16], ALU.pow).then_inc(ss_rstd, 1)
            for t in range(TT + 1):
                n = P if t < TT else NB
                if t == TT:
                    pool.wait_ge(ss_var, 2)
                    pool.tensor_tensor(rs[0:NB, 16:18], ss[0:NB, 16:18], half[0:NB, 0:2], ALU.pow).then_inc(ss_rstd, 1)
                pool.wait_ge(m_var, t + 1)
                pool.tensor_tensor(rs[0:n, 20 + t % 2:21 + t % 2], ss[0:n, 20 + t % 2:21 + t % 2],
                                   half[0:n, 0:1], ALU.pow).then_inc(m_rstd, 1)

        @block.scalar
        def _(act):
            def run(out, in_, func, done, **kw):
                nc.scalar.activation(out, in_, func, **kw).then_inc(done, 1)

            act.preload_act_table_set(ACT_SET)
            act.wait_ge(c_in, 32)
            run(cwk, cnat, ACT.Abs, c_act)
            act.wait_ge(c_act, 1)
            run(cwk, cwk, ACT.Exp, c_act, scale=-1.0)
            act.wait_ge(c_act, 2)
            run(cwk, cwk, ACT.Ln, c_act, bias=1.0)
            act.wait_ge(c_w, 1)
            run(cwk, cwk, ACT.Exp, c_act)
            for t in range(TT):
                if t % 4 == 0:
                    act.wait_ge(x_in[t // 4], 16)
                if t >= 2:
                    act.wait_ge(ssq, t - 1)
                run((tmp if t % 2 else hcb)[:, 0:D], xy[:, t, :], ACT.Square, ssq, accum_out=ss[:, t:t + 1])
            act.wait_ge(ssq, TT)
            act.wait_ge(small_in, 16 * N_SMALL)
            run(tmp[0:NB, 0:D], xs, ACT.Square, ssq, accum_out=ss[0:NB, TT:TT + 1])
            def ada_copy(n):
                act.wait_ge(ada_ps, n + 1)
                run(ada_cols(HALF * n, HALF), ps[:, PJB + n % 2, :], ACT.Copy, ada_copied)

            for n in range(3):
                ada_copy(n)
            for n in range(0, 2 * KT, 2):
                if n == ADA3_AT:
                    ada_copy(3)
                act.wait_ge(xT_full, n + 1)
                run(hT[:, n // 2, 0:HALF], ps[:, n % 4, :], ACT.Copy, xT_act)
            act.wait_ge(qs_ps, 1)
            run(qsP[:, :], ps[:, DB, :], ACT.Copy, qs_copied, scale=HD ** -0.5)

            def gate_strips(n):
                act.wait_ge(ada_ps, 5 + n)
                run(ada_cols(HALF * (4 + n), HALF), ps[:, DB, :], ACT.Copy, ada_copied)

            def evac(g, first, m):
                act.wait_ge(pj_full, PJ * g + m + 1)
                src = ps[:, PJB + m % 2, :]
                if m < 3:
                    n = CH if m < 2 else SEQ - 2 * CH
                    cols = slice(CH * m, CH * m + n)
                    nc.scalar.activation(qz[0:HD, 0, cols], src[0:HD, 0:n], ACT.Copy, scale=HD ** -0.5)
                    run(qz[HD:P, 1, cols], src[HD:P, 0:n], ACT.Copy, pj_free, scale=HD ** -0.5)
                elif m < 6:
                    run(kT[:, CH * (m - 3):CH * (m - 2)], src[:, 0:CH], ACT.Copy, pj_free)
                elif m < 8:
                    if m == 6 and not first:
                        act.wait_ge(vout, 16 * g)
                    run(vN[:, 4 * (m - 6):4 * (m - 5), :], src.rearrange("p (t c) -> p t c", t=4), ACT.Copy, pj_free)
                elif m == 8:
                    run(vS[:, bass.ds(g * P, P)], src[0:NB, 0:P], ACT.Copy, pj_free)
                else:
                    s, c = (m - 9) // 3, (m - 9) % 3
                    buf, off = ((gcb, 0), (gab, 0), (hcb, 0), (ub, 2), (bcb, 0))[s]
                    if m == 9 and not first:
                        act.wait_ge(group_done, g)
                    run(buf[:, off + CH * c:off + CH * (c + 1)], src[:, 0:CH], ACT.Copy, pj_free)

            def silu_mid(g, k):
                act.wait_ge(pj_free, PJ * g + (15 if k else 12))
                if k:
                    act.wait_ge(silu_done, 2 * g + 1)
                run(tmp[:, :], (gab if k else gcb)[:, :], ACT.Abs, s_abs)
                act.wait_ge(s_abs, 2 * g + k + 1)
                run(tmp[:, :], tmp[:, :], ACT.Exp, s_exp, scale=-1.0)
                act.wait_ge(s_exp, 2 * g + k + 1)
                run(tmp[:, :], tmp[:, :], ACT.Ln, s_ln, bias=1.0)

            def silu_end(g, k):
                act.wait_ge(s_min, 2 * g + k + 1)
                run(tmp[:, :], tmp[:, :], ACT.Exp, s_sig)

            def decode_ln(g, k):
                act.wait_ge(d_zx, 2 * g + k + 1)
                run(zx[:, :], zx[:, :], ACT.Exp, d_exp)
                act.wait_ge(d_exp, 2 * g + k + 1)
                run(zx[:, :], zx[:, :], ACT.Ln, d_ln, bias=1.0)

            def decode_a(g, k, first):
                act.wait_ge(d_t, 2 * g + k + 1)
                if not (first and k == 0):
                    act.wait_ge(v_used, 32 * g - 16 + 16 * k + 16)
                run(apad[:, 0:NH, :], zb[:, :].rearrange("p (h r) -> p h r", h=NH), ACT.Exp, d_a)

            def body(g, first, last):
                act.preload_act_table_set(ACT_SET)
                for t in range(SLOTS + 1):
                    u = t - 8
                    if 0 <= u < NU:
                        lo, z = first_col(u), zc[:, u % 2, first_col(u):QC]
                        act.wait_ge(zc_ready, NU * g + u + 1)
                        run(z, z, ACT.Exp, exp_done)
                        act.wait_ge(exp_done, NU * g + u + 1)
                        run(z, z, ACT.Ln, ln_done, bias=1.0)
                    if 1 <= u <= NU:
                        v, lo = u - 1, first_col(u - 1)
                        head = UNITS[v][2]
                        act.wait_ge(c_full, NU * g + v + 1)
                        if not (first and v < 2):
                            act.wait_ge(pv_done, NU * g + v - 1)
                        run(av[:, v % 2, lo:QC], ps[:, Z + v % 3, lo:QC], ACT.Exp, a_ready,
                            bias=bsb[:, bass.ds(2 * g + head, 1)])
                    if t < 8:
                        evac(g, first, t)
                        if t == 7:
                            evac(g, first, 8)
                    elif t < SLOTS and u % 2 == 1:
                        evac(g, first, 9 + u // 2)
                    if first and t in (4, 10):
                        gate_strips(t // 10)
                    if t == 15:
                        silu_mid(g, 0)
                    if t == 16:
                        decode_ln(g, 0)
                        silu_end(g, 0)
                    if t == 17:
                        decode_a(g, 0, first)
                    if t == 21:
                        silu_mid(g, 1)
                    if t == 22:
                        silu_end(g, 1)
                decode_ln(g, 1)
                evac(g, first, 21)
                evac(g, first, 22)
                evac(g, first, 23)
                decode_a(g, 1, first)
                act.wait_ge(ob_ready, g + 1)
                run(tmp[:, 0:SEQ], oT[:, :], ACT.Square, sq_done)
                act.wait_ge(bconv_ready, g + 1)
                run(gab[:, 0:SEQ], hcb[:, 0:SEQ], ACT.Square, sq_done)

            run_groups(act, body)

            act.wait_ge(ss_rstd, 1)
            for n in range(OUT_UNITS):
                t, j = divmod(n, 2)
                rows_ = P if t < TT else NB
                col = t if t < TT else 16
                if n == LAST_PV + 1:
                    act.wait_ge(e_w, 1)
                    run(tmp[:, 0:64], tmp[:, 64:128], ACT.Square, e_exp)
                if n == 2 * TT:
                    act.wait_ge(ss_rstd, 2)
                if t >= 2 and j == 0:
                    act.wait_ge(m_ready, 2 * t - 2)
                act.wait_ge(m_ps, n + 1)
                run(ma(t)[0:rows_, HALF * j:HALF * (j + 1)], ps[0:rows_, 2 * (n % 3), :],
                    ACT.Copy, ma_ready, scale=rs[0:rows_, col:col + 1])
                if j == 1:
                    act.wait_ge(m_ready, 2 * t + 2)
                    if t >= 2:
                        act.wait_ge(m_var, t - 1)
                    run(ma(t)[0:rows_], mm_(t)[0:rows_], ACT.Square, msq, accum_out=ss[0:rows_, 24 + t % 2:25 + t % 2])

        @block.vector
        def _(v):
            links = [0]

            def link(ins, base=None):
                links[0] += 1
                ins.then_inc(step_dve, 1)
                v.wait_ge(step_dve, links[0] if base is None else base + links[0])

            v.memset(ones[:, :], 1.0).then_inc(dve_const, 1)
            v.memset(nones[:, :], -1.0).then_inc(dve_const, 1)
            v.memset(qz[:, :, :], 0.0).then_inc(dve_const, 1)
            v.memset(cT, 0.0).then_inc(dve_const, 1)
            v.memset(hT[:, :, SEQ:NTP], 0.0).then_inc(dve_const, 1)
            v.memset(ub[:, 0:2], 0.0).then_inc(dve_const, 1)
            v.memset(apad[:, :, :], 0.0).then_inc(dve_const, 1)
            v.memset(ssb[:, :], 0.0).then_inc(dve_const, 1)
            v.memset(keep[:, :, :], 1.0).then_inc(dve_const, 1)
            v.memset(tsh[:, :, :], 0.0).then_inc(dve_const, 1)
            v.wait_ge(dve_const, 10)
            v.memset(keep[:, :, 0:1], 0.0).then_inc(dve_const, 1)
            v.wait_ge(pool_const, POOL_CONSTS)
            v.tensor_reduce(e32[:, :], ident[:, :].rearrange("p (a i) -> p i a", a=4), AX_X, ALU.add)\
                .then_inc(dve_const, 1)
            v.wait_ge(dve_const, 12)

            v.wait_ge(c_act, 3)
            v.scalar_tensor_tensor(cwk, cnat, 0.0, cwk, ALU.min, ALU.subtract).then_inc(c_w, 1)
            v.wait_ge(c_act, 4)
            v.tensor_tensor(cwk, cnat, cwk, ALU.mult).then_inc(c_silu, 1)
            v.wait_ge(cT_full, 1)
            v.tensor_copy(cT[:, :, 0:9], ps[:, MB, 0:9 * KT].rearrange("p (k c) -> p k c", k=KT)).then_inc(cT_copied, 1)
            v.wait_ge(par_full, 1)
            v.tensor_copy(par[:, :], ps[:, DB, 0:NPAR]).then_inc(par_copied, 1)
            v.tensor_copy(stT[:, :, :, :], ps[:, DB, 64:64 + 64].rearrange("p (g b w) -> p g b w", g=GROUPS, b=NB))\
                .then_inc(par_copied, 1)

            v.wait_ge(ssq, TT + 1)
            v.tensor_scalar(ss[:, 0:TT], ss[:, 0:TT], 1.0 / D, EPS, ALU.mult, ALU.add).then_inc(var_ready, 1)
            v.tensor_scalar(ss[0:NB, TT:TT + 1], ss[0:NB, TT:TT + 1], 1.0 / D, EPS, ALU.mult, ALU.add)\
                .then_inc(var_ready, 1)
            v.wait_ge(rstd_ready, 2)
            for t in range(TT):
                v.tensor_scalar(xy[:, t, :], xy[:, t, :], rs[:, t:t + 1], None, ALU.mult).then_inc(x_scaled, 1)
            v.tensor_scalar(xs, xs, rs[0:NB, TT:TT + 1], None, ALU.mult).then_inc(x_scaled, 1)
            for n in range(1, 2 * KT, 2):
                v.wait_ge(xT_full, n + 1)
                v.tensor_copy(hT[:, n // 2, HALF:SEQ], ps[:, n % 4, :]).then_inc(xT_dve, 1)
            v.wait_ge(xT_full, 2 * KT + 1)
            v.tensor_copy(hT[:, :, SEQ:NT], ps[:, MB, 128:128 + NB * KT].rearrange("p (k b) -> p k b", k=KT))\
                .then_inc(xT_sdve, 1)

            v.wait_ge(mod_ps, 1)
            mps = ps[:, MB, 256:256 + 9 * 2 * KT].rearrange("p (k c) -> p k c", c=9)
            link(v.tensor_tensor(mods[:, :, :], mps, par[:, R_BA:R_BA + 16].unsqueeze(2).to_broadcast([P, 16, 9]), ALU.add))
            link(v.tensor_scalar(mods[:, KT:, :], mods[:, KT:, :], 1.0, None, ALU.add))
            link(v.tensor_tensor(mods[:, KT:, :], mods[:, KT:, :],
                                 par[:, R_GP:R_GP + 8].unsqueeze(2).to_broadcast([P, KT, 9]), ALU.mult))
            v.wait_ge(xT_act, KT)
            v.wait_ge(xT_sdve, 1)
            link(v.tensor_tensor(hT[:, :, SEQ:NT], hT[:, :, SEQ:NT], mods[:, KT:, 1:9], ALU.mult))
            v.tensor_tensor(hT[:, :, SEQ:NT], hT[:, :, SEQ:NT], mods[:, 0:KT, 1:9], ALU.add).then_inc(h_ready, 1)
            for k in range(KT):
                v.tensor_scalar(hT[:, k, 0:SEQ], hT[:, k, 0:SEQ], mods[:, KT + k, 0:1], mods[:, k, 0:1],
                                ALU.mult, ALU.add).then_inc(h_ready, 1)
            PRO = links[0]

            def gates(n):
                cols = slice(HALF * n, HALF * (n + 1))
                gs = 3 * n
                if n == 0:
                    v.wait_ge(gate_in, 32)
                v.wait_ge(gate_ps, 2 * n + 1)
                v.tensor_tensor(gps[:, cols], ps[0:NB, DB, :], bb[0:NB, cols], ALU.add).then_inc(gate_step, 1)
                v.wait_ge(gate_step, gs + 1)
                v.tensor_tensor(gps[:, cols], gps[:, cols], gp[0:NB, cols], ALU.mult).then_inc(gate_step, 1)
                v.wait_ge(gate_step, gs + 2)
                v.wait_ge(gate_ps, 2 * n + 2)
                v.tensor_tensor(bb[:, cols], ps[:, DB, :], bb[:, cols], ALU.add).then_inc(gate_step, 1)
                v.wait_ge(gate_step, gs + 3)
                v.tensor_tensor(gp[:, cols], gp[:, cols], bb[:, cols], ALU.mult)
                if n == 1:
                    v.memset(ssa[:, :], 0.0).then_inc(ssa_zero, 1)
                    v.wait_ge(ssa_zero, 1)

            def seq_q(g, k):
                if k == 0 and isinstance(g, int):
                    v.wait_ge(qs_copied, 1)
                v.tensor_scalar(qsel[:, :], qsP[:, :], e32[:, bass.ds(2 * g + k, 1)], None, ALU.mult)\
                    .then_inc(qsel_ready, 1)

            def seq_q_copy(g, k):
                v.wait_ge(ms_full, MS * g + (M_QB1 if k else M_QB0) + 1)
                v.tensor_copy(qb[:, k, :], ps[:, MB, :]).then_inc(ms_free, 1)

            def body(g, first, last):
                links[0] = 0
                base = PRO + g * LINKS

                def lk(ins):
                    link(ins, base)

                def decode_scores(k):
                    lk(v.tensor_tensor(zb[:, :].rearrange("p (h r) -> p h r", h=NH), zd[:, k],
                                       bsb[:, :].unsqueeze(2).to_broadcast([P, NH, PAGES]), ALU.add))
                    v.tensor_scalar(zx[:, :], zb[:, :], CLAMP, None, ALU.min).then_inc(d_zx, 1)

                def decode_softplus(k):
                    v.wait_ge(d_ln, 2 * g + k + 1)
                    v.tensor_tensor(spd[:, :], zb[:, :], zx[:, :], ALU.max).then_inc(d_sp, 1)

                def decode_log_weights(k):
                    v.wait_ge(ms_full, MS * g + (M_CUM1 if k else M_CUM0) + 1)
                    tot = ps[:, MB, 256:512].rearrange("p (h r) -> p h r", h=NH)
                    lk(v.tensor_copy(tsh[:, :, 1:PAGES], tot[:, :, 0:PAGES - 1]))
                    lk(v.tensor_tensor_scan(tsc[:, :], keep[:, :, :].rearrange("p h r -> p (h r)"),
                                            tsh[:, :, :].rearrange("p h r -> p (h r)"), 0.0, ALU.mult, ALU.add))
                    ins = v.tensor_tensor(zb[:, :], ps[:, MB, 0:256], zb[:, :], ALU.add)
                    ins.then_inc(ms_free, 1)
                    v.wait_ge(ms_free, MS * g + (M_CUM1 if k else M_CUM0) + 1)
                    v.tensor_tensor(zb[:, :], zb[:, :], tsc[:, :], ALU.add).then_inc(d_t, 1)

                def own_heads(parity):
                    seq = 2 * g - parity
                    v.wait_ge(v_used, NPAIR * (seq + 1))
                    v.tensor_tensor(om[:, :].rearrange("p (h d) -> p h d", h=NH),
                                    ps[:, DB, :].rearrange("p (h d) -> p h d", h=NH),
                                    e32[:, 0:NH].unsqueeze(2).to_broadcast([P, NH, HD]), ALU.mult).then_inc(d_om, 1)

                def own_heads_copy(parity):
                    seq = 2 * g - parity
                    v.wait_ge(d_oT, seq + 1)
                    v.tensor_copy(osT[:, :, bass.ds(seq, 1)], ps[:, DB, 0:GROUPS].unsqueeze(2)).then_inc(d_free, 1)

                seq_q(g, 0)
                seq_q_copy(g, 0)
                for t in range(SLOTS):
                    u = t - 8
                    if t == 16:
                        v.wait_ge(red_done, 32 * g + 16)
                        decode_scores(0)
                    if u >= 0:
                        c, i, h = UNITS[u]
                        lo = first_col(u)
                        v.wait_ge(z_full, NU * g + u + 1)
                        v.tensor_scalar(zc[:, u % 2, lo:QC], ps[:, Z + u % 3, lo:QC], bsb[:, bass.ds(2 * g + h, 1)],
                                        CLAMP, ALU.add, ALU.min).then_inc(zc_ready, 1)
                    v.wait_ge(prod_ready, 32 * g + t + 1)
                    r = 2 * (t % 16)
                    v.tensor_reduce(zd[:, t // 16, :, r:r + 2],
                                    prod[:, t % 2].rearrange("p (j h d) -> p h j d", j=2, h=NH), AX_X, ALU.add)\
                        .then_inc(red_done, 1)
                    if u >= 0:
                        v.wait_ge(ln_done, NU * g + u + 1)
                        v.scalar_tensor_tensor(sp[:, u % 2, lo:QC], ps[:, Z + u % 3, lo:QC],
                                               bsb[:, bass.ds(2 * g + h, 1)], zc[:, u % 2, lo:QC],
                                               ALU.add, ALU.max).then_inc(sp_ready, 1)
                    if u >= 1:
                        add_later(g, u - 1)
                    if first and t in (6, 12):
                        gates(t // 12)
                    if t in (8, 9):
                        v.wait_ge(ms_full, MS * g + M_KN0 + t - 8 + 1)
                        v.tensor_copy(kN[:, 4 * (t - 8):4 * (t - 7), :],
                                      ps[:, MB, :].rearrange("p (t c) -> p t c", t=4)).then_inc(ms_free, 1)
                    if t == 10:
                        v.wait_ge(ms_full, MS * g + M_KNS + 1)
                        v.tensor_copy(kS[:, bass.ds(g * P, P)], ps[0:NB, MB, 0:P]).then_inc(ms_free, 1)
                    if t == 11:
                        seq_q(g, 1)
                    if t == 13:
                        seq_q_copy(g, 1)
                    if t in (15, 21):
                        silu_min(g, gcb if t == 15 else gab, t == 21)
                    if t in (16, 22):
                        silu_mul(g, gcb if t == 16 else gab, t == 22)
                    if t == 16:
                        decode_softplus(0)
                        if not first:
                            own_heads(1)
                    if t == 17:
                        if not first:
                            own_heads_copy(1)
                        decode_log_weights(0)
                    if t == 18:
                        out_copy(g, 0)
                v.wait_ge(red_done, 32 * g + 32)
                decode_scores(1)
                own_heads(0)
                add_later(g, NU - 1)
                v.wait_ge(pj_free, PJ * g + 21)
                lk(v.tensor_tensor(ub[:, 2:2 + NT], ub[:, 2:2 + NT], hcb[:, :], ALU.mult))
                decode_softplus(1)
                tap = lambda w: par[:, bass.ds(R_CW + 4 * w + g, 1)]
                lk(v.tensor_scalar(hcb[:, 0:SEQ], ub[:, 2:2 + SEQ], tap(2), None, ALU.mult))
                lk(v.scalar_tensor_tensor(hcb[:, 0:SEQ], ub[:, 1:1 + SEQ], tap(1), hcb[:, 0:SEQ], ALU.mult, ALU.add))
                lk(v.scalar_tensor_tensor(hcb[:, 0:SEQ], ub[:, 0:SEQ], tap(0), hcb[:, 0:SEQ], ALU.mult, ALU.add))
                out_copy(g, 1)
                own_heads_copy(0)
                decode_log_weights(1)
                v.scalar_tensor_tensor(yT[:, bass.ds(GROUPS + g, 1), :].rearrange("p a s -> p (a s)"), oT[:, :],
                                       par[:, bass.ds(R_GA + g, 1)], gab[:, 0:SEQ], ALU.mult, ALU.mult)
                v.tensor_copy(tail[:, bass.ds(g, 1), :].rearrange("p a s -> p (a s)"), ub[:, SEQ:SEQ + 2])
                v.tensor_copy(samp[:, 0, bass.ds(g, 1), :].rearrange("p a s -> p (a s)"), ub[:, 2 + SEQ:2 + NT])
                v.tensor_copy(samp[:, 2, bass.ds(g, 1), :].rearrange("p a s -> p (a s)"), gcb[:, SEQ:NT])
                v.tensor_copy(samp[:, 3, bass.ds(g, 1), :].rearrange("p a s -> p (a s)"), gab[:, SEQ:NT])
                v.wait_ge(pj_free, PJ * g + 24)
                v.tensor_copy(samp[:, 1, bass.ds(g, 1), :].rearrange("p a s -> p (a s)"), bcb[:, SEQ:NT])
                v.tensor_tensor(hcb[:, 0:SEQ], hcb[:, 0:SEQ], bcb[:, 0:SEQ], ALU.mult).then_inc(bconv_ready, 1)
                v.wait_ge(bconv_ready, g + 1)
                v.scalar_tensor_tensor(yT[:, bass.ds(g, 1), :].rearrange("p a s -> p (a s)"), hcb[:, 0:SEQ],
                                       par[:, bass.ds(R_GC + g, 1)], gcb[:, 0:SEQ], ALU.mult, ALU.mult)
                v.wait_ge(sq_done, 2 * g + 1)
                v.tensor_tensor(ssb[:, :], ssb[:, :], tmp[:, 0:SEQ], ALU.add)
                v.wait_ge(sq_done, 2 * g + 2)
                v.tensor_tensor(ssa[:, :], ssa[:, :], gab[:, 0:SEQ], ALU.add).then_inc(group_done, 1)
                v.wait_ge(group_done, g + 1)
                assert links[0] == LINKS, links

            def add_later(g, u):
                c, i, h = UNITS[u]
                lo, di = first_col(u), i - 4 * c
                v.wait_ge(c_full, NU * g + u + 1)
                if i == 0:
                    return
                fresh = P if di >= 0 else 0
                if fresh:
                    ins = v.tensor_copy(later[:, h, lo:lo + P], sp[:, u % 2, lo:lo + P])
                if lo + fresh < QC:
                    ins = v.tensor_tensor(later[:, h, lo + fresh:QC], later[:, h, lo + fresh:QC],
                                          sp[:, u % 2, lo + fresh:QC], ALU.add)
                ins.then_inc(later_ready, 1)

            def silu_min(g, x, k):
                v.wait_ge(s_ln, 2 * g + int(k) + 1)
                v.scalar_tensor_tensor(tmp[:, :], x[:, :], 0.0, tmp[:, :], ALU.min, ALU.subtract).then_inc(s_min, 1)

            def silu_mul(g, x, k):
                v.wait_ge(s_sig, 2 * g + int(k) + 1)
                v.tensor_tensor(x[:, :], x[:, :], tmp[:, :], ALU.mult).then_inc(silu_done, 1)

            def out_copy(g, c):
                v.wait_ge(pv_done, NU * g + (8 if c == 0 else NU))
                if c == 0:
                    v.wait_ge(kout, 16 * (g + 1))
                v.tensor_copy(oT[:, QC * c:QC * (c + 1)], ps[:, OB, :]).then_inc(o_free if c == 0 else ob_ready, 1)
                if c == 1:
                    v.wait_ge(ob_ready, g + 1)

            run_groups(v, body)

            links[0] = 0
            base = PRO + GROUPS * LINKS

            def lk(ins):
                link(ins, base)

            v.wait_ge(ss_ps, 1)
            v.tensor_scalar(ss[:, 0:16], ps[:, MB, 0:16], 1.0 / HALF, EPS, ALU.mult, ALU.add).then_inc(ss_var, 1)

            def last_sequence():
                v.wait_ge(v_used, NPAIR * NB)
                v.tensor_tensor(om[:, :].rearrange("p (h d) -> p h d", h=NH), ps[:, DB, :].rearrange("p (h d) -> p h d", h=NH),
                                e32[:, 0:NH].unsqueeze(2).to_broadcast([P, NH, HD]), ALU.mult).then_inc(d_om, 1)

            def decode_rows():
                v.wait_ge(d_oT, NB)
                v.tensor_copy(osT[:, :, NB - 1:NB], ps[:, DB, 0:GROUPS].unsqueeze(2)).then_inc(d_free, 1)
                v.wait_ge(d_free, NB)
                blk = lambda k: tmp[:, 32 * k:32 * k + 32].rearrange("p (g b) -> p g b", g=GROUPS)
                chan = lambda row: par[:, row:row + GROUPS].unsqueeze(2).to_broadcast([P, GROUPS, NB])
                lk(v.tensor_tensor(blk(2), stT[:, :, :, 0], chan(R_CW), ALU.mult))
                lk(v.tensor_tensor(blk(4), stT[:, :, :, 1], chan(R_CW + 4), ALU.mult))
                lk(v.tensor_tensor(blk(2), blk(2), blk(4), ALU.add))
                lk(v.tensor_tensor(blk(4), samp[:, 0], chan(R_CW + 8), ALU.mult))
                lk(v.tensor_tensor(blk(2), blk(2), blk(4), ALU.add))
                lk(v.tensor_tensor(blk(2), blk(2), samp[:, 1], ALU.mult))
                v.tensor_copy(blk(3), osT[:, :, :]).then_inc(e_w, 1)
                v.wait_ge(e_w, 1)
                lk(v.tensor_tensor(blk(4), blk(2), chan(R_GC), ALU.mult))
                lk(v.tensor_tensor(blk(5), blk(3), chan(R_GA), ALU.mult))
                v.tensor_tensor(blk(6), blk(4), samp[:, 2], ALU.mult).then_inc(e_ysT, 1)
                v.tensor_tensor(blk(7), blk(5), samp[:, 3], ALU.mult).then_inc(e_ysT, 1)
                v.wait_ge(conv_ps, 1)
                lk(v.tensor_copy(om[0:NB, :], ps[0:NB, DB, :]))
                v.tensor_copy(qb[0:2, 0, :], ps[0:2, MB, :]).then_inc(conv_sb, 1)
                v.wait_ge(ss_ps, 2)
                v.tensor_scalar(ss[0:NB, 16:18], ps[0:NB, MB, 16:18], 1.0 / HALF, EPS, ALU.mult, ALU.add)\
                    .then_inc(ss_var, 1)

            v.wait_ge(ss_rstd, 1)
            for n in range(OUT_UNITS):
                t, j = divmod(n, 2)
                rows_ = P if t < TT else NB
                col = 8 + t if t < TT else 17
                if n == LAST_PV:
                    last_sequence()
                if n == LAST_PV + 1:
                    decode_rows()
                if n == 2 * TT:
                    v.wait_ge(ss_rstd, 2)
                v.wait_ge(ma_ready, n + 1)
                if t >= 2 and j == 0:
                    v.wait_ge(msq, t - 1)
                half_cols = slice(HALF * j, HALF * (j + 1))
                v.scalar_tensor_tensor(mm_(t)[0:rows_, half_cols], ps[0:rows_, 2 * (n % 3) + 1, :],
                                       rs[0:rows_, col:col + 1], ma(t)[0:rows_, half_cols], ALU.mult, ALU.add)\
                    .then_inc(m_ready, 1)
                if j == 0:
                    continue
                v.wait_ge(msq, t + 1)
                v.tensor_scalar(ss[0:rows_, 20 + t % 2:21 + t % 2], ss[0:rows_, 24 + t % 2:25 + t % 2], 1.0 / D, EPS,
                                ALU.mult, ALU.add).then_inc(m_var, 1)
                v.wait_ge(m_rstd, t + 1)
                if t >= 2:
                    v.wait_ge(y_out[t % 2], 16 * (t // 2))
                gate = gp if t < TT else gps
                lk(v.scalar_tensor_tensor(yo(t)[0:rows_], mm_(t)[0:rows_], rs[0:rows_, 20 + t % 2:21 + t % 2],
                                          gate[0:rows_, :], ALU.mult, ALU.mult))
                v.wait_ge(xr_full[t % 4], 16 * (t // 4 + 1))
                v.tensor_tensor(yo(t)[0:rows_], yo(t)[0:rows_], kring[0:rows_, t % 4].rearrange("p j c -> p (j c)"),
                                ALU.add).then_inc(y_ready, 1)

        @block.tensor
        def _(pe):
            def mm(out, l, r, start, stop):
                return nc.tensor.matmul(out, l, r, start=start, stop=stop, skip_group_check=True)

            pe.wait_ge(pool_const, POOL_CONSTS)
            pe.wait_ge(c_silu, 1)
            for k in range(KT):
                last = nc.tensor.transpose(ps[:, MB, 9 * k:9 * k + 9], cwk[:, P * k:P * (k + 1)], ident[0:9, 0:9])
            last.then_inc(cT_full, 1)
            pe.wait_ge(small_in, 16 * N_SMALL)
            nc.tensor.transpose(ps[:, DB, 0:NPAR], parN, ident[0:NPAR, 0:NPAR])
            for g in range(GROUPS):
                last = nc.tensor.transpose(ps[:, DB, 64 + 16 * g:80 + 16 * g], stN[:, g, :], ident[0:16, 0:16])
            last.then_inc(par_full, 1)

            pe.wait_ge(dve_const, 12)
            pe.wait_ge(cT_copied, 1)

            def strips(bank, lhs, slot, n):
                pe.wait_ge(ada_full[n % 2], 16 * (n // 2 + 1))
                for k in range(KT):
                    j = k % 4
                    last = mm(ps[32 * j:32 * j + 32, bank, :], lhs(k), ada_slot[n % 2][:, k, :], k < 4, k >= 4)
                return last

            def ada(n, chunk):
                if n >= 2:
                    pe.wait_ge(ada_copied, n - 1)
                strips(PJB + n % 2, lambda k: cT[:, k, :], n % 2, chunk).then_inc(ada_ps, 1)

            ada(0, 0)
            ada(1, 1)
            ada(2, 2)
            pe.wait_ge(x_scaled, TT + 1)
            for n in range(2 * KT):
                if n == ADA3_AT:
                    ada(3, 3)
                if n >= 4:
                    pe.wait_ge(xT_dve if n % 2 else xT_act, (n - 4) // 2 + 1)
                for j in range(4):
                    last = nc.tensor.transpose(ps[:, n % 4, P * j:P * (j + 1)],
                                               xy[:, 4 * (n % 2) + j, P * (n // 2):P * (n // 2 + 1)], ident[:, :])
                last.then_inc(xT_full, 1)
            for k in range(KT):
                last = nc.tensor.transpose(ps[:, MB, P + NB * k:P + NB * (k + 1)], xs[:, P * k:P * (k + 1)],
                                           ident[0:NB, 0:NB])
            last.then_inc(xT_full, 1)
            pe.wait_ge(ada_copied, 4)
            pe.wait_ge(xT_sdve, 1)
            for k in range(2 * KT):
                last = mm(ps[:, MB, 256 + 9 * k:265 + 9 * k], ada_cols(P * k, P), e32[:, 0:9], True, True)
            last.then_inc(mod_ps, 1)
            pe.wait_ge(h_ready, 1)
            pe.wait_ge(par_copied, 2)
            strips(DB, lambda k: hT[:, k, SEQ:NTP], 0, 4).then_inc(qs_ps, 1)
            pe.wait_ge(h_ready, KT + 1)
            pe.wait_ge(qs_copied, 1)
            pe.wait_ge(ada_copied, 4)

            def gate_strips(n):
                if n:
                    pe.wait_ge(gate_step, 3)
                strips(DB, lambda k: cT[:, k, :], 1, 5 + 2 * n).then_inc(ada_ps, 1)

            def gate_sums(n):
                pe.wait_ge(ada_copied, 5 + n)
                mm(ps[0:NB, DB, :], e32[:, 1:9], ada_cols(2048 + HALF * n, HALF), True, True).then_inc(gate_ps, 1)
                pe.wait_ge(gate_step, 3 * n + 1)
                mm(ps[:, DB, :], e32[:, 0:1].to_broadcast([P, P]), ada_cols(2048 + HALF * n, HALF), True, True)\
                    .then_inc(gate_ps, 1)

            def body(g, first, last_):
                def project(m, part, chunk, ks=range(KT)):
                    if ks[0] == 0:
                        if chunk == 0:
                            pe.wait_ge(w_full[part % 4], 16 * (2 * g + part // 4 + 1))
                        if not (first and m < 2):
                            pe.wait_ge(pj_free, PJ * g + m - 1)
                    for k in ks:
                        last = mm(ps[:, PJB + m % 2, 0:CH], wsl[:, part % 4, k, :], hT[:, k, CH * chunk:CH * (chunk + 1)],
                                  k == 0, k == KT - 1)
                    if ks[-1] == KT - 1:
                        last.then_inc(pj_full, 1)

                def values(m):
                    pe.wait_ge(pj_free, PJ * g + m - 1)
                    if m == 6:
                        pe.wait_ge(w_full[V_], 16 * (2 * g + 1))
                    if m < 8:
                        for j in range(4):
                            for k in range(KT):
                                t = 4 * (m - 6) + j
                                last = mm(ps[:, PJB + m % 2, P * j:P * (j + 1)], hT[:, k, P * t:P * (t + 1)],
                                          wsl[:, V_, k, :], k == 0, k == KT - 1)
                    else:
                        for k in range(KT):
                            last = mm(ps[0:NB, PJB + m % 2, 0:P], hT[:, k, SEQ:NT], wsl[:, V_, k, :], k == 0, k == KT - 1)
                    last.then_inc(pj_full, 1)

                def misc_ready(n):
                    if not (first and n == 0):
                        pe.wait_ge(ms_free, MS * g + n)

                def spread_q(k):
                    misc_ready(M_QB1 if k else M_QB0)
                    pe.wait_ge(qsel_ready, 2 * g + k + 1)
                    mm(ps[:, MB, :], ones[:, :], qsel[:, :], True, True).then_inc(ms_full, 1)

                def cumulate(k):
                    misc_ready(M_CUM1 if k else M_CUM0)
                    pe.wait_ge(d_sp, 2 * g + k + 1)
                    mm(ps[:, MB, 0:256], ntri[:, :], spd[:, :], True, True)
                    mm(ps[:, MB, 256:512], nones[:, :], spd[:, :], True, True).then_inc(ms_full, 1)

                def page_values(t):
                    parity, prs = pairs_of(t)
                    if first and parity == 1:
                        return
                    for rr in prs:
                        value_pair(2 * g - parity, 32 * g - 16 * parity + rr, rr, 2 * g - parity)

                def own_heads_T(parity):
                    pe.wait_ge(d_om, 2 * g - parity + 1)
                    heads_T(2 * g - parity)

                def scores(u):
                    c, i, h = UNITS[u]
                    lo = first_col(u)
                    if u == 0:
                        pe.wait_ge(pj_free, PJ * g + 6)
                    if not (first and u < 3):
                        pe.wait_ge(a_ready, NU * g + u - 2)
                    last = mm(ps[:, Z + u % 3, lo:QC], kT[:, P * i:P * (i + 1)], qz[:, h, QC * c + lo:QC * (c + 1)],
                              True, False)
                    if i >= 4 * c:
                        last = mm(ps[:, Z + u % 3, lo:lo + P], ident_b[:, :], unseen[:, :], False, False)
                    last.then_inc(z_full, 1)

                def suffix(u):
                    c, i, h = UNITS[u]
                    lo, di = first_col(u), i - 4 * c
                    pe.wait_ge(sp_ready, NU * g + u + 1)
                    seen = min(QC, lo + (P if di >= 0 else 0))
                    if seen < QC:
                        pe.wait_ge(later_ready, len(RUPD) * g + RUPD.index(u - 2) + 1)
                        mm(ps[:, Z + u % 3, seen:QC], nones[:, :], later[:, h, seen:QC], False, False)
                    mm(ps[:, Z + u % 3, lo:QC], ntri[:, :], sp[:, u % 2, lo:QC], False, True).then_inc(c_full, 1)

                def outputs(u):
                    c, i, h = UNITS[u]
                    lo = first_col(u)
                    pe.wait_ge(a_ready, NU * g + u + 1)
                    if u == 0:
                        pe.wait_ge(pj_free, PJ * g + 8)
                        if not first:
                            pe.wait_ge(ob_ready, g)
                    if u == 8:
                        pe.wait_ge(o_free, g + 1)
                    mm(ps[HD * h:HD * (h + 1), OB, lo:QC], vN[:, i, HD * h:HD * (h + 1)], av[:, u % 2, lo:QC],
                       i == 4 * c + 3, i == 0).then_inc(pv_done, 1)

                def key_rows(n):
                    misc_ready(M_KN0 + n)
                    if n < 2:
                        for j in range(4):
                            last = nc.tensor.transpose(ps[:, MB, P * j:P * (j + 1)],
                                                       kT[:, P * (4 * n + j):P * (4 * n + j + 1)], ident[:, :])
                    else:
                        last = nc.tensor.transpose(ps[0:NB, MB, 0:P], kT[:, SEQ:NT], ident[:, :])
                    last.then_inc(ms_full, 1)

                for t in range(8):
                    if t < 3:
                        project(t, Q_, t)
                    elif t < 6:
                        project(t, K_, t - 3)
                    else:
                        values(t)
                    if t == 2:
                        spread_q(0)
                    if first and t == 4:
                        gate_strips(0)
                    if first and t == 6:
                        gate_sums(0)
                    page_values(t)
                values(8)
                for t in range(8, SLOTS + 2):
                    u = t - 8
                    if u < NU:
                        scores(u)
                        m = 9 + u // 2
                        ks = range(0, 4) if u % 2 == 0 else range(4, 8)
                        part, chunk = GC_ + (m - 9) // 3, (m - 9) % 3
                        project(m, part, chunk, ks[0:2])
                        if t == 17:
                            cumulate(0)
                    else:
                        project(21 + u - NU, BC_, u - NU)
                    if 1 <= u <= NU:
                        suffix(u - 1)
                    if u < NU:
                        project(m, part, chunk, ks[2:4])
                    if u >= 2:
                        outputs(u - 2)
                    if t in (8, 9, 10):
                        key_rows(t - 8)
                    if first and t == 9:
                        gate_strips(1)
                    if first and t == 12:
                        gate_sums(1)
                    if t == 12:
                        spread_q(1)
                    if t == 16 and not first:
                        own_heads_T(1)
                    page_values(t)
                project(23, BC_, 2)
                own_heads_T(0)
                cumulate(1)

            def value_pair(seq, q, rr, done_before):
                if rr == 0:
                    pe.wait_ge(d_a, seq + 1)
                    if not (isinstance(seq, int) and seq == 0):
                        pe.wait_ge(d_free, done_before)
                pe.wait_ge(v_full[rr % 4], v_fill(seq, rr))
                for j in range(2):
                    r = 2 * rr + j
                    strip = 32 * (r % 4)
                    last = mm(ps[strip:strip + 32, DB, :], apad[:, :, r], vring[:, rr % 4, j, :], r < 4, r >= PAGES - 4)
                last.then_inc(v_used, 1)

            def v_fill(seq, rr):
                return 32 * (4 * seq + rr // 4 + 1)

            def heads_T(seq):
                for c in range(GROUPS):
                    last = mm(ps[:, DB, c:c + 1], om[:, P * c:P * (c + 1)], ones[:, 0:1], True, True)
                last.then_inc(d_oT, 1)

            run_groups(pe, body)

            def last_pair(rr):
                value_pair(NB - 1, 16 * (NB - 1) + rr, rr, NB - 1)

            def decode_sums():
                pe.wait_ge(d_free, NB)
                for c in range(GROUPS):
                    nc.tensor.transpose(ps[0:NB, DB, P * c:P * (c + 1)], samp[:, 0, c, :], ident[:, :])
                pe.wait_ge(ss_var, 1)
                for c in range(GROUPS):
                    last = nc.tensor.transpose(ps[0:2, MB, P * c:P * (c + 1)], tail[:, c, :], ident[:, :])
                last.then_inc(conv_ps, 1)
                pe.wait_ge(conv_sb, 1)
                pe.wait_ge(e_exp, 1)
                for b in range(2):
                    for c in range(GROUPS):
                        last = mm(ps[0:NB, MB, 16 + b:17 + b], tmp[:, 32 * b + 8 * c:32 * b + 8 * c + 8], ones[:, 0:1],
                                  c == 0, c == GROUPS - 1)
                last.then_inc(ss_ps, 1)

            def out_unit(n, ks):
                t, j = divmod(n, 2)
                rows_ = P if t < TT else NB
                for k in ks:
                    for b in range(2):
                        if n == 0:
                            pe.wait_ge(wo_full[GROUPS * b + k], 16)
                        lhs = yT[:, GROUPS * b + k, P * t:P * (t + 1)] if t < TT else tmp_s(b, k)
                        last = mm(ps[0:rows_, 2 * (n % 3) + b, :], lhs, wo(GROUPS * b + k)[:, HALF * j:HALF * (j + 1)],
                                  k == 0, k == GROUPS - 1)
                if k == GROUPS - 1:
                    last.then_inc(m_ps, 1)

            pe.wait_ge(group_done, GROUPS - 1)
            for n in range(3):
                if n == 1:
                    pe.wait_ge(ob_ready, GROUPS)
                if n == 2:
                    pe.wait_ge(pj_free, PJ * GROUPS)
                out_unit(n, range(GROUPS - 1))
            pe.wait_ge(group_done, GROUPS)
            pe.wait_ge(ms_free, MS * GROUPS)
            for b, src in enumerate((ssa, ssb)):
                for t in range(TT):
                    last = mm(ps[:, MB, 8 * b + t:8 * b + t + 1], src[:, P * t:P * (t + 1)], ones[:, 0:1], True, True)
            last.then_inc(ss_ps, 1)

            for rr in range(4):
                last_pair(rr)
            for n in range(OUT_UNITS):
                if n == 2 * TT:
                    pe.wait_ge(e_ysT, 2)
                if n >= 3:
                    pe.wait_ge(m_ready, n - 2)
                out_unit(n, range(GROUPS) if n >= 3 else [GROUPS - 1])
                if n < LAST_PV:
                    last_pair(4 + n)
                if n == LAST_PV:
                    pe.wait_ge(d_om, NB)
                    heads_T(NB - 1)
                if n == LAST_PV + 1:
                    decode_sums()


_INS = ["x_prompt", "x_sample", "c_prompt", "c_sample", "cache_k", "cache_v", "state_conv", "page_table",
        "w_ada", "b_ada", "g_pre", "w_in", "conv_w", "g_conv", "b_sb", "g_attn", "w_out", "g_post"]
_OUTS = [(1, SEQ, D), (NB, 1, D), (1, 1, SEQ, NH, HD), (1, 1, SEQ, NH, HD), (1, 1, 2, HALF),
         (1, NB, 1, NH, HD), (1, NB, 1, NH, HD), (1, NB, 2, HALF)]


def kernel(**inputs):
    import numpy as _np
    import concourse.bacc as _bacc
    from concourse import mybir as _mybir
    from concourse.bass_utils import run_bass_kernel_spmd as _run

    nc = _bacc.Bacc("TRN2", target_bir_lowering=False, num_devices=1, dynamic_dma_scratch_size=1024)
    nc.disable_value_cache = True
    arrays, args = {}, []
    for name in _INS:
        a = _np.ascontiguousarray(inputs[name])
        arrays[f"in_{name}_dram"] = a
        args.append(nc.dram_tensor(f"in_{name}_dram", a.shape, _mybir.dt.from_np(a.dtype), kind="ExternalInput").ap())
    for i, shape in enumerate(_OUTS):
        args.append(nc.dram_tensor(f"out_{i}_dram", shape, _mybir.dt.float32, kind="ExternalOutput").ap())
    stick_breaking_mixer(nc, *args)
    r = _run(nc, [arrays], core_ids=[0])
    return tuple(r.results[0][f"out_{i}_dram"] for i in range(len(_OUTS)))
```

```python
from contextlib import ExitStack

import concourse.bass as bass
from concourse import mybir

F32 = mybir.dt.float32
BF16 = mybir.dt.bfloat16
F32R = mybir.dt.float32r
I32 = mybir.dt.int32
ALU = mybir.AluOpType
ACT = mybir.ActivationFunctionType
AX_X = mybir.AxisListType.X

P = 128
D = 1024
KT = D // P
SEQ = 1024
TT = SEQ // P
NB = 8
NT = SEQ + NB
NTP = SEQ + 32
CH = NT // 3
HALF = 512
GROUPS = HALF // P
HD = 64
NH = 8
QC = 512
PAGES = 32
NPAIR = PAGES // 2
EPS = 1e-6
CLAMP = 40.0
HIDE = -2.0 ** 100
ADA_AT = (6, 14)
OUT_UNITS = 2 * (TT + 1)
WO_ORDER = [0, 4, 1, 5, 2, 6, 3, 7]
LAST_PV = NPAIR - 4
POOL_CONSTS = 9
SLOTS = 32
ACT_SET = "natural_log_exp_and_others"

Q_, K_, V_, GC_, GA_, HC_, CC_, BC_ = range(8)
PART = [4, 5, 6, 3, 7, 0, 2, 1]
PJ = 24
MS = 7
M_QB0, M_KN0, M_KN1, M_KNS, M_QB1, M_CUM0, M_CUM1 = range(MS)
UNITS = [(c, i, h) for c in range(2) for i in range(4 * c + 3, -1, -1) for h in range(2)]
NU = len(UNITS)
RUPD = [u for u, (c, i, h) in enumerate(UNITS) if i > 0]

R_BA, R_GP, R_CW, R_GC, R_GA, NPAR = 0, 16, 24, 36, 40, 44

LINKS = 10


def first_col(u):
    c, i, h = UNITS[u]
    return max(0, P * (i - 4 * c))


def pairs_of(slot):
    for parity, slots, doubles in ((1, range(1, 16), (7,)), (0, range(20, SLOTS), (23, 25, 27, 29))):
        if slot in slots:
            n = slot - slots[0] + sum(d < slot for d in doubles)
            return parity, [n, n + 1] if slot in doubles else [n]
    return 0, []


def stick_breaking_mixer(nc, x_prompt, x_sample, c_prompt, c_sample, cache_k, cache_v, state_conv,
                         page_table, w_ada, b_ada, g_pre, w_in, conv_w, g_conv, b_sb, g_attn, w_out,
                         g_post, y_prompt, y_sample, k_prompt, v_prompt, conv_prompt, k_sample,
                         v_sample, conv_sample):
    ctx = ExitStack()
    with ctx:
        ctx.enter_context(nc.allow_non_contiguous_dma(reason="per-channel rows of 512 bytes"))

        def sb(name, shape, dt=F32):
            return ctx.enter_context(nc.sbuf_tensor(name, shape, dt))

        def sem(name):
            return ctx.enter_context(nc.semaphore(name))

        hT = sb("hT", [P, KT, NTP])
        xy = sb("xy", [P, TT, D])
        ring = sb("ring", [P, 8192])
        wsl = sb("wsl", [P, 2, KT, P])
        qz = sb("qz", [P, 2, SEQ])
        kT = sb("kT", [P, NT])
        vN = sb("vN", [P, TT, P])
        gcb = sb("gcb", [P, NT])
        gab = sb("gab", [P, NT])
        hcb = sb("hcb", [P, NT])
        ub = sb("ub", [P, 2 + NT])
        bcb = sb("bcb", [P, NT])
        tmp = sb("tmp", [P, NT])
        oT = sb("oT", [P, SEQ])
        ssa = sb("ssa", [P, SEQ])
        ssb = sb("ssb", [P, SEQ])
        sp = sb("sp", [P, 2, QC])
        sp_hi = sb("sp_hi", [P, 2, QC], F32R)
        sp_lo = sb("sp_lo", [P, 2, QC], F32R)
        av = sb("av", [P, 2, QC])
        later = sb("later", [P, 2, QC])
        later_hi = sb("later_hi", [P, QC], F32R)
        later_lo = sb("later_lo", [P, QC], F32R)
        qsP = sb("qsP", [P, HALF])
        qb = sb("qb", [P, 2, HALF])
        prod = sb("prod", [P, 2, 2 * HALF])
        zd = sb("zd", [P, 2, NH, PAGES])
        zb = sb("zb", [P, NH * PAGES])
        zx = sb("zx", [P, NH * PAGES])
        tsc = zx
        spd = sb("spd", [P, NH * PAGES])
        tsh = sb("tsh", [P, NH, PAGES])
        keep = sb("keep", [P, NH, PAGES])
        apad = sb("apad", [P, 32, PAGES])
        om = sb("om", [P, HALF])
        osT = sb("osT", [P, GROUPS, NB])
        samp = sb("samp", [P, 4, GROUPS, NB])
        tail = sb("tail", [P, GROUPS, 2])
        ident = sb("ident", [P, P])
        e32 = sb("e32", [P, 32])
        ntri = sb("ntri", [P, P], F32R)
        nones = sb("nones", [P, P], F32R)
        unseen = sb("unseen", [P, P], BF16)
        ident_b = sb("ident_b", [P, P], BF16)
        ones = sb("ones", [P, P])
        par = sb("par", [P, NPAR])
        bsb = sb("bsb", [P, NH])
        gp = sb("gp", [P, D])
        rows = sb("rows", [64, D])
        pages = sb("pages", [1, NB * PAGES], I32)
        stT = sb("stT", [P, GROUPS, NB, 2])
        mods = sb("mods", [P, 2 * KT, 9])
        ss = sb("ss", [P, 32])
        rs = sb("rs", [P, 32])
        half = sb("half", [P, 16])

        kring = ring[:, 0:4096].rearrange("p (s j c) -> p s j c", s=4, j=2)
        vring = ring[:, 4096:8192].rearrange("p (s j c) -> p s j c", s=4, j=2)
        ada_slot = [ring[:, 4096 * i:4096 * (i + 1)].rearrange("p (k c) -> p k c", k=KT) for i in range(2)]
        yT = xy
        kN = oT[:, :].rearrange("p (t c) -> p t c", t=TT)
        qsel = om
        gps = rows[0:NB, :]
        kS, vS = rows[32:32 + NB, 0:HALF], rows[32:32 + NB, HALF:D]

        ps = ctx.enter_context(nc.psum_tensor("ps", [P, 8, HALF], F32))
        Z, OB, PJB, DB, MB = 0, 3, 4, 6, 7

        c_in = sem("c_in"); small_in = sem("small_in"); gate_in = sem("gate_in")
        x_in = [sem(f"x_in{i}") for i in range(2)]
        ada_full = [sem(f"ada_full{i}") for i in range(2)]
        w_full = [sem(f"w_full{i}") for i in range(2)]
        k_full = [sem(f"k_full{i}") for i in range(4)]
        v_full = [sem(f"v_full{i}") for i in range(4)]; v_used = sem("v_used")
        pool_const = sem("pool_const"); dve_const = sem("dve_const")
        c_w = sem("c_w"); c_act = sem("c_act"); c_silu = sem("c_silu")
        cT_full = sem("cT_full"); cT_copied = sem("cT_copied")
        par_full = sem("par_full"); par_copied = sem("par_copied")
        ssq = sem("ssq"); var_ready = sem("var_ready"); rstd_ready = sem("rstd_ready")
        x_scaled = sem("x_scaled"); xT_full = sem("xT_full")
        xT_act = sem("xT_act"); xT_dve = sem("xT_dve"); xT_sdve = sem("xT_sdve")
        ada_ps = sem("ada_ps"); ada_copied = sem("ada_copied")
        mod_ps = sem("mod_ps"); h_ready = sem("h_ready")
        qs_ps = sem("qs_ps"); qs_copied = sem("qs_copied")
        gate_ps = sem("gate_ps"); gate_step = sem("gate_step"); ssa_zero = sem("ssa_zero")
        step_dve = sem("step_dve")
        pj_full = sem("pj_full"); pj_free = sem("pj_free")
        ms_full = sem("ms_full"); ms_free = sem("ms_free")
        qsel_ready = sem("qsel_ready")
        z_full = sem("z_full"); zc_ready = sem("zc_ready"); exp_done = sem("exp_done")
        ln_done = sem("ln_done"); sp_ready = sem("sp_ready")
        hi_ready = sem("hi_ready"); lo_ready = sem("lo_ready")
        later_hi_ready = sem("later_hi_ready"); later_lo_ready = sem("later_lo_ready")
        c_full = sem("c_full"); later_ready = sem("later_ready")
        a_ready = sem("a_ready"); pv_done = sem("pv_done")
        o_free = sem("o_free")
        prod_ready = sem("prod_ready"); red_done = sem("red_done")
        d_zx = sem("d_zx"); d_exp = sem("d_exp"); d_ln = sem("d_ln"); d_sp = sem("d_sp")
        d_t = sem("d_t"); d_a = sem("d_a")
        d_om = sem("d_om"); d_oT = sem("d_oT"); d_free = sem("d_free")
        s_abs = sem("s_abs"); s_exp = sem("s_exp"); s_ln = sem("s_ln"); s_min = sem("s_min"); silu_done = sem("silu_done")
        s_sig = sem("s_sig")
        ob_ready = sem("ob_ready"); bconv_ready = sem("bconv_ready"); sq_done = sem("sq_done")
        group_done = sem("group_done")
        kout = sem("kout"); vout = sem("vout"); out_done = sem("out_done")
        wo_full = [sem(f"wo_full{k}") for k in range(KT)]; xr_full = [sem(f"xr_full{i}") for i in range(4)]
        e_w = sem("e_w"); e_exp = sem("e_exp"); e_ysT = sem("e_ysT")
        ss_ps = sem("ss_ps"); ss_var = sem("ss_var"); ss_rstd = sem("ss_rstd")
        conv_ps = sem("conv_ps"); conv_sb = sem("conv_sb")
        m_ps = sem("m_ps"); ma_ready = sem("ma_ready"); m_ready = sem("m_ready")
        msq = sem("msq"); m_var = sem("m_var"); m_rstd = sem("m_rstd"); y_ready = sem("y_ready")
        y_out = [sem(f"y_out{i}") for i in range(2)]

        tri, minus1 = av[:, 0, 0:P], av[:, 1, 0:P]
        xs = bcb[0:NB, 0:D]
        cnat = gcb[0:9, 0:D]
        cwk = gab[0:9, 0:D]
        parN = qb[0:NPAR, 0, 0:P]
        stN = qb[0:2 * NB, 1, :].rearrange("p (r c) -> p r c", c=P)
        cT = zb[:, :].rearrange("p (k c) -> p k c", k=KT)
        bb = ub[:, 2:2 + D]
        adaA = prod[:, :, :].rearrange("p a b -> p (a b)")
        adaB = ssa[:, :]

        def wo(k):
            early = {WO_ORDER[0]: qz[:, 0, :], WO_ORDER[1]: qz[:, 1, :],
                     WO_ORDER[2]: wsl[:, 0, :, :].rearrange("p k c -> p (k c)")}
            return early.get(k, hT[:, k, 0:D])

        def ma(t):
            return (gcb if t % 2 else gab)[:, 0:D]

        def mm_(t):
            return (hcb if t % 2 else bcb)[:, 0:D]

        def yo(t):
            return (ub if t % 2 else oT)[:, 0:D]

        def tmp_s(b, k):
            return tmp[:, 192 + 32 * b + 8 * k:200 + 32 * b + 8 * k]

        def ada_cols(lo, n):
            return adaA[:, lo:lo + n] if lo < 2048 else adaB[:, lo - 2048:lo - 2048 + n]

        N_SMALL = 9

        def run_groups(eng, body, last_differs=False):
            body(0, True, False)
            if last_differs:
                with eng.Fori(1, GROUPS - 1) as g:
                    body(g, False, False)
                body(GROUPS - 1, False, True)
            else:
                with eng.Fori(1, GROUPS) as g:
                    body(g, False, False)

        block = ctx.enter_context(nc.Block())

        @block.sync
        def _(sp_e):
            def bcast(ap, n):
                return ap.to_broadcast([P, n])

            ada_v = w_ada.rearrange("a (k p) (n c) -> n p (a k) c", p=P, c=HALF)
            w_v = w_in.rearrange("a (k p) (s g c) -> s g p (a k) c", p=P, s=8, g=GROUPS)
            x_v = x_prompt.rearrange("b (h t p) d -> h p (b t) d", p=P, h=2)

            def load_w(g, s):
                src = w_v[PART[s]][bass.ds(g, 1)].rearrange("a p k c -> (a p) k c")
                sp_e.dma_start(wsl[:, s % 2, :, :], src).then_inc(w_full[s % 2], 16)

            ADA_FREE = {2: 1, 3: 2, 4: 3, 5: 4, 7: 5}

            def load_ada(n, src):
                if n >= 2:
                    sp_e.wait_ge(ada_ps, ADA_FREE[n])
                sp_e.dma_start(ada_slot[n % 2], src).then_inc(ada_full[n % 2], 16)

            sp_e.dma_start(cnat[0:1, :], c_prompt).then_inc(c_in, 16)
            sp_e.dma_start(cnat[1:9, :], c_sample).then_inc(c_in, 16)
            sp_e.dma_start(xy[:, 0:4, :], x_v[0]).then_inc(x_in[0], 16)
            sp_e.dma_start(xy[:, 4:8, :], x_v[1]).then_inc(x_in[1], 16)
            load_ada(0, ada_v[0])
            sp_e.dma_start(xs, x_sample.rearrange("b l d -> (b l) d")).then_inc(small_in, 16)
            sp_e.dma_start(parN[R_BA:R_BA + 16, :],
                           b_ada[:, 0:2048].rearrange("a (r c) -> (a r) c", c=P)).then_inc(small_in, 16)
            sp_e.dma_start(parN[R_GP:R_GP + 8, :],
                           g_pre.rearrange("a (r c) -> (a r) c", c=P)).then_inc(small_in, 16)
            sp_e.dma_start(parN[R_CW:R_CW + 12, :],
                           conv_w.rearrange("a w (r c) -> (a w r) c", c=P)).then_inc(small_in, 16)
            sp_e.dma_start(parN[R_GC:R_GC + 4, :],
                           g_conv.rearrange("a (r c) -> (a r) c", c=P)).then_inc(small_in, 16)
            sp_e.dma_start(parN[R_GA:R_GA + 4, :],
                           g_attn.rearrange("a (r c) -> (a r) c", c=P)).then_inc(small_in, 16)
            sp_e.dma_start(stN, state_conv.rearrange("a b w (r c) -> (a b w) r c", c=P)).then_inc(small_in, 16)
            sp_e.dma_start(bsb[:, :], bcast(b_sb, NH)).then_inc(small_in, 16)
            sp_e.dma_start(pages[:, :], page_table.rearrange("(a b) n -> a (b n)", a=1)).then_inc(small_in, 16)
            sp_e.dma_start(conv_sample[0, :, 0, :], state_conv[0, :, 1, :]).then_inc(out_done, 16)

            load_ada(1, ada_v[1])
            load_ada(2, ada_v[2])
            load_ada(3, ada_v[3])
            load_ada(4, w_in[0, :, 2048:2560].rearrange("(k p) c -> p k c", p=P))
            load_w(0, 0)
            load_w(0, 1)
            sp_e.dma_start(gp[:, :], bcast(g_post, D)).then_inc(gate_in, 16)
            sp_e.dma_start(bb, bcast(b_ada[:, 2048:3072], D)).then_inc(gate_in, 16)
            load_ada(5, ada_v[4])
            sp_e.wait_ge(small_in, 16 * N_SMALL)
            sp_e.wait_ge(qs_ps, 1)

            def pair_numbers(seq, r):
                _, numbers = nc.values_load_multi_w_load_instructions(
                    pages[0:1, bass.ds(seq * PAGES + (PAGES - 2 - r), 2)], engines=[mybir.EngineType.SP],
                    min_val=0, max_val=cache_k.shape[1] - 1)
                return numbers

            def load_pair(dst, cache, numbers, full):
                for j in range(2):
                    src = cache[0][bass.ds(numbers[1 - j], 1)].rearrange("a p h d -> (a p) (h d)")
                    sp_e.dma_start(dst[:, j, :], src).then_inc(full, 16)

            wo_v = w_out.rearrange("a (k p) n -> k p (a n)", p=P)

            def load_wo(k):
                sp_e.dma_start(wo(k), wo_v[k]).then_inc(wo_full[k], 16)

            def load_v(seq, rr, used):
                numbers = pair_numbers(seq, 2 * rr)
                if used is not None:
                    sp_e.wait_ge(v_used, used)
                load_pair(vring[:, rr % 4], cache_v, numbers, v_full[rr % 4])

            def body(g, first, last):
                for t in range(SLOTS):
                    numbers = pair_numbers(2 * g + t // 16, 2 * (t % 16))
                    if not (first and t < 4):
                        sp_e.wait_ge(prod_ready, 32 * g + t - 3)
                    load_pair(kring[:, t % 4], cache_k, numbers, k_full[t % 4])
                    if first and t == 5:
                        load_ada(7, ada_v[5])
                    parity, prs = pairs_of(t)
                    if first and t == 20:
                        sp_e.wait_ge(ada_ps, 6)
                    if not (first and parity == 1):
                        for rr in prs:
                            seq = 2 * g - parity
                            q = 32 * g - 16 * parity + rr
                            load_v(seq, rr, None if first and rr < 4 else q - 3)
                    for slot, s in ((0, K_), (3, V_), (6, GC_), (8, GA_), (14, HC_), (20, CC_), (26, BC_)):
                        if slot == t and not (first and s == K_):
                            sp_e.wait_ge(pj_full, PJ * g + 3 * (s - 1))
                            load_w(g, s)
                    if t == 12:
                        sp_e.wait_ge(pj_free, PJ * g + 8)
                        sp_e.dma_start(v_prompt.rearrange("a b (t p) (g h) d -> g (a b) p t (h d)", p=P, g=GROUPS)[
                            bass.ds(g, 1)].rearrange("a b p t c -> (a b p) t c"), vN[:, :, :]).then_inc(vout, 16)
                    if t == 13:
                        sp_e.wait_ge(ms_free, MS * g + M_KN1 + 1)
                        sp_e.dma_start(k_prompt.rearrange("a b (t p) (g h) d -> g (a b) p t (h d)", p=P, g=GROUPS)[
                            bass.ds(g, 1)].rearrange("a b p t c -> (a b p) t c"), kN[:, :, :]).then_inc(kout, 16)

                if not last:
                    sp_e.wait_ge(pj_full, PJ * g + 21)
                    load_w(g + 1, Q_)

            run_groups(sp_e, body, last_differs=True)

            def last_values(rrs):
                for rr in rrs:
                    load_v(NB - 1, rr, 32 * GROUPS - 16 + rr - 3)

            sp_e.wait_ge(z_full, NU * GROUPS)
            load_wo(WO_ORDER[0])
            load_wo(WO_ORDER[1])
            sp_e.wait_ge(pj_full, PJ * GROUPS - 3)
            load_wo(WO_ORDER[2])
            last_values(range(4))
            sp_e.wait_ge(pj_full, PJ * GROUPS)
            for k in WO_ORDER[3:]:
                load_wo(k)
            sp_e.wait_ge(prod_ready, 32 * GROUPS)
            xr_v = x_prompt.rearrange("b (t p) d -> t (b p) d", p=P)

            def load_residual(t):
                dst = kring[:, t % 4].rearrange("p j c -> p (j c)")
                if t < TT:
                    sp_e.dma_start(dst, xr_v[t]).then_inc(xr_full[t % 4], 16)
                else:
                    sp_e.dma_start(dst[0:NB, :], x_sample.rearrange("b l d -> (b l) d")).then_inc(xr_full[t % 4], 16)

            for t in range(4):
                load_residual(t)
                last_values(range(4 + 3 * t, 7 + 3 * t))
            sp_e.wait_ge(ms_free, MS * GROUPS)
            sp_e.wait_ge(pj_free, PJ * GROUPS)
            sp_e.dma_start(k_sample.rearrange("a b l h d -> (a b l) (h d)"), kS[:, :]).then_inc(out_done, 16)
            sp_e.dma_start(v_sample.rearrange("a b l h d -> (a b l) (h d)"), vS[:, :]).then_inc(out_done, 16)
            for t in range(TT + 1):
                sp_e.wait_ge(y_ready, t + 1)
                if t < TT:
                    sp_e.dma_start(y_prompt.rearrange("b (t p) d -> t (b p) d", p=P)[t], yo(t)).then_inc(y_out[t % 2], 16)
                else:
                    sp_e.dma_start(y_sample.rearrange("b l d -> (b l) d"), yo(t)[0:NB, :]).then_inc(y_out[t % 2], 16)
                if t + 4 <= TT:
                    load_residual(t + 4)
                if t == TT - 2:
                    sp_e.wait_ge(conv_sb, 1)
                    sp_e.dma_start(conv_sample[0, :, 1, :], om[0:NB, :]).then_inc(out_done, 16)
                    sp_e.dma_start(conv_prompt[0, 0], qb[0:2, 0, :]).then_inc(out_done, 16)
            sp_e.wait_ge(out_done, 16 * 5)
            sp_e.wait_ge(kout, 16 * GROUPS)
            sp_e.wait_ge(vout, 16 * GROUPS)
            sp_e.wait_ge(y_out[0], 16 * 5)
            sp_e.wait_ge(y_out[1], 16 * 4)

        @block.gpsimd
        def _(pool):
            pool.memset(ident[:, :], 0.0).then_inc(pool_const, 1)
            pool.memset(tri, -1.0).then_inc(pool_const, 1)
            pool.memset(half[:, :], -0.5).then_inc(pool_const, 1)
            pool.memset(unseen[:, :], HIDE).then_inc(pool_const, 1)
            pool.memset(ident_b[:, :], 0.0).then_inc(pool_const, 1)
            pool.wait_ge(pool_const, 5)
            pool.affine_select(out=ident[:, :], in_=ident[:, :], compare_op=ALU.not_equal, fill=1.0, base=0,
                               pattern=[[-1, P]], channel_multiplier=1).then_inc(pool_const, 1)
            pool.affine_select(out=tri, in_=tri, compare_op=ALU.is_ge, fill=0.0, base=0,
                               pattern=[[-1, P]], channel_multiplier=1).then_inc(pool_const, 1)
            pool.affine_select(out=unseen[:, :], in_=unseen[:, :], compare_op=ALU.is_ge, fill=0.0, base=0,
                               pattern=[[-1, P]], channel_multiplier=1).then_inc(pool_const, 1)
            pool.affine_select(out=ident_b[:, :], in_=ident_b[:, :], compare_op=ALU.not_equal, fill=1.0, base=0,
                               pattern=[[-1, P]], channel_multiplier=1).then_inc(pool_const, 1)
            pool.wait_ge(var_ready, 2)
            pool.tensor_tensor(rs[:, 0:TT], ss[:, 0:TT], half[:, 0:TT], ALU.pow).then_inc(rstd_ready, 1)
            pool.tensor_tensor(rs[0:NB, TT:TT + 1], ss[0:NB, TT:TT + 1], half[0:NB, 0:1], ALU.pow).then_inc(rstd_ready, 1)

            def body(g, first, last):
                for t in range(SLOTS):
                    if t % 16 == 0:
                        pool.wait_ge(ms_free, MS * g + (M_QB1 if t else M_QB0) + 1)
                    pool.wait_ge(k_full[t % 4], 32 * (8 * g + t // 4 + 1))
                    if not (first and t < 2):
                        pool.wait_ge(red_done, 32 * g + t - 1)
                    pool.tensor_tensor(
                        prod[:, t % 2].rearrange("p (j c) -> p j c", j=2), kring[:, t % 4],
                        qb[:, t // 16].unsqueeze(1).to_broadcast([P, 2, HALF]), ALU.mult).then_inc(prod_ready, 1)
                    if t - 10 in RUPD:
                        u = t - 10
                        pool.wait_ge(later_hi_ready, len(RUPD) * g + RUPD.index(u) + 1)
                        pool.tensor_tensor(later_lo[:, first_col(u):QC], later[:, UNITS[u][2], first_col(u):QC],
                                           later_hi[:, first_col(u):QC], ALU.subtract).then_inc(later_lo_ready, 1)

            run_groups(pool, body)
            pool.wait_ge(ss_var, 1)
            pool.tensor_tensor(rs[:, 0:16], ss[:, 0:16], half[:, 0:16], ALU.pow).then_inc(ss_rstd, 1)
            for t in range(TT + 1):
                n = P if t < TT else NB
                if t == TT - 1:
                    pool.wait_ge(ss_var, 2)
                    pool.tensor_tensor(rs[0:NB, 16:18], ss[0:NB, 16:18], half[0:NB, 0:2], ALU.pow).then_inc(ss_rstd, 1)
                pool.wait_ge(m_var, t + 1)
                pool.tensor_tensor(rs[0:n, 20 + t % 2:21 + t % 2], ss[0:n, 20 + t % 2:21 + t % 2],
                                   half[0:n, 0:1], ALU.pow).then_inc(m_rstd, 1)

        @block.scalar
        def _(act):
            def run(out, in_, func, done, **kw):
                nc.scalar.activation(out, in_, func, **kw).then_inc(done, 1)

            act.preload_act_table_set(ACT_SET)
            act.wait_ge(c_in, 32)
            run(cwk, cnat, ACT.Abs, c_act)
            act.wait_ge(c_act, 1)
            run(cwk, cwk, ACT.Exp, c_act, scale=-1.0)
            act.wait_ge(c_act, 2)
            run(cwk, cwk, ACT.Ln, c_act, bias=1.0)
            act.wait_ge(c_w, 1)
            run(cwk, cwk, ACT.Exp, c_act)
            for t in range(TT):
                if t % 4 == 0:
                    act.wait_ge(x_in[t // 4], 16)
                if t >= 2:
                    act.wait_ge(ssq, t - 1)
                run((tmp if t % 2 else hcb)[:, 0:D], xy[:, t, :], ACT.Square, ssq, accum_out=ss[:, t:t + 1])
            act.wait_ge(ssq, TT)
            act.wait_ge(small_in, 16 * N_SMALL)
            run(tmp[0:NB, 0:D], xs, ACT.Square, ssq, accum_out=ss[0:NB, TT:TT + 1])

            def ada_copy(n):
                act.wait_ge(ada_ps, n + 1)
                run(ada_cols(HALF * n, HALF), ps[:, PJB + n % 2, :], ACT.Copy, ada_copied)

            for n in range(2):
                ada_copy(n)
            for n in range(0, 2 * KT, 2):
                if n in ADA_AT:
                    ada_copy(2 + ADA_AT.index(n))
                act.wait_ge(xT_full, n + 1)
                run(hT[:, n // 2, 0:HALF], ps[:, n % 4, :], ACT.Copy, xT_act)
            act.wait_ge(qs_ps, 1)
            run(qsP[:, :], ps[:, DB, :], ACT.Copy, qs_copied, scale=HD ** -0.5)

            def gate_strips(n):
                act.wait_ge(ada_ps, 5 + n)
                run(ada_cols(HALF * (4 + n), HALF), ps[:, DB, :], ACT.Copy, ada_copied)

            def evac(g, first, m):
                act.wait_ge(pj_full, PJ * g + m + 1)
                src = ps[:, PJB + m % 2, :]
                if m < 3:
                    n = CH if m < 2 else SEQ - 2 * CH
                    cols = slice(CH * m, CH * m + n)
                    nc.scalar.activation(qz[0:HD, 0, cols], src[0:HD, 0:n], ACT.Copy, scale=HD ** -0.5)
                    run(qz[HD:P, 1, cols], src[HD:P, 0:n], ACT.Copy, pj_free, scale=HD ** -0.5)
                elif m < 6:
                    run(kT[:, CH * (m - 3):CH * (m - 2)], src[:, 0:CH], ACT.Copy, pj_free)
                elif m < 8:
                    if m == 6 and not first:
                        act.wait_ge(vout, 16 * g)
                    run(vN[:, 4 * (m - 6):4 * (m - 5), :], src.rearrange("p (t c) -> p t c", t=4), ACT.Copy, pj_free)
                elif m == 8:
                    run(vS[:, bass.ds(g * P, P)], src[0:NB, 0:P], ACT.Copy, pj_free)
                else:
                    s, c = (m - 9) // 3, (m - 9) % 3
                    buf, off = ((gcb, 0), (gab, 0), (hcb, 0), (ub, 2), (bcb, 0))[s]
                    if m == 9 and not first:
                        act.wait_ge(group_done, g)
                    run(buf[:, off + CH * c:off + CH * (c + 1)], src[:, 0:CH], ACT.Copy, pj_free)

            def silu_step(g, k, step):
                if step == 0:
                    act.wait_ge(pj_free, PJ * g + (15 if k else 12))
                    if k:
                        act.wait_ge(silu_done, 2 * g + 1)
                    run(tmp[:, :], (gab if k else gcb)[:, :], ACT.Abs, s_abs)
                elif step == 1:
                    act.wait_ge(s_abs, 2 * g + k + 1)
                    run(tmp[:, :], tmp[:, :], ACT.Exp, s_exp, scale=-1.0)
                else:
                    act.wait_ge(s_exp, 2 * g + k + 1)
                    run(tmp[:, :], tmp[:, :], ACT.Ln, s_ln, bias=1.0)

            def silu_end(g, k):
                act.wait_ge(s_min, 2 * g + k + 1)
                run(tmp[:, :], tmp[:, :], ACT.Exp, s_sig)

            def decode_ln(g, k):
                act.wait_ge(d_zx, 2 * g + k + 1)
                run(zx[:, :], zx[:, :], ACT.Exp, d_exp)
                act.wait_ge(d_exp, 2 * g + k + 1)
                run(zx[:, :], zx[:, :], ACT.Ln, d_ln, bias=1.0)

            def decode_a(g, k, first):
                act.wait_ge(d_t, 2 * g + k + 1)
                if not (first and k == 0):
                    act.wait_ge(v_used, 32 * g - 16 + 16 * k + 16)
                run(apad[:, 0:NH, :], zb[:, :].rearrange("p (h r) -> p h r", h=NH), ACT.Exp, d_a)

            def body(g, first, last):
                act.preload_act_table_set(ACT_SET)
                for t in range(SLOTS + 1):
                    u = t - 8
                    if 0 <= u < NU:
                        lo, z = first_col(u), sp[:, u % 2, first_col(u):QC]
                        act.wait_ge(zc_ready, NU * g + u + 1)
                        run(z, z, ACT.Exp, exp_done)
                        act.wait_ge(exp_done, NU * g + u + 1)
                        run(z, z, ACT.Ln, ln_done, bias=1.0)
                    if 1 <= u <= NU:
                        v, lo = u - 1, first_col(u - 1)
                        head = UNITS[v][2]
                        act.wait_ge(c_full, NU * g + v + 1)
                        if not (first and v < 2):
                            act.wait_ge(pv_done, NU * g + v - 1)
                        run(av[:, v % 2, lo:QC], ps[:, Z + v % 3, lo:QC], ACT.Exp, a_ready,
                            bias=bsb[:, bass.ds(2 * g + head, 1)])
                    if 0 <= u < NU:
                        act.wait_ge(sp_ready, NU * g + u + 1)
                        run(sp_hi[:, u % 2, first_col(u):QC], z, ACT.Copy, hi_ready)
                    if u - 2 in RUPD:
                        w, lo = u - 2, first_col(u - 2)
                        act.wait_ge(later_ready, len(RUPD) * g + RUPD.index(w) + 1)
                        run(later_hi[:, lo:QC], later[:, UNITS[w][2], lo:QC], ACT.Copy, later_hi_ready)
                    if t < 8:
                        evac(g, first, t)
                        if t == 7:
                            evac(g, first, 8)
                    elif t < SLOTS and u % 2 == 1:
                        evac(g, first, 9 + u // 2)
                    if first and t in (4, 10):
                        gate_strips(t // 10)
                    if t in (14, 15, 16):
                        silu_step(g, 0, t - 14)
                    if t in (20, 21, 22):
                        silu_step(g, 1, t - 20)
                    if t in (18, 24):
                        silu_end(g, int(t == 24))
                    if t == 17:
                        decode_ln(g, 0)
                    if t == 19:
                        decode_a(g, 0, first)
                decode_ln(g, 1)
                evac(g, first, 21)
                evac(g, first, 22)
                evac(g, first, 23)
                decode_a(g, 1, first)
                act.wait_ge(ob_ready, g + 1)
                run(tmp[:, 0:SEQ], oT[:, :], ACT.Square, sq_done)
                act.wait_ge(bconv_ready, g + 1)
                run(gab[:, 0:SEQ], hcb[:, 0:SEQ], ACT.Square, sq_done)

            run_groups(act, body)

            act.wait_ge(ss_rstd, 1)
            for n in range(OUT_UNITS):
                t, j = divmod(n, 2)
                rows_ = P if t < TT else NB
                col = t if t < TT else 16
                if n == LAST_PV + 1:
                    act.wait_ge(e_w, 1)
                    run(tmp[:, 0:64], tmp[:, 64:128], ACT.Square, e_exp)
                if n == 2 * TT:
                    act.wait_ge(ss_rstd, 2)
                if t >= 2 and j == 0:
                    act.wait_ge(m_ready, 2 * t - 2)
                act.wait_ge(m_ps, n + 1)
                run(ma(t)[0:rows_, HALF * j:HALF * (j + 1)], ps[0:rows_, 2 * (n % 3), :],
                    ACT.Copy, ma_ready, scale=rs[0:rows_, col:col + 1])
                if j == 1:
                    act.wait_ge(m_ready, 2 * t + 2)
                    if t >= 2:
                        act.wait_ge(m_var, t - 1)
                    run(ma(t)[0:rows_], mm_(t)[0:rows_], ACT.Square, msq, accum_out=ss[0:rows_, 24 + t % 2:25 + t % 2])

        @block.vector
        def _(v):
            links = [0]

            def link(ins, base=None):
                links[0] += 1
                ins.then_inc(step_dve, 1)
                v.wait_ge(step_dve, links[0] if base is None else base + links[0])

            v.memset(ones[:, :], 1.0).then_inc(dve_const, 1)
            v.memset(minus1, -1.0).then_inc(dve_const, 1)
            v.memset(qz[:, :, :], 0.0).then_inc(dve_const, 1)
            v.memset(cT, 0.0).then_inc(dve_const, 1)
            v.memset(hT[:, :, SEQ:NTP], 0.0).then_inc(dve_const, 1)
            v.memset(ub[:, 0:2], 0.0).then_inc(dve_const, 1)
            v.memset(apad[:, :, :], 0.0).then_inc(dve_const, 1)
            v.memset(ssb[:, :], 0.0).then_inc(dve_const, 1)
            v.memset(keep[:, :, :], 1.0).then_inc(dve_const, 1)
            v.memset(tsh[:, :, :], 0.0).then_inc(dve_const, 1)
            v.wait_ge(dve_const, 10)
            v.memset(keep[:, :, 0:1], 0.0).then_inc(dve_const, 1)
            v.wait_ge(pool_const, POOL_CONSTS)
            v.tensor_reduce(e32[:, :], ident[:, :].rearrange("p (a i) -> p i a", a=4), AX_X, ALU.add)\
                .then_inc(dve_const, 1)
            v.tensor_copy(ntri[:, :], tri).then_inc(dve_const, 1)
            v.tensor_copy(nones[:, :], minus1).then_inc(dve_const, 1)
            v.wait_ge(dve_const, 14)

            v.wait_ge(c_act, 3)
            v.scalar_tensor_tensor(cwk, cnat, 0.0, cwk, ALU.min, ALU.subtract).then_inc(c_w, 1)
            v.wait_ge(c_act, 4)
            v.tensor_tensor(cwk, cnat, cwk, ALU.mult).then_inc(c_silu, 1)
            v.wait_ge(cT_full, 1)
            v.tensor_copy(cT[:, :, 0:9], ps[:, MB, 0:9 * KT].rearrange("p (k c) -> p k c", k=KT)).then_inc(cT_copied, 1)
            v.wait_ge(par_full, 1)
            v.tensor_copy(par[:, :], ps[:, DB, 0:NPAR]).then_inc(par_copied, 1)
            v.tensor_copy(stT[:, :, :, :], ps[:, DB, 64:64 + 64].rearrange("p (g b w) -> p g b w", g=GROUPS, b=NB))\
                .then_inc(par_copied, 1)

            v.wait_ge(ssq, TT + 1)
            v.tensor_scalar(ss[:, 0:TT], ss[:, 0:TT], 1.0 / D, EPS, ALU.mult, ALU.add).then_inc(var_ready, 1)
            v.tensor_scalar(ss[0:NB, TT:TT + 1], ss[0:NB, TT:TT + 1], 1.0 / D, EPS, ALU.mult, ALU.add)\
                .then_inc(var_ready, 1)
            v.wait_ge(rstd_ready, 2)
            for t in range(TT):
                v.tensor_scalar(xy[:, t, :], xy[:, t, :], rs[:, t:t + 1], None, ALU.mult).then_inc(x_scaled, 1)
            v.tensor_scalar(xs, xs, rs[0:NB, TT:TT + 1], None, ALU.mult).then_inc(x_scaled, 1)
            for n in range(1, 2 * KT, 2):
                v.wait_ge(xT_full, n + 1)
                v.tensor_copy(hT[:, n // 2, HALF:SEQ], ps[:, n % 4, :]).then_inc(xT_dve, 1)
            v.wait_ge(xT_full, 2 * KT + 1)
            v.tensor_copy(hT[:, :, SEQ:NT], ps[:, MB, 128:128 + NB * KT].rearrange("p (k b) -> p k b", k=KT))\
                .then_inc(xT_sdve, 1)

            v.wait_ge(mod_ps, 1)
            mps = ps[:, MB, 256:256 + 9 * 2 * KT].rearrange("p (k c) -> p k c", c=9)
            link(v.tensor_tensor(mods[:, :, :], mps, par[:, R_BA:R_BA + 16].unsqueeze(2).to_broadcast([P, 16, 9]), ALU.add))
            link(v.tensor_scalar(mods[:, KT:, :], mods[:, KT:, :], 1.0, None, ALU.add))
            link(v.tensor_tensor(mods[:, KT:, :], mods[:, KT:, :],
                                 par[:, R_GP:R_GP + 8].unsqueeze(2).to_broadcast([P, KT, 9]), ALU.mult))
            v.wait_ge(xT_act, KT)
            v.wait_ge(xT_sdve, 1)
            link(v.tensor_tensor(hT[:, :, SEQ:NT], hT[:, :, SEQ:NT], mods[:, KT:, 1:9], ALU.mult))
            v.tensor_tensor(hT[:, :, SEQ:NT], hT[:, :, SEQ:NT], mods[:, 0:KT, 1:9], ALU.add).then_inc(h_ready, 1)
            for c in range(3):
                cols = slice(CH * c, min(CH * (c + 1), SEQ))
                for k in range(KT):
                    v.tensor_scalar(hT[:, k, cols], hT[:, k, cols], mods[:, KT + k, 0:1], mods[:, k, 0:1],
                                    ALU.mult, ALU.add).then_inc(h_ready, 1)
            PRO = links[0]

            def gates(n):
                cols = slice(HALF * n, HALF * (n + 1))
                gs = 3 * n
                if n == 0:
                    v.wait_ge(gate_in, 32)
                v.wait_ge(gate_ps, 2 * n + 1)
                v.tensor_tensor(gps[:, cols], ps[0:NB, DB, :], bb[0:NB, cols], ALU.add).then_inc(gate_step, 1)
                v.wait_ge(gate_step, gs + 1)
                v.tensor_tensor(gps[:, cols], gps[:, cols], gp[0:NB, cols], ALU.mult).then_inc(gate_step, 1)
                v.wait_ge(gate_step, gs + 2)
                v.wait_ge(gate_ps, 2 * n + 2)
                v.tensor_tensor(bb[:, cols], ps[:, DB, :], bb[:, cols], ALU.add).then_inc(gate_step, 1)
                v.wait_ge(gate_step, gs + 3)
                v.tensor_tensor(gp[:, cols], gp[:, cols], bb[:, cols], ALU.mult)
                if n == 1:
                    v.memset(ssa[:, :], 0.0).then_inc(ssa_zero, 1)
                    v.wait_ge(ssa_zero, 1)

            def seq_q(g, k):
                if k == 0 and isinstance(g, int):
                    v.wait_ge(qs_copied, 1)
                v.tensor_scalar(qsel[:, :], qsP[:, :], e32[:, bass.ds(2 * g + k, 1)], None, ALU.mult)\
                    .then_inc(qsel_ready, 1)

            def seq_q_copy(g, k):
                v.wait_ge(ms_full, MS * g + (M_QB1 if k else M_QB0) + 1)
                v.tensor_copy(qb[:, k, :], ps[:, MB, :]).then_inc(ms_free, 1)

            def body(g, first, last):
                links[0] = 0
                base = PRO + g * LINKS

                def lk(ins):
                    link(ins, base)

                def decode_scores(k):
                    lk(v.tensor_tensor(zb[:, :].rearrange("p (h r) -> p h r", h=NH), zd[:, k],
                                       bsb[:, :].unsqueeze(2).to_broadcast([P, NH, PAGES]), ALU.add))
                    v.tensor_scalar(zx[:, :], zb[:, :], CLAMP, None, ALU.min).then_inc(d_zx, 1)

                def decode_softplus(k):
                    v.wait_ge(d_ln, 2 * g + k + 1)
                    v.tensor_tensor(spd[:, :], zb[:, :], zx[:, :], ALU.max).then_inc(d_sp, 1)

                def decode_log_weights(k):
                    v.wait_ge(ms_full, MS * g + (M_CUM1 if k else M_CUM0) + 1)
                    tot = ps[:, MB, 256:512].rearrange("p (h r) -> p h r", h=NH)
                    lk(v.tensor_copy(tsh[:, :, 1:PAGES], tot[:, :, 0:PAGES - 1]))
                    lk(v.tensor_tensor_scan(tsc[:, :], keep[:, :, :].rearrange("p h r -> p (h r)"),
                                            tsh[:, :, :].rearrange("p h r -> p (h r)"), 0.0, ALU.mult, ALU.add))
                    ins = v.tensor_tensor(zb[:, :], ps[:, MB, 0:256], zb[:, :], ALU.add)
                    ins.then_inc(ms_free, 1)
                    v.wait_ge(ms_free, MS * g + (M_CUM1 if k else M_CUM0) + 1)
                    v.tensor_tensor(zb[:, :], zb[:, :], tsc[:, :], ALU.add).then_inc(d_t, 1)

                def own_heads(parity):
                    seq = 2 * g - parity
                    v.wait_ge(v_used, NPAIR * (seq + 1))
                    v.tensor_tensor(om[:, :].rearrange("p (h d) -> p h d", h=NH),
                                    ps[:, DB, :].rearrange("p (h d) -> p h d", h=NH),
                                    e32[:, 0:NH].unsqueeze(2).to_broadcast([P, NH, HD]), ALU.mult).then_inc(d_om, 1)

                def own_heads_copy(parity):
                    seq = 2 * g - parity
                    v.wait_ge(d_oT, seq + 1)
                    v.tensor_copy(osT[:, :, bass.ds(seq, 1)], ps[:, DB, 0:GROUPS].unsqueeze(2)).then_inc(d_free, 1)

                seq_q(g, 0)
                seq_q_copy(g, 0)
                for t in range(SLOTS):
                    u = t - 8
                    if t == 17:
                        v.wait_ge(red_done, 32 * g + 16)
                        decode_scores(0)
                    if u >= 0:
                        c, i, h = UNITS[u]
                        lo = first_col(u)
                        v.wait_ge(z_full, NU * g + u + 1)
                        if not (first and u < 2):
                            v.wait_ge(lo_ready, NU * g + u - 1)
                        if u - 2 in RUPD:
                            v.wait_ge(later_ready, len(RUPD) * g + RUPD.index(u - 2) + 1)
                        v.tensor_scalar(sp[:, u % 2, lo:QC], ps[:, Z + u % 3, lo:QC], bsb[:, bass.ds(2 * g + h, 1)],
                                        CLAMP, ALU.add, ALU.min).then_inc(zc_ready, 1)
                    if t > 0:
                        reduce_pair(g, t - 1)
                    if u >= 0:
                        v.wait_ge(ln_done, NU * g + u + 1)
                        v.scalar_tensor_tensor(sp[:, u % 2, lo:QC], ps[:, Z + u % 3, lo:QC],
                                               bsb[:, bass.ds(2 * g + h, 1)], sp[:, u % 2, lo:QC],
                                               ALU.add, ALU.max).then_inc(sp_ready, 1)
                    if u >= 1:
                        add_later(g, u - 1, first)
                    if u >= 0:
                        if not (first and u < 2):
                            v.wait_ge(c_full, NU * g + u - 1)
                        v.wait_ge(hi_ready, NU * g + u + 1)
                        v.tensor_tensor(sp_lo[:, u % 2, lo:QC], sp[:, u % 2, lo:QC], sp_hi[:, u % 2, lo:QC],
                                        ALU.subtract).then_inc(lo_ready, 1)
                    if first and t in (6, 12):
                        gates(t // 12)
                    if t in (8, 9):
                        v.wait_ge(ms_full, MS * g + M_KN0 + t - 8 + 1)
                        v.tensor_copy(kN[:, 4 * (t - 8):4 * (t - 7), :],
                                      ps[:, MB, :].rearrange("p (t c) -> p t c", t=4)).then_inc(ms_free, 1)
                    if t == 10:
                        v.wait_ge(ms_full, MS * g + M_KNS + 1)
                        v.tensor_copy(kS[:, bass.ds(g * P, P)], ps[0:NB, MB, 0:P]).then_inc(ms_free, 1)
                    if t == 11:
                        seq_q(g, 1)
                    if t == 13:
                        seq_q_copy(g, 1)
                    if t in (17, 23):
                        silu_min(g, gcb if t == 17 else gab, t == 23)
                    if t in (19, 25):
                        silu_mul(g, gcb if t == 19 else gab, t == 25)
                    if t == 16 and not first:
                        own_heads(1)
                    if t == 17:
                        if not first:
                            own_heads_copy(1)
                        decode_softplus(0)
                    if t == 19:
                        decode_log_weights(0)
                    if t == 18:
                        out_copy(g, 0)
                reduce_pair(g, SLOTS - 1)
                v.wait_ge(red_done, 32 * g + 32)
                decode_scores(1)
                own_heads(0)
                v.wait_ge(pj_free, PJ * g + 21)
                lk(v.tensor_tensor(ub[:, 2:2 + NT], ub[:, 2:2 + NT], hcb[:, :], ALU.mult))
                decode_softplus(1)
                tap = lambda w: par[:, bass.ds(R_CW + 4 * w + g, 1)]
                lk(v.tensor_scalar(hcb[:, 0:SEQ], ub[:, 2:2 + SEQ], tap(2), None, ALU.mult))
                lk(v.scalar_tensor_tensor(hcb[:, 0:SEQ], ub[:, 1:1 + SEQ], tap(1), hcb[:, 0:SEQ], ALU.mult, ALU.add))
                lk(v.scalar_tensor_tensor(hcb[:, 0:SEQ], ub[:, 0:SEQ], tap(0), hcb[:, 0:SEQ], ALU.mult, ALU.add))
                out_copy(g, 1)
                own_heads_copy(0)
                decode_log_weights(1)
                v.scalar_tensor_tensor(yT[:, bass.ds(GROUPS + g, 1), :].rearrange("p a s -> p (a s)"), oT[:, :],
                                       par[:, bass.ds(R_GA + g, 1)], gab[:, 0:SEQ], ALU.mult, ALU.mult)
                v.tensor_copy(tail[:, bass.ds(g, 1), :].rearrange("p a s -> p (a s)"), ub[:, SEQ:SEQ + 2])
                v.tensor_copy(samp[:, 0, bass.ds(g, 1), :].rearrange("p a s -> p (a s)"), ub[:, 2 + SEQ:2 + NT])
                v.tensor_copy(samp[:, 2, bass.ds(g, 1), :].rearrange("p a s -> p (a s)"), gcb[:, SEQ:NT])
                v.tensor_copy(samp[:, 3, bass.ds(g, 1), :].rearrange("p a s -> p (a s)"), gab[:, SEQ:NT])
                v.wait_ge(pj_free, PJ * g + 24)
                v.tensor_copy(samp[:, 1, bass.ds(g, 1), :].rearrange("p a s -> p (a s)"), bcb[:, SEQ:NT])
                v.tensor_tensor(hcb[:, 0:SEQ], hcb[:, 0:SEQ], bcb[:, 0:SEQ], ALU.mult).then_inc(bconv_ready, 1)
                v.wait_ge(bconv_ready, g + 1)
                v.scalar_tensor_tensor(yT[:, bass.ds(g, 1), :].rearrange("p a s -> p (a s)"), hcb[:, 0:SEQ],
                                       par[:, bass.ds(R_GC + g, 1)], gcb[:, 0:SEQ], ALU.mult, ALU.mult)
                v.wait_ge(sq_done, 2 * g + 1)
                v.tensor_tensor(ssb[:, :], ssb[:, :], tmp[:, 0:SEQ], ALU.add)
                v.wait_ge(sq_done, 2 * g + 2)
                v.tensor_tensor(ssa[:, :], ssa[:, :], gab[:, 0:SEQ], ALU.add).then_inc(group_done, 1)
                v.wait_ge(group_done, g + 1)
                assert links[0] == LINKS, links

            def reduce_pair(g, t):
                v.wait_ge(prod_ready, 32 * g + t + 1)
                r = 2 * (t % 16)
                v.tensor_reduce(zd[:, t // 16, :, r:r + 2],
                                prod[:, t % 2].rearrange("p (j h d) -> p h j d", j=2, h=NH), AX_X, ALU.add)\
                    .then_inc(red_done, 1)

            def add_later(g, u, first):
                c, i, h = UNITS[u]
                lo, di = first_col(u), i - 4 * c
                if u not in RUPD:
                    return
                before = RUPD.index(u) - 1
                if before > 0:
                    v.wait_ge(later_lo_ready, len(RUPD) * g + before)
                elif not first:
                    v.wait_ge(later_lo_ready, len(RUPD) * g)
                fresh = P if di >= 0 else 0
                if fresh:
                    ins = v.tensor_copy(later[:, h, lo:lo + P], sp[:, u % 2, lo:lo + P])
                if lo + fresh < QC:
                    ins = v.tensor_tensor(later[:, h, lo + fresh:QC], later[:, h, lo + fresh:QC],
                                          sp[:, u % 2, lo + fresh:QC], ALU.add)
                ins.then_inc(later_ready, 1)

            def silu_min(g, x, k):
                v.wait_ge(s_ln, 2 * g + int(k) + 1)
                v.scalar_tensor_tensor(tmp[:, :], x[:, :], 0.0, tmp[:, :], ALU.min, ALU.subtract).then_inc(s_min, 1)

            def silu_mul(g, x, k):
                v.wait_ge(s_sig, 2 * g + int(k) + 1)
                v.tensor_tensor(x[:, :], x[:, :], tmp[:, :], ALU.mult).then_inc(silu_done, 1)

            def out_copy(g, c):
                v.wait_ge(pv_done, NU * g + (8 if c == 0 else NU))
                if c == 0:
                    v.wait_ge(kout, 16 * (g + 1))
                v.tensor_copy(oT[:, QC * c:QC * (c + 1)], ps[:, OB, :]).then_inc(o_free if c == 0 else ob_ready, 1)
                if c == 1:
                    v.wait_ge(ob_ready, g + 1)

            run_groups(v, body)

            links[0] = 0
            base = PRO + GROUPS * LINKS

            def lk(ins):
                link(ins, base)

            v.wait_ge(ss_ps, 1)
            v.tensor_scalar(ss[:, 0:16], ps[:, MB, 0:16], 1.0 / HALF, EPS, ALU.mult, ALU.add).then_inc(ss_var, 1)

            def last_sequence():
                v.wait_ge(v_used, NPAIR * NB)
                v.tensor_tensor(om[:, :].rearrange("p (h d) -> p h d", h=NH), ps[:, DB, :].rearrange("p (h d) -> p h d", h=NH),
                                e32[:, 0:NH].unsqueeze(2).to_broadcast([P, NH, HD]), ALU.mult).then_inc(d_om, 1)

            def decode_rows():
                v.wait_ge(d_oT, NB)
                v.tensor_copy(osT[:, :, NB - 1:NB], ps[:, DB, 0:GROUPS].unsqueeze(2)).then_inc(d_free, 1)
                v.wait_ge(d_free, NB)
                blk = lambda k: tmp[:, 32 * k:32 * k + 32].rearrange("p (g b) -> p g b", g=GROUPS)
                chan = lambda row: par[:, row:row + GROUPS].unsqueeze(2).to_broadcast([P, GROUPS, NB])
                lk(v.tensor_tensor(blk(2), stT[:, :, :, 0], chan(R_CW), ALU.mult))
                lk(v.tensor_tensor(blk(4), stT[:, :, :, 1], chan(R_CW + 4), ALU.mult))
                lk(v.tensor_tensor(blk(2), blk(2), blk(4), ALU.add))
                lk(v.tensor_tensor(blk(4), samp[:, 0], chan(R_CW + 8), ALU.mult))
                lk(v.tensor_tensor(blk(2), blk(2), blk(4), ALU.add))
                lk(v.tensor_tensor(blk(2), blk(2), samp[:, 1], ALU.mult))
                v.tensor_copy(blk(3), osT[:, :, :]).then_inc(e_w, 1)
                v.wait_ge(e_w, 1)
                lk(v.tensor_tensor(blk(4), blk(2), chan(R_GC), ALU.mult))
                lk(v.tensor_tensor(blk(5), blk(3), chan(R_GA), ALU.mult))
                v.tensor_tensor(blk(6), blk(4), samp[:, 2], ALU.mult).then_inc(e_ysT, 1)
                v.tensor_tensor(blk(7), blk(5), samp[:, 3], ALU.mult).then_inc(e_ysT, 1)
                v.wait_ge(conv_ps, 1)
                lk(v.tensor_copy(om[0:NB, :], ps[0:NB, DB, :]))
                v.tensor_copy(qb[0:2, 0, :], ps[0:2, MB, :]).then_inc(conv_sb, 1)
            def decode_mean():
                v.wait_ge(ss_ps, 2)
                v.tensor_scalar(ss[0:NB, 16:18], ps[0:NB, MB, 16:18], 1.0 / HALF, EPS, ALU.mult, ALU.add)\
                    .then_inc(ss_var, 1)

            v.wait_ge(ss_rstd, 1)
            for n in range(OUT_UNITS):
                t, j = divmod(n, 2)
                rows_ = P if t < TT else NB
                col = 8 + t if t < TT else 17
                if n == LAST_PV:
                    last_sequence()
                if n == LAST_PV + 1:
                    decode_rows()
                if n == 2 * TT - 1:
                    decode_mean()
                if n == 2 * TT:
                    v.wait_ge(ss_rstd, 2)
                v.wait_ge(ma_ready, n + 1)
                if t >= 2 and j == 0:
                    v.wait_ge(msq, t - 1)
                half_cols = slice(HALF * j, HALF * (j + 1))
                v.scalar_tensor_tensor(mm_(t)[0:rows_, half_cols], ps[0:rows_, 2 * (n % 3) + 1, :],
                                       rs[0:rows_, col:col + 1], ma(t)[0:rows_, half_cols], ALU.mult, ALU.add)\
                    .then_inc(m_ready, 1)
                if j == 0:
                    continue
                v.wait_ge(msq, t + 1)
                v.tensor_scalar(ss[0:rows_, 20 + t % 2:21 + t % 2], ss[0:rows_, 24 + t % 2:25 + t % 2], 1.0 / D, EPS,
                                ALU.mult, ALU.add).then_inc(m_var, 1)
                v.wait_ge(m_rstd, t + 1)
                if t >= 2:
                    v.wait_ge(y_out[t % 2], 16 * (t // 2))
                gate = gp if t < TT else gps
                lk(v.scalar_tensor_tensor(yo(t)[0:rows_], mm_(t)[0:rows_], rs[0:rows_, 20 + t % 2:21 + t % 2],
                                          gate[0:rows_, :], ALU.mult, ALU.mult))
                v.wait_ge(xr_full[t % 4], 16 * (t // 4 + 1))
                v.tensor_tensor(yo(t)[0:rows_], yo(t)[0:rows_], kring[0:rows_, t % 4].rearrange("p j c -> p (j c)"),
                                ALU.add).then_inc(y_ready, 1)

        @block.tensor
        def _(pe):
            def mm(out, l, r, start, stop):
                return nc.tensor.matmul(out, l, r, start=start, stop=stop, skip_group_check=True)

            pe.wait_ge(pool_const, POOL_CONSTS)
            pe.wait_ge(c_silu, 1)
            for k in range(KT):
                last = nc.tensor.transpose(ps[:, MB, 9 * k:9 * k + 9], cwk[:, P * k:P * (k + 1)], ident[0:9, 0:9])
            last.then_inc(cT_full, 1)
            pe.wait_ge(small_in, 16 * N_SMALL)
            nc.tensor.transpose(ps[:, DB, 0:NPAR], parN, ident[0:NPAR, 0:NPAR])
            for g in range(GROUPS):
                last = nc.tensor.transpose(ps[:, DB, 64 + 16 * g:80 + 16 * g], stN[:, g, :], ident[0:16, 0:16])
            last.then_inc(par_full, 1)

            pe.wait_ge(dve_const, 14)
            pe.wait_ge(cT_copied, 1)

            def strips(bank, lhs, n):
                pe.wait_ge(ada_full[n % 2], 16 * (n // 2 + 1))
                for k in range(KT):
                    j = k % 4
                    last = mm(ps[32 * j:32 * j + 32, bank, :], lhs(k), ada_slot[n % 2][:, k, :], k < 4, k >= 4)
                return last

            def ada(n):
                if n >= 2:
                    pe.wait_ge(ada_copied, n - 1)
                strips(PJB + n % 2, lambda k: cT[:, k, :], n).then_inc(ada_ps, 1)

            ada(0)
            ada(1)
            pe.wait_ge(x_scaled, TT + 1)
            for n in range(2 * KT):
                if n in ADA_AT:
                    ada(2 + ADA_AT.index(n))
                if n >= 4:
                    pe.wait_ge(xT_dve if n % 2 else xT_act, (n - 4) // 2 + 1)
                for j in range(4):
                    last = nc.tensor.transpose(ps[:, n % 4, P * j:P * (j + 1)],
                                               xy[:, 4 * (n % 2) + j, P * (n // 2):P * (n // 2 + 1)], ident[:, :])
                last.then_inc(xT_full, 1)
            for k in range(KT):
                last = nc.tensor.transpose(ps[:, MB, P + NB * k:P + NB * (k + 1)], xs[:, P * k:P * (k + 1)],
                                           ident[0:NB, 0:NB])
            last.then_inc(xT_full, 1)
            pe.wait_ge(ada_copied, 4)
            pe.wait_ge(xT_sdve, 1)
            for k in range(2 * KT):
                last = mm(ps[:, MB, 256 + 9 * k:265 + 9 * k], ada_cols(P * k, P), e32[:, 0:9], True, True)
            last.then_inc(mod_ps, 1)
            pe.wait_ge(h_ready, 1)
            pe.wait_ge(par_copied, 2)
            strips(DB, lambda k: hT[:, k, SEQ:NTP], 4).then_inc(qs_ps, 1)
            pe.wait_ge(ada_copied, 4)

            def gate_strips(n):
                if n:
                    pe.wait_ge(gate_step, 3)
                else:
                    pe.wait_ge(qs_copied, 1)
                strips(DB, lambda k: cT[:, k, :], 5 + 2 * n).then_inc(ada_ps, 1)

            def gate_sums(n):
                pe.wait_ge(ada_copied, 5 + n)
                mm(ps[0:NB, DB, :], e32[:, 1:9], ada_cols(2048 + HALF * n, HALF), True, True).then_inc(gate_ps, 1)
                pe.wait_ge(gate_step, 3 * n + 1)
                mm(ps[:, DB, :], e32[:, 0:1].to_broadcast([P, P]), ada_cols(2048 + HALF * n, HALF), True, True)\
                    .then_inc(gate_ps, 1)

            def body(g, first, last_):
                def project(m, part, chunk, ks=range(KT)):
                    if first and part == Q_:
                        pe.wait_ge(h_ready, 1 + KT * (chunk + 1))
                    if ks[0] == 0:
                        if chunk == 0:
                            pe.wait_ge(w_full[part % 2], 16 * (4 * g + part // 2 + 1))
                        if not (first and m < 2):
                            pe.wait_ge(pj_free, PJ * g + m - 1)
                    for k in ks:
                        last = mm(ps[:, PJB + m % 2, 0:CH], wsl[:, part % 2, k, :], hT[:, k, CH * chunk:CH * (chunk + 1)],
                                  k == 0, k == KT - 1)
                    if ks[-1] == KT - 1:
                        last.then_inc(pj_full, 1)

                def values(m):
                    pe.wait_ge(pj_free, PJ * g + m - 1)
                    if m == 6:
                        pe.wait_ge(w_full[V_ % 2], 16 * (4 * g + V_ // 2 + 1))
                    if m < 8:
                        for j in range(4):
                            for k in range(KT):
                                t = 4 * (m - 6) + j
                                last = mm(ps[:, PJB + m % 2, P * j:P * (j + 1)], hT[:, k, P * t:P * (t + 1)],
                                          wsl[:, V_ % 2, k, :], k == 0, k == KT - 1)
                    else:
                        for k in range(KT):
                            last = mm(ps[0:NB, PJB + m % 2, 0:P], hT[:, k, SEQ:NT], wsl[:, V_ % 2, k, :], k == 0, k == KT - 1)
                    last.then_inc(pj_full, 1)

                def misc_ready(n):
                    if not (first and n == 0):
                        pe.wait_ge(ms_free, MS * g + n)

                def spread_q(k):
                    misc_ready(M_QB1 if k else M_QB0)
                    pe.wait_ge(qsel_ready, 2 * g + k + 1)
                    mm(ps[:, MB, :], ones[:, :], qsel[:, :], True, True).then_inc(ms_full, 1)

                def cumulate(k):
                    misc_ready(M_CUM1 if k else M_CUM0)
                    pe.wait_ge(d_sp, 2 * g + k + 1)
                    mm(ps[:, MB, 0:256], ntri[:, :].bitcast(F32), spd[:, :], True, True)
                    mm(ps[:, MB, 256:512], nones[:, :].bitcast(F32), spd[:, :], True, True).then_inc(ms_full, 1)

                def page_values(t):
                    parity, prs = pairs_of(t)
                    if first and parity == 1:
                        return
                    for rr in prs:
                        value_pair(2 * g - parity, 32 * g - 16 * parity + rr, rr, 2 * g - parity)

                def own_heads_T(parity):
                    pe.wait_ge(d_om, 2 * g - parity + 1)
                    heads_T(2 * g - parity)

                def scores(u):
                    c, i, h = UNITS[u]
                    lo = first_col(u)
                    if u == 0:
                        pe.wait_ge(pj_free, PJ * g + 6)
                    if not (first and u < 3):
                        pe.wait_ge(a_ready, NU * g + u - 2)
                    last = mm(ps[:, Z + u % 3, lo:QC], kT[:, P * i:P * (i + 1)], qz[:, h, QC * c + lo:QC * (c + 1)],
                              True, False)
                    if i >= 4 * c:
                        last = mm(ps[:, Z + u % 3, lo:lo + P], ident_b[:, :], unseen[:, :], False, False)
                    last.then_inc(z_full, 1)

                def suffix(u):
                    c, i, h = UNITS[u]
                    lo, di = first_col(u), i - 4 * c
                    seen = min(QC, lo + (P if di >= 0 else 0))
                    pe.wait_ge(hi_ready, NU * g + u + 1)
                    mm(ps[:, Z + u % 3, lo:QC], ntri[:, :], sp_hi[:, u % 2, lo:QC], False, False)
                    if seen < QC:
                        pe.wait_ge(later_hi_ready, len(RUPD) * g + RUPD.index(u - 2) + 1)
                        mm(ps[:, Z + u % 3, seen:QC], nones[:, :], later_hi[:, seen:QC], False, False)
                        pe.wait_ge(later_lo_ready, len(RUPD) * g + RUPD.index(u - 2) + 1)
                        mm(ps[:, Z + u % 3, seen:QC], nones[:, :], later_lo[:, seen:QC], False, False)
                    pe.wait_ge(lo_ready, NU * g + u + 1)
                    mm(ps[:, Z + u % 3, lo:QC], ntri[:, :], sp_lo[:, u % 2, lo:QC], False, True).then_inc(c_full, 1)

                def outputs(u):
                    c, i, h = UNITS[u]
                    lo = first_col(u)
                    pe.wait_ge(a_ready, NU * g + u + 1)
                    if u == 0:
                        pe.wait_ge(pj_free, PJ * g + 8)
                        if not first:
                            pe.wait_ge(ob_ready, g)
                    if u == 8:
                        pe.wait_ge(o_free, g + 1)
                    mm(ps[HD * h:HD * (h + 1), OB, lo:QC], vN[:, i, HD * h:HD * (h + 1)], av[:, u % 2, lo:QC],
                       i == 4 * c + 3, i == 0).then_inc(pv_done, 1)

                def key_rows(n):
                    misc_ready(M_KN0 + n)
                    if n < 2:
                        for j in range(4):
                            last = nc.tensor.transpose(ps[:, MB, P * j:P * (j + 1)],
                                                       kT[:, P * (4 * n + j):P * (4 * n + j + 1)], ident[:, :])
                    else:
                        last = nc.tensor.transpose(ps[0:NB, MB, 0:P], kT[:, SEQ:NT], ident[:, :])
                    last.then_inc(ms_full, 1)

                for t in range(8):
                    if t < 3:
                        project(t, Q_, t)
                    elif t < 6:
                        project(t, K_, t - 3)
                    else:
                        values(t)
                    if t == 2:
                        spread_q(0)
                    if first and t == 4:
                        gate_strips(0)
                    if first and t == 6:
                        gate_sums(0)
                    page_values(t)
                values(8)
                for t in range(8, SLOTS + 2):
                    u = t - 8
                    if u < NU:
                        scores(u)
                        m = 9 + u // 2
                        ks = range(0, 4) if u % 2 == 0 else range(4, 8)
                        part, chunk = GC_ + (m - 9) // 3, (m - 9) % 3
                        project(m, part, chunk, ks[0:2])
                    else:
                        project(21 + u - NU, BC_, u - NU)
                    if 1 <= u <= NU:
                        suffix(u - 1)
                    if u < NU:
                        project(m, part, chunk, ks[2:4])
                    if t == 19:
                        cumulate(0)
                    if u >= 2:
                        outputs(u - 2)
                    if t in (8, 9, 10):
                        key_rows(t - 8)
                    if first and t == 9:
                        gate_strips(1)
                    if first and t == 12:
                        gate_sums(1)
                    if t == 12:
                        spread_q(1)
                    if t == 17 and not first:
                        own_heads_T(1)
                    page_values(t)
                project(23, BC_, 2)
                own_heads_T(0)
                cumulate(1)

            def value_pair(seq, q, rr, done_before):
                if rr == 0:
                    pe.wait_ge(d_a, seq + 1)
                    if not (isinstance(seq, int) and seq == 0):
                        pe.wait_ge(d_free, done_before)
                pe.wait_ge(v_full[rr % 4], v_fill(seq, rr))
                for j in range(2):
                    r = 2 * rr + j
                    strip = 32 * (r % 4)
                    last = mm(ps[strip:strip + 32, DB, :], apad[:, :, r], vring[:, rr % 4, j, :], r < 4, r >= PAGES - 4)
                last.then_inc(v_used, 1)

            def v_fill(seq, rr):
                return 32 * (4 * seq + rr // 4 + 1)

            def heads_T(seq):
                for c in range(GROUPS):
                    last = mm(ps[:, DB, c:c + 1], om[:, P * c:P * (c + 1)], ones[:, 0:1], True, True)
                last.then_inc(d_oT, 1)

            run_groups(pe, body)

            def last_pair(rr):
                value_pair(NB - 1, 16 * (NB - 1) + rr, rr, NB - 1)

            def conv_rows():
                pe.wait_ge(d_free, NB)
                for c in range(GROUPS):
                    nc.tensor.transpose(ps[0:NB, DB, P * c:P * (c + 1)], samp[:, 0, c, :], ident[:, :])
                pe.wait_ge(ss_var, 1)
                for c in range(GROUPS):
                    last = nc.tensor.transpose(ps[0:2, MB, P * c:P * (c + 1)], tail[:, c, :], ident[:, :])
                last.then_inc(conv_ps, 1)

            def decode_sums():
                pe.wait_ge(conv_sb, 1)
                pe.wait_ge(e_exp, 1)
                for b in range(2):
                    for c in range(GROUPS):
                        last = mm(ps[0:NB, MB, 16 + b:17 + b], tmp[:, 32 * b + 8 * c:32 * b + 8 * c + 8], ones[:, 0:1],
                                  c == 0, c == GROUPS - 1)
                last.then_inc(ss_ps, 1)

            def out_unit(n, ks):
                t, j = divmod(n, 2)
                rows_ = P if t < TT else NB
                for k in ks:
                    for b in range(2):
                        if n == 0:
                            pe.wait_ge(wo_full[GROUPS * b + k], 16)
                        lhs = yT[:, GROUPS * b + k, P * t:P * (t + 1)] if t < TT else tmp_s(b, k)
                        last = mm(ps[0:rows_, 2 * (n % 3) + b, :], lhs, wo(GROUPS * b + k)[:, HALF * j:HALF * (j + 1)],
                                  k == 0, k == GROUPS - 1)
                if k == GROUPS - 1:
                    last.then_inc(m_ps, 1)

            pe.wait_ge(group_done, GROUPS - 1)
            for n in range(3):
                if n == 1:
                    pe.wait_ge(ob_ready, GROUPS)
                if n == 2:
                    pe.wait_ge(pj_free, PJ * GROUPS)
                out_unit(n, range(GROUPS - 1))
            pe.wait_ge(group_done, GROUPS)
            pe.wait_ge(ms_free, MS * GROUPS)
            for b, src in enumerate((ssa, ssb)):
                for t in range(TT):
                    last = mm(ps[:, MB, 8 * b + t:8 * b + t + 1], src[:, P * t:P * (t + 1)], ones[:, 0:1], True, True)
            last.then_inc(ss_ps, 1)

            for rr in range(4):
                last_pair(rr)
            for n in range(OUT_UNITS):
                if n == 2 * TT:
                    pe.wait_ge(e_ysT, 2)
                if n >= 3:
                    pe.wait_ge(m_ready, n - 2)
                out_unit(n, range(GROUPS) if n >= 3 else [GROUPS - 1])
                if n < LAST_PV:
                    last_pair(4 + n)
                if n == LAST_PV:
                    pe.wait_ge(d_om, NB)
                    heads_T(NB - 1)
                if n == LAST_PV + 1:
                    conv_rows()
                if n == LAST_PV + 2:
                    decode_sums()


_INS = ["x_prompt", "x_sample", "c_prompt", "c_sample", "cache_k", "cache_v", "state_conv", "page_table",
        "w_ada", "b_ada", "g_pre", "w_in", "conv_w", "g_conv", "b_sb", "g_attn", "w_out", "g_post"]
_OUTS = [(1, SEQ, D), (NB, 1, D), (1, 1, SEQ, NH, HD), (1, 1, SEQ, NH, HD), (1, 1, 2, HALF),
         (1, NB, 1, NH, HD), (1, NB, 1, NH, HD), (1, NB, 2, HALF)]


def kernel(**inputs):
    import numpy as _np
    import concourse.bacc as _bacc
    from concourse import mybir as _mybir
    from concourse.bass_utils import run_bass_kernel_spmd as _run

    nc = _bacc.Bacc("TRN2", target_bir_lowering=False, num_devices=1, dynamic_dma_scratch_size=1024)
    nc.disable_value_cache = True
    arrays, args = {}, []
    for name in _INS:
        a = _np.ascontiguousarray(inputs[name])
        arrays[f"in_{name}_dram"] = a
        args.append(nc.dram_tensor(f"in_{name}_dram", a.shape, _mybir.dt.from_np(a.dtype), kind="ExternalInput").ap())
    for i, shape in enumerate(_OUTS):
        args.append(nc.dram_tensor(f"out_{i}_dram", shape, _mybir.dt.float32, kind="ExternalOutput").ap())
    stick_breaking_mixer(nc, *args)
    r = _run(nc, [arrays], core_ids=[0])
    return tuple(r.results[0][f"out_{i}_dram"] for i in range(len(_OUTS)))
```
